# Optimizing a Trainium2 kernel written in Bass

```python
import jax, jax.numpy as jnp
from jax import lax
import numpy as np

D_MODEL = 1024
BATCH = 1
SEQ = 1024
DEPTH = 2
DEC_BATCH = 8
DEC_SEQ = 8
PAST_LEN = 1024
PAGE_SIZE = 128

N_MIXERS = 2
N_A_LAYERS = (DEPTH + 1) // 2
N_B_LAYERS = DEPTH // 2
P_DIM = 256
EPS = 1e-6
ROPE_THETA = 10000.0

CHUNK = 128
A_WIDTH = 2 * D_MODEL
A_GROUPS = 8
A_GROUP_DIM = A_WIDTH // A_GROUPS

N_HEADS = 8
HEAD_DIM = D_MODEL // N_HEADS
N_KV_HEADS = 2
B_WIDTH = N_HEADS * HEAD_DIM
KV_WIDTH = N_KV_HEADS * HEAD_DIM
IDX_HEADS = 8
IDX_DIM = 64
TOPK_MAX = 256
Q_BLOCK = 128
B_SPLITS = (B_WIDTH, KV_WIDTH, KV_WIDTH, IDX_HEADS * IDX_DIM, IDX_DIM, IDX_HEADS, B_WIDTH)
B_IN = sum(B_SPLITS)

kernel_name = 'hybrid_gmlp_dsa_decode_step'

def rmsnorm(x, g):
    xf = x.astype(jnp.float32)
    r = lax.rsqrt(jnp.mean(xf * xf, axis=-1, keepdims=True) + EPS)
    return (xf * r).astype(x.dtype) * g

def rope(x, pos):
    half = x.shape[-1] // 2
    inv = ROPE_THETA ** (-jnp.arange(half, dtype=jnp.float32) / half)
    ang = pos.astype(jnp.float32)[:, None] * inv[None, :]
    cos = jnp.cos(ang)[:, None, :]
    sin = jnp.sin(ang)[:, None, :]
    x1, x2 = x[..., :half], x[..., half:]
    return jnp.concatenate([x1 * cos - x2 * sin, x2 * cos + x1 * sin], axis=-1).astype(x.dtype)

def mixer_a(h, w_in, w_s, b_s, g_v, w_out):
    bsz, t, _ = h.shape
    u, v, z = jnp.split(h @ w_in, 3, axis=-1)
    v = rmsnorm(v, g_v)
    c = min(t, CHUNK)
    n_chunks = t // c
    causal = jnp.tril(jnp.ones((c, c), dtype=bool))
    ws = jnp.where(causal[None], w_s[:, :c, :c], jnp.zeros((), w_s.dtype))
    vc = v.reshape(bsz, n_chunks, c, A_GROUPS, A_GROUP_DIM)
    mixed = jnp.einsum('gts,bnsgd->bntgd', ws, vc) + b_s[:, :c].T[None, None, :, :, None]
    y = u * mixed.reshape(bsz, t, A_WIDTH) * jax.nn.silu(z)
    return y @ w_out, v

def project_b(h, pos, w_in, g_q, g_k, g_ik):
    bsz, t, _ = h.shape
    pts = np.cumsum(B_SPLITS)[:-1].tolist()
    q, k, v, iq, ik, iw, z = jnp.split(h @ w_in, pts, axis=-1)
    q = rope(rmsnorm(q.reshape(bsz, t, N_HEADS, HEAD_DIM), g_q), pos)
    k = rope(rmsnorm(k.reshape(bsz, t, N_KV_HEADS, HEAD_DIM), g_k), pos)
    v = v.reshape(bsz, t, N_KV_HEADS, HEAD_DIM)
    iq = rope(iq.reshape(bsz, t, IDX_HEADS, IDX_DIM), pos)
    ik = rope(rmsnorm(ik, g_ik)[:, :, None, :], pos)[:, :, 0, :]
    return q, k, v, iq, ik, iw, z

def indexer_scores(iq, iw, ik):
    s = jax.nn.relu(jnp.einsum('bthd,bsd->bths', iq, ik).astype(jnp.float32))
    return jnp.einsum('bths,bth->bts', s, iw.astype(jnp.float32)) * (IDX_DIM ** -0.5 * IDX_HEADS ** -0.5)

def attend_selected(q, k_sel, v_sel, valid):
    bsz, t, h, d = q.shape
    qg = q.reshape(bsz, t, N_KV_HEADS, h // N_KV_HEADS, d)
    s = jnp.einsum('btgrd,btkgd->btgrk', qg, k_sel).astype(jnp.float32) * (d ** -0.5)
    s = jnp.where(valid[:, :, None, None, :], s, -jnp.inf)
    p = jax.nn.softmax(s, axis=-1).astype(v_sel.dtype)
    o = jnp.einsum('btgrk,btkgd->btgrd', p, v_sel)
    return o.reshape(bsz, t, h * d)

def dsa_prompt(q, k, v, iq, ik, iw):
    bsz, s = q.shape[:2]
    topk = min(TOPK_MAX, s // 4)
    n_blocks = s // Q_BLOCK
    key_pos = jnp.arange(s)
    bi = jnp.arange(bsz)[:, None, None]

    def block(i):
        start = i * Q_BLOCK
        qb = lax.dynamic_slice_in_dim(q, start, Q_BLOCK, axis=1)
        iqb = lax.dynamic_slice_in_dim(iq, start, Q_BLOCK, axis=1)
        iwb = lax.dynamic_slice_in_dim(iw, start, Q_BLOCK, axis=1)
        qpos = start + jnp.arange(Q_BLOCK)
        sc = indexer_scores(iqb, iwb, ik)
        adm = key_pos[None, :] <= qpos[:, None]
        sc = jnp.where(adm[None], sc, -jnp.inf)
        _, idx = lax.top_k(sc, topk)
        valid = idx <= qpos[None, :, None]
        return attend_selected(qb, k[bi, idx], v[bi, idx], valid)

    out = lax.map(block, jnp.arange(n_blocks))
    return out.transpose(1, 0, 2, 3).reshape(bsz, s, B_WIDTH)

def dsa_sample(q, k_new, v_new, iq, ik_new, iw, cache_k, cache_v, cache_ik, page_table, layer):
    db, t = q.shape[:2]
    n_pages = page_table.shape[1]
    past = n_pages * PAGE_SIZE
    L = past + t
    topk = min(TOPK_MAX, L // 4)
    ik_past = cache_ik[page_table, layer].reshape(db, past, IDX_DIM)
    ik_all = jnp.concatenate([ik_past, ik_new], axis=1)
    sc = indexer_scores(iq, iw, ik_all)
    qpos = past + jnp.arange(t)
    adm = jnp.arange(L)[None, :] <= qpos[:, None]
    sc = jnp.where(adm[None], sc, -jnp.inf)
    _, idx = lax.top_k(sc, topk)
    valid = idx <= qpos[None, :, None]
    from_past = idx < past
    pidx = jnp.minimum(idx, past - 1)
    phys = jnp.take_along_axis(page_table, (pidx // PAGE_SIZE).reshape(db, t * topk), axis=1).reshape(db, t, topk)
    slot = pidx % PAGE_SIZE
    nidx = jnp.clip(idx - past, 0, t - 1)
    bi = jnp.arange(db)[:, None, None]
    sel = from_past[..., None, None]
    k_sel = jnp.where(sel, cache_k[phys, layer, slot], k_new[bi, nidx])
    v_sel = jnp.where(sel, cache_v[phys, layer, slot], v_new[bi, nidx])
    return attend_selected(q, k_sel, v_sel, valid)

def per_layer_embed(x, p, g, w_gate, w_pe):
    return x + jax.nn.sigmoid(rmsnorm(x, g) @ w_gate) * (p @ w_pe)

def setup_inputs(seed: int = 0) -> dict:
    key = jax.random.key(seed)
    ks = jax.random.split(key, 24)
    n_pages = PAST_LEN // PAGE_SIZE
    n_pool = (DEC_BATCH * n_pages * 5) // 4
    nrm = lambda k, shape, scale=1.0: jax.random.normal(k, shape, jnp.float32) * scale
    page_table = jax.random.permutation(ks[5], n_pool)[:DEC_BATCH * n_pages].reshape(DEC_BATCH, n_pages).astype(jnp.int32)
    return {
        'x_prompt': nrm(ks[0], (BATCH, SEQ, D_MODEL)),
        'x_sample': nrm(ks[1], (DEC_BATCH, DEC_SEQ, D_MODEL)),
        'cache_k': nrm(ks[2], (n_pool, N_B_LAYERS, PAGE_SIZE, N_KV_HEADS, HEAD_DIM)),
        'cache_v': nrm(ks[3], (n_pool, N_B_LAYERS, PAGE_SIZE, N_KV_HEADS, HEAD_DIM)),
        'cache_ik': nrm(ks[4], (n_pool, N_B_LAYERS, PAGE_SIZE, IDX_DIM)),
        'page_table': page_table,
        'p_prompt': nrm(ks[6], (DEPTH, BATCH, SEQ, P_DIM)),
        'p_sample': nrm(ks[7], (DEPTH, DEC_BATCH, DEC_SEQ, P_DIM)),
        'g_norm': 1.0 + nrm(ks[8], (DEPTH, D_MODEL), 0.05),
        'w_in_a': nrm(ks[9], (N_A_LAYERS, D_MODEL, 3 * A_WIDTH), D_MODEL ** -0.5),
        'w_s_a': nrm(ks[10], (N_A_LAYERS, A_GROUPS, CHUNK, CHUNK), CHUNK ** -0.5),
        'b_s_a': 1.0 + nrm(ks[11], (N_A_LAYERS, A_GROUPS, CHUNK), 0.1),
        'g_v_a': 1.0 + nrm(ks[12], (N_A_LAYERS, A_WIDTH), 0.05),
        'w_out_a': nrm(ks[13], (N_A_LAYERS, A_WIDTH, D_MODEL), A_WIDTH ** -0.5),
        'w_in_b': nrm(ks[14], (N_B_LAYERS, D_MODEL, B_IN), D_MODEL ** -0.5),
        'g_q_b': 1.0 + nrm(ks[15], (N_B_LAYERS, HEAD_DIM), 0.05),
        'g_k_b': 1.0 + nrm(ks[16], (N_B_LAYERS, HEAD_DIM), 0.05),
        'g_ik_b': 1.0 + nrm(ks[17], (N_B_LAYERS, IDX_DIM), 0.05),
        'w_out_b': nrm(ks[18], (N_B_LAYERS, B_WIDTH, D_MODEL), B_WIDTH ** -0.5),
        'g_pe': 1.0 + nrm(ks[19], (DEPTH, D_MODEL), 0.05),
        'w_pe_gate': nrm(ks[20], (DEPTH, D_MODEL, D_MODEL), D_MODEL ** -0.5),
        'w_pe_proj': nrm(ks[21], (DEPTH, P_DIM, D_MODEL), P_DIM ** -0.5),
    }

def reference(x_prompt, x_sample, cache_k, cache_v, cache_ik, page_table, p_prompt, p_sample,
              g_norm, w_in_a, w_s_a, b_s_a, g_v_a, w_out_a, w_in_b, g_q_b, g_k_b, g_ik_b, w_out_b,
              g_pe, w_pe_gate, w_pe_proj):
    yp, ys = x_prompt, x_sample
    past = page_table.shape[1] * PAGE_SIZE
    pos_p = jnp.arange(x_prompt.shape[1])
    pos_s = past + jnp.arange(x_sample.shape[1])
    kp_l, vp_l, ikp_l, ks_l, vs_l, iks_l, cv_l = [], [], [], [], [], [], []
    for i in range(DEPTH):
        j = i // N_MIXERS
        hp = rmsnorm(yp, g_norm[i])
        hs = rmsnorm(ys, g_norm[i])
        if i % N_MIXERS == 0:
            op, _ = mixer_a(hp, w_in_a[j], w_s_a[j], b_s_a[j], g_v_a[j], w_out_a[j])
            os_, v_rows = mixer_a(hs, w_in_a[j], w_s_a[j], b_s_a[j], g_v_a[j], w_out_a[j])
            cv_l.append(v_rows)
        else:
            q, k, v, iq, ik, iw, z = project_b(hp, pos_p, w_in_b[j], g_q_b[j], g_k_b[j], g_ik_b[j])
            op = (dsa_prompt(q, k, v, iq, ik, iw) * jax.nn.silu(z)) @ w_out_b[j]
            kp_l.append(k)
            vp_l.append(v)
            ikp_l.append(ik)
            q, k, v, iq, ik, iw, z = project_b(hs, pos_s, w_in_b[j], g_q_b[j], g_k_b[j], g_ik_b[j])
            att = dsa_sample(q, k, v, iq, ik, iw, cache_k, cache_v, cache_ik, page_table, j)
            os_ = (att * jax.nn.silu(z)) @ w_out_b[j]
            ks_l.append(k)
            vs_l.append(v)
            iks_l.append(ik)
        yp = per_layer_embed(yp + op, p_prompt[i], g_pe[i], w_pe_gate[i], w_pe_proj[i])
        ys = per_layer_embed(ys + os_, p_sample[i], g_pe[i], w_pe_gate[i], w_pe_proj[i])
    k_prompt = jnp.stack(kp_l, axis=1)
    v_prompt = jnp.stack(vp_l, axis=1)
    ik_prompt = jnp.stack(ikp_l, axis=1)
    k_sample = jnp.stack(ks_l, axis=1)
    v_sample = jnp.stack(vs_l, axis=1)
    ik_sample = jnp.stack(iks_l, axis=1)
    chunk_v_sample = jnp.stack(cv_l, axis=1)
    return (yp, ys, k_prompt, v_prompt, ik_prompt, k_sample, v_sample, ik_sample, chunk_v_sample)


_drawn_inputs = setup_inputs


def setup_inputs(seed=0):
    import zlib

    import numpy as np

    out = dict(_drawn_inputs(seed))
    spreads = {}
    factors = {'g_q_b': 8.0, 'g_pe': 5.063}
    for name, (base, spread) in spreads.items():
        noise = np.random.default_rng([zlib.crc32(name.encode()), seed]).standard_normal(out[name].shape)
        drawn = base * np.exp(spread * noise) if base else spread * noise
        out[name] = __import__('jax').numpy.asarray(drawn.astype(out[name].dtype))
    for name, factor in factors.items():
        out[name] = (out[name] * factor).astype(out[name].dtype)
    return out
```

```python
from contextlib import ExitStack

import numpy as np

import concourse.bass as bass
from concourse import mybir

F32 = mybir.dt.float32
F32R = mybir.dt.float32r
BF16 = mybir.dt.bfloat16
I32 = mybir.dt.int32
U32 = mybir.dt.uint32
ALU = mybir.AluOpType
ACT = mybir.ActivationFunctionType
AX = mybir.AxisListType

P = 128
D = 1024
KD = D // P
SEQ, DEC_B, DEC_T = 1024, 8, 8
NS = DEC_B * DEC_T
NT = NS + SEQ
TP = NT + 4
NC3 = TP // 3
CHUNK = 128
NBLK = SEQ // CHUNK
AW = 2 * D
KA = AW // P
NGRP = 8
PD = 256
EPS = 1e-6
THETA = 10000.0
PAGE, NPAGE = 128, 8
PAST = PAGE * NPAGE
NH, DH, NKV, REP = 8, 128, 2, 4
IH, ID = 8, 64
TOPK = 256
SLS = PAST + NS
QOFF, KOFF, VOFF, IQOFF, IKOFF, ZOFF = 0, 1024, 1280, 1536, 2048, 2120
MASKED = -2.0e38
BIG = 1.0e30
BANK = 512

GROUPS = [(0, 576, 4, True), (576, 516, 4, False)]
GW = 576
U_A = [0, 64]
U_GATE = [128, 169]
U_IQ, U_IK, U_K, U_V, U_Q, U_Z, U_O = 136, 140, 141, 143, 145, 153, 161
N_UNITS = 177


def tile_cols(j):
    return (0, NS) if j == 0 else (NS + CHUNK * (j - 1), CHUNK)


def block_off(b):
    return P * sum(c + 1 for c in range(2, b))


def rope_tables(half, heads):
    pos = np.concatenate([np.tile(PAST + np.arange(DEC_T), DEC_B), np.arange(SEQ), np.zeros(TP - NT)])
    e = (-np.arange(half, dtype=np.float32) / np.float32(half)).astype(np.float64)
    inv = (THETA ** e).astype(np.float32)
    ang = (inv[:, None] * pos.astype(np.float32)[None, :]).astype(np.float32).astype(np.float64)
    c, s = np.cos(ang).astype(np.float32), np.sin(ang).astype(np.float32)
    return (np.concatenate([c, c] * heads, 0), np.concatenate([-s, s] * heads, 0))


class Turn:

    def __init__(self, sems, before):
        self.sems, self.before = sems, before

    def __getitem__(self, name):
        return self.sems[name]

    def at(self, name, value):
        return self.before[name] + value


class Tally:

    def __init__(self, eng, sem):
        self.eng, self.sem, self.n, self.i, self.per = eng, sem, 0, 0, 0

    def link(self, instruction):
        instruction.then_inc(self.sem, 1)
        self.n += 1
        self.eng.wait_ge(self.sem, self.i * self.per + self.n)

    def enter(self, i, per):
        self.i, self.per, self.at = i, per, self.n

    def leave(self, trips):
        assert self.n - self.at == self.per, (self.n - self.at, self.per)
        self.n = self.at + self.per * trips
        self.i = self.per = 0


def hybrid_trunk(nc, x_prompt, x_sample, cache_k, cache_v, cache_ik, page_table, p_prompt, p_sample,
                 g_norm, w_in_a, w_s_a, b_s_a, g_v_a, w_out_a, w_in_b, g_q_b, g_k_b, g_ik_b, w_out_b,
                 g_pe, w_pe_gate, w_pe_proj,
                 y_prompt, y_sample, k_prompt, v_prompt, ik_prompt, k_sample, v_sample, ik_sample,
                 chunk_v_sample):
    ctx = ExitStack()
    with ctx:
        def sem(name):
            return ctx.enter_context(nc.semaphore(name))

        at = [(nc.sbuf_base + 63) // 64 * 64]

        def fixed(name, shape, dt=F32):
            size = int(np.prod(shape[1:])) * mybir.dt.size(dt)
            t = nc.alloc_sbuf_tensor_at(name, shape, dt, offset=at[0])
            at[0] += (size + 31) // 32 * 32
            return t

        def region(start, limit):
            pos = [start]

            def place(name, shape, dt=F32):
                size = int(np.prod(shape[1:])) * mybir.dt.size(dt)
                t = nc.alloc_sbuf_tensor_at(name, shape, dt, offset=pos[0])
                pos[0] += (size + 31) // 32 * 32
                assert pos[0] <= limit, (name, pos[0], limit)
                return t
            return place

        ident = fixed("ident", [P, P])
        ones = fixed("ones", [P, P])
        gn = fixed("gn", [P, 2, KD])
        gp = fixed("gp", [P, 2, KD])
        gv = fixed("gv", [P, KA])
        gqk = fixed("gqk", [P, 3])
        eps = fixed("eps", [P, 1])
        ss = fixed("ss", [P, 9])
        sv = fixed("sv", [P, 5])
        rv = fixed("rv", [P, 5])
        wraw = [fixed(f"wraw{s}", [P, KD, P]) for s in range(2)]
        whi = [fixed(f"whi{s}", [P, KD, P], F32R) for s in range(2)]
        wlo = [fixed(f"wlo{s}", [P, KD, P], F32R) for s in range(2)]
        acc = fixed("acc", [P, TP])
        rbc = fixed("rbc", [P, TP])
        fixed_ptab = nc.alloc_sbuf_tensor_at("ptab", [1, DEC_B * NPAGE], I32, offset=at[0])
        at[0] += 256
        X0 = at[0]
        xT = fixed("xT", [P, KD, TP])
        D0, END = at[0], nc.sbuf_usable_end

        pl = region(D0, END)
        hhi_g = pl("hhi_g", [P, KD, GW], F32R)
        hlo_g = pl("hlo_g", [P, KD, GW], F32R)
        V0 = D0 + 2 * KD * GW * 4
        v_raw = pl("v_raw", [P, KA, 5 * P])
        Y0 = V0 + KA * 5 * P * 4
        ylo = pl("ylo", [P, KA, GW], F32R)
        wsT = pl("wsT", [P, NGRP, P])
        wsbd = pl("wsbd", [NS, NGRP, NS])
        bsb = pl("bsb", [P, NGRP, P])
        szt = pl("szt", [P, GW])
        t1a = pl("t1a", [P, GW])
        t2a = pl("t2a", [P, GW])
        vs = pl("vs", [P, 5 * P])
        hfa = pl("hfa", [P, 2, GW])
        sqa = hfa[:, 0, :]
        yhi = nc.alloc_sbuf_tensor_at("yhi", [P, KA, 5 * P], F32R, offset=V0)
        vtmp = [szt, t1a]
        pl = region(Y0, Y0 + KA * GW * 4)
        xstage = pl("xstage", [P, 3, D])
        sqdump = pl("sqdump", [P, D], BF16)
        vdump = nc.alloc_sbuf_tensor_at("vdump", [P, KA, P], F32, offset=Y0)
        wsraw = pl("wsraw", [P, NGRP, P])
        gvb = pl("gvb", [NS, AW])
        v_out = pl("v_out", [NS, AW])

        pl = region(D0, END)
        hhi = pl("hhi", [P, KD, TP], F32R)
        hlo = pl("hlo", [P, KD, TP], F32R)
        H1 = D0 + 2 * KD * TP * 4
        pl = region(H1, END)
        pst = pl("pst", [P, 9, PD])
        xo = nc.alloc_sbuf_tensor_at("xo", [P, 2, TP], F32, offset=H1)
        pThi = pl("pThi", [P, 2, TP], F32R)
        pTlo = pl("pTlo", [P, 2, TP], F32R)
        peraw = pl("peraw", [P, 2, D])
        pehi = pl("pehi", [P, 2, P], F32R)
        pelo = pl("pelo", [P, 2, P], F32R)
        sig = pl("sig", [P, TP])
        tpe = pl("tpe", [P, TP])
        hfb = pl("hfb", [P, 2, TP])
        sqb = hfb[:, 0, :]
        ystage = pl("ystage", [P, 2, 9, P])

        pl = region(H1, END)
        qT = pl("qT", [P, NH, TP])
        sc = pl("sc", [P, block_off(NBLK)])
        scs = pl("scs", [NS, SLS])
        swp = pl("swp", [P, TP])
        tq = pl("tq", [P, TP])
        sqt = pl("sqt", [P, TP])
        caus = pl("caus", [P, 2 * P])
        iwt = pl("iwt", [P, 9, IH])
        qs = pl("qs", [P, 9, NH])
        nqs = pl("nqs", [P, 9, NH])
        repb = pl("repb", [NS, DEC_B, NS], BF16)
        tbit, cand, mbit = (pl(n, [P, 7], U32) for n in ("tbit", "cand", "mbit"))
        bitc = pl("bitc", [P, 7], U32)
        sgn, thr, cnt = (pl(n, [P, 7]) for n in ("sgn", "thr", "cnt"))
        pl = region(H1, H1 + NH * TP * 4)
        iqT = pl("iqT", [P, IH // 2, TP])
        csI, snI = pl("csI", [P, TP]), pl("snI", [P, TP])
        ikT = pl("ikT", [P, TP])
        iwT = nc.alloc_sbuf_tensor_at("iwT", [IH, TP], F32, offset=H1 + NH * TP * 4)
        pl = region(X0, X0 + KD * TP * 4)
        ikpg = [pl(f"ikpg{q}", [P, NPAGE, 2, ID]) for q in range(2)]
        ikTb = [pl(f"ikTb{q}", [P, PAST]) for q in range(2)]
        rels = pl("rels", [NS, SLS])
        sbT = pl("sbT", [NS, DEC_B, NS])
        sbw = pl("sbw", [NS, DEC_B, NS])
        iqb = pl("iqb", [P, DEC_B, NS])
        ikout = pl("ikout", [P, 9, ID])
        pl = region(X0, X0 + KD * TP * 4)
        kT = pl("kT", [P, NKV, TP])
        vtok = pl("vtok", [P, 9, NKV * DH])
        csQ, snQ = pl("csQ", [P, TP]), pl("snQ", [P, TP])
        qb = pl("qb", [P, DEC_B, NKV, NS])
        kout = nc.alloc_sbuf_tensor_at("kout", [P, 9, NKV * DH], F32, offset=H1 + (IH // 2) * TP * 4)
        pl = region(D0, H1)
        PTs = pl("PTs", [P, NBLK, REP, P])
        kpg = [pl(f"kpg{q}", [P, NPAGE, NKV * DH]) for q in range(2)]
        vpg = [pl(f"vpg{q}", [P, NPAGE, NKV * DH]) for q in range(2)]
        kTb = pl("kTb", [P, NKV, PAST])
        Ps = pl("Ps", [NS, SLS])
        PsT = pl("PsT", [P, 9, NS])
        amx, anb, asm, ars = (pl(n, [P, NBLK * NH]) for n in ("amx", "anb", "asm", "ars"))
        smx, snb, ssm, srs, qcol, nqcol = (pl(n, [NS, DEC_B]) for n in ("smx", "snb", "ssm", "srs", "qcol", "nqcol"))
        d8 = pl("d8", [NS, DEC_T])
        bd8 = pl("bd8", [NS, DEC_B])
        qa8 = pl("qa8", [NS, NH, DEC_T])
        need = nc.alloc_sbuf_tensor_at("need", [P, 7], F32, offset=D0)
        pring = [swp, tq]
        zst = [swp, tq]
        ptab = fixed_ptab

        PS = ctx.enter_context(nc.psum_tensor("PS", [P, 8, BANK], F32))
        PSF = PS[:].rearrange("p b n -> p (b n)")

        def slot3(s):
            return PS[:, 3 * s:3 * s + 3, 0:NC3]

        def as3(ap):
            return ap.rearrange("p (b n) -> p b n", b=3)

        w_raw = [sem("w_raw0"), sem("w_raw1")]
        w_hi, w_lo = sem("w_hi"), sem("w_lo")
        w_used = sem("w_used")
        cst, cst_dma = sem("cst"), sem("cst_dma")
        dv, av, gv_ = sem("dv"), sem("av"), sem("gp_own")
        x_in = [sem(f"x_in{s}") for s in range(3)]
        x_tr, x_sq, x_ev, x_eva, x_dg = (sem(n) for n in ("x_tr", "x_sq", "x_ev", "x_eva", "x_dg"))
        ws_in, ws_tr, ws_ev, bd_in, gvb_in = (sem(n) for n in
                                                     ("ws_in", "ws_tr", "ws_ev", "bd_in", "gvb_in"))

        norm = {n: sem(f"norm_{n}") for n in ("sum", "rt", "hf", "hi", "lo")}
        turns = [Turn(norm, {n: (0, 2, 4, 7, 10)[t] if n in ("sum", "rt") else KD * t for n in norm})
                 for t in range(5)]
        nA, nG, nB = turns[0:2], [turns[2], turns[4]], turns[3]
        gmlp = {n: sem(f"A_{n}") for n in ("vev", "vtr", "vst", "vsq", "rv", "vs", "mix", "mt", "sz", "ut",
                                           "y", "yhi", "ylo", "xup")}
        sA = [Turn(gmlp, {n: g * {"vsq": 5, "rv": 1, "xup": KD}.get(n, KA) for n in gmlp}) for g in range(2)]
        vo_ok, vo_st = sem("vo_ok"), sem("vo_st")
        embed_sems = {n: sem(f"G_{n}") for n in ("pin", "pein", "ptr", "phi", "plo", "wph", "wpl", "pe", "sig",
                                                 "t", "xup")}
        sG = [Turn(embed_sems, {n: l * {"pin": 32, "pein": 16, "ptr": 6, "phi": 6, "plo": 8}.get(n, KD)
                                for n in embed_sems}) for l in range(2)]
        stat = sem("stat")
        xs_out, xs_in, tabI, tabQ, pt_in = (sem(n) for n in ("xs_out", "xs_in", "tabI", "tabQ", "pt_in"))
        iq = {n: sem(f"iq_{n}") for n in ("swa", "t1d", "add")}
        qq = {n: sem(f"qq_{n}") for n in ("swa", "t1d", "add", "st", "end", "rt")}
        kk_ = {n: sem(f"k_{n}") for n in ("swa", "t1d", "sum", "rt", "done", "vev", "st")}
        tt_tr, tt_ev = sem("tt_tr"), sem("tt_ev")
        iw_tr, iw_ev = sem("iw_tr"), sem("iw_ev")
        sc_mm, sc_re, sc_ad, sc_ok = sem("sc_mm"), sem("sc_re"), sem("sc_ad"), sem("sc_ok")
        ikp = [sem("ikp0"), sem("ikp1")]
        ss_ = {n: sem(f"ss_{n}") for n in ("pre", "tr", "ev", "mm", "re", "sum", "wt", "cp", "ok")}
        cs_ok = sem("cs_ok")
        z_ev, z_in = sem("z_ev"), [sem("z_in0"), sem("z_in1")]
        z_st = [sem("z_st0"), sem("z_st1")]
        at_ = {n: sem(f"at_{n}") for n in ("s", "mx", "nb", "ex", "nr", "tr", "pt", "pv", "o")}
        sa = {n: sem(f"sa_{n}") for n in ("pre", "qc", "kt", "ke", "s", "mx", "nb", "ex", "nr", "tr", "pt", "pv", "o")}
        kvp = [sem("kvp0"), sem("kvp1")]
        oy = {n: sem(f"oy_{n}") for n in ("y", "hi", "lo", "xup")}
        oy_turn = Turn(oy, {"lo": 0})
        xs = nc.dram_tensor("xs", [P, KD * TP], F32).ap()
        zs = nc.dram_tensor("zs", [KD, P, TP], F32).ap()
        tab = {n: nc.inline_tensor(a, name=n).ap() for n, a in
               zip(("tcI", "tsI", "tcQ", "tsQ"), rope_tables(ID // 2, 2) + rope_tables(DH // 2, 1))}
        STEPS = [(b, h) for b in range(NBLK) for h in range(NH)]
        PIECES = [(n, b, h, m) for n, (b, h) in enumerate(STEPS) for m in range((b + 4) // 4)]
        FIRST = [next(i for i, x in enumerate(PIECES) if x[0] == n) for n in range(len(STEPS))] + [len(PIECES)]
        SCORES = [(b, c, h) for b in range(2, NBLK) for c in range((b + 4) // 4) for h in range(IH)]

        y_tr, y_ev = sem("y_tr"), sem("y_ev")
        y_st = [sem("y_st0"), sem("y_st1")]

        block = ctx.enter_context(nc.Block())

        def split_hi(act, par, n, u):
            act.wait_ge(w_raw[par], 16 * n)
            if not (isinstance(u, int) and u < 2):
                act.wait_ge(w_used, u - 1)
            nc.scalar.activation(whi[par][:], wraw[par][:], ACT.Copy).then_inc(w_hi, 1)

        def split_lo(pool, par, u):
            pool.wait_ge(w_hi, u + 1)
            nc.gpsimd.tensor_tensor(wlo[par][:], wraw[par][:], whi[par][:].bitcast(F32),
                                    ALU.subtract).then_inc(w_lo, 1)

        def gemm(pe, par, out, rhs_hi, rhs_lo, first=True, last=True, kwait=None):
            for k in range(KD):
                if kwait is not None:
                    pe.wait_ge(kwait["lo"], kwait.at("lo", k + 1))
                for n, (w, r) in enumerate(((whi, rhs_hi), (whi, rhs_lo), (wlo, rhs_hi))):
                    for o, (c0, cn) in out:
                        mm = nc.tensor.matmul(o, w[par][:, k, :], r(k, c0, cn),
                                              start=first and k == 0 and n == 0,
                                              stop=last and k == KD - 1 and n == 2)
            return mm

        def norm_pe(pe, s, cols):
            for c, (a, n) in enumerate(cols):
                if c >= 2:
                    pe.wait_ge(s["rt"], s.at("rt", c - 1))
                nc.tensor.matmul(PS[:, 6 + c % 2, 0:n], ones[:], acc[:, a:a + n],
                                 start=True, stop=True).then_inc(s["sum"], 1)

        def norm_act(act, s, cols, hi):
            for c, (a, n) in enumerate(cols):
                act.wait_ge(s["sum"], s.at("sum", c + 1))
                nc.scalar.activation(rbc[:, a:a + n], PS[:, 6 + c % 2, 0:n], ACT.Sqrt,
                                     bias=eps[:], scale=1.0 / D).then_inc(s["rt"], 1)
            a, n = cols[0][0], sum(c[1] for c in cols)
            for k in range(KD):
                act.wait_ge(s["hf"], s.at("hf", k + 1))
                nc.scalar.activation(hi[0](k), hi[1](k), ACT.Copy).then_inc(s["hi"], 1)

        def norm_dve(dve, own, s, cols, g, hf, hi, lo):
            a, n = cols[0][0], sum(c[1] for c in cols)
            dve.wait_ge(s["rt"], s.at("rt", len(cols)))
            own.link(nc.vector.reciprocal(rbc[:, a:a + n], rbc[:, a:a + n]))
            for k in range(KD + 1):
                if k < KD:
                    if k >= 2:
                        dve.wait_ge(s["lo"], s.at("lo", k - 1))
                    nc.vector.scalar_tensor_tensor(hf(k), xT[:, k, a:a + n], g(k), rbc[:, a:a + n],
                                                   ALU.mult, ALU.mult).then_inc(s["hf"], 1)
                if k >= 1:
                    dve.wait_ge(s["hi"], s.at("hi", k))
                    dve.wait_ge(s["hf"], s.at("hf", k))
                    nc.vector.tensor_tensor(lo(k - 1), hf(k - 1), hi(k - 1).bitcast(F32),
                                            ALU.subtract).then_inc(s["lo"], 1)

        def group_cols(g):
            c0, n, _, _ = GROUPS[g]
            return [(c0, n // 2), (c0 + n // 2, n // 2)]

        ALL_COLS = [(NC3 * c, NC3) for c in range(3)]

        @block.sync
        def _(sp):
            def unit(par, u, src):
                if not (isinstance(u, int) and u < 2):
                    sp.wait_ge(w_lo, u - 1)
                sp.dma_start(wraw[par][:], src.rearrange("(k p) c -> p k c", p=P)).then_inc(w_raw[par], 16)

            def slab(w, row, col):
                return w[row:row + D, bass.ds(col, P)]

            def pair(w, col, i, ff):
                return w[:, bass.ds(col + 2 * P * i, 2 * P)][:, ff * P:(ff + 1) * P]

            for j in range(9):
                c0, n = tile_cols(j)
                if j >= 3:
                    sp.wait_ge(x_tr, j - 2)
                    sp.wait_ge(x_sq, j - 2)
                src = (x_sample.rearrange("b t d -> (b t) d") if j == 0
                       else x_prompt[0, CHUNK * (j - 1):CHUNK * j, :])
                sp.dma_start(xstage[0:n, j % 3, :], src).then_inc(x_in[j % 3], 16)
                if j == 2:
                    unit(0, 0, slab(w_in_a[0], 0, AW))
                    unit(1, 1, slab(w_in_a[0], 0, AW + P))
            for g in range(2):
                with sp.Fori(1 if g == 0 else 0, KA // 2) as i:
                    for ff in range(2):
                        unit(ff, U_A[g] + 2 * i + ff, pair(w_in_a[0], AW, i, ff))
                with sp.Fori(0, KA) as i:
                    unit(0, U_A[g] + KA + 2 * i, slab(w_in_a[0], 0, 2 * AW + i * P))
                    unit(1, U_A[g] + KA + 2 * i + 1, slab(w_in_a[0], 0, (2 * i) * (P // 2)))
                with sp.Fori(0, KD) as i:
                    for half in range(2):
                        unit(half, U_A[g] + 3 * KA + 2 * i + half, slab(w_out_a[0], half * D, i * P))

            def gate_loads(layer):
                base, s = U_GATE[layer], sG[layer]
                for ff in range(2):
                    unit((base + ff) % 2, base + ff, slab(w_pe_gate[layer], 0, ff * P))
                sp.wait_ge(nG[layer]["sum"], nG[layer].at("sum", 3))
                sp.dma_start(pst[0:NS, 0, :], p_sample[layer].rearrange("b t d -> (b t) d")).then_inc(s["pin"], 16)
                sp.dma_start(pst[:, 1:9, :], p_prompt[layer, 0].rearrange("(j p) d -> p j d", p=P)).then_inc(s["pin"], 16)
                sp.dma_start(peraw[:], w_pe_proj[layer].rearrange("(k p) c -> p k c", p=P)).then_inc(s["pein"], 16)
                with sp.Fori(1, KD // 2) as i:
                    for ff in range(2):
                        unit((base + ff) % 2, base + 2 * i + ff, pair(w_pe_gate[layer], 0, i, ff))

            gate_loads(0)
            for ff in range(2):
                unit(ff, U_IQ + ff, slab(w_in_b[0], 0, IQOFF + ff * P))
            sp.dma_start(ptab[:], page_table.rearrange("b n -> (b n)").unsqueeze(0)).then_inc(pt_in, 16)
            sp.wait_ge(nB["sum"], nB.at("sum", 3))
            sp.dma_start(csI[:], tab["tcI"]).then_inc(tabI, 16)
            sp.dma_start(snI[:], tab["tsI"]).then_inc(tabI, 16)
            for ff in range(2):
                unit(ff, U_IQ + 2 + ff, slab(w_in_b[0], 0, IQOFF + (2 + ff) * P))
            sp.wait_ge(nB["hf"], nB.at("hf", KD))
            sp.dma_start(xs, xT[:].rearrange("p f n -> p (f n)")).then_inc(xs_out, 16)
            unit(0, U_IK, slab(w_in_b[0], 0, IKOFF))
            unit(1, U_K, slab(w_in_b[0], 0, KOFF))
            sp.wait_ge(xs_out, 16)
            sp.wait_ge(pt_in, 16)
            for b in range(DEC_B):
                if b >= 2:
                    sp.wait_ge(ss_["tr"], b - 1)
                for g in range(NPAGE):
                    page = sp.value_load(ptab[0:1, b * NPAGE + g:b * NPAGE + g + 1],
                                         min_val=0, max_val=cache_ik.shape[0] - 1)
                    for q in range(2):
                        sp.dma_start(ikpg[b % 2][:, g, q, :],
                                     cache_ik[bass.ds(page, 1), 0].rearrange("a s d -> s (a d)")).then_inc(ikp[b % 2], 16)
            sp.wait_ge(ss_["cp"], 1)
            sp.dma_start(ik_prompt[0, 0].rearrange("(j p) d -> p j d", p=P), ikout[:, 1:9, :]).then_inc(kk_["st"], 16)
            sp.dma_start(ik_sample.rearrange("b l t d -> (b l t) d"), ikout[0:NS, 0, :]).then_inc(kk_["st"], 16)
            sp.dma_start(csQ[:], tab["tcQ"]).then_inc(tabQ, 16)
            sp.dma_start(snQ[:], tab["tsQ"]).then_inc(tabQ, 16)
            unit(0, U_K + 1, slab(w_in_b[0], 0, KOFF + P))
            for f in range(2):
                unit((U_V + f) % 2, U_V + f, slab(w_in_b[0], 0, VOFF + f * P))
            for ff in range(2):
                unit((U_Q + ff) % 2, U_Q + ff, slab(w_in_b[0], 0, ff * P))
            sp.wait_ge(tt_ev, 15)
            for t, pr, sm in ((kout, k_prompt, k_sample), (vtok, v_prompt, v_sample)):
                sp.dma_start(pr[0, 0].rearrange("(j p) g d -> p j (g d)", p=P), t[:, 1:9, :]).then_inc(kk_["st"], 16)
                sp.dma_start(sm.rearrange("b l t g d -> (b l t) (g d)"), t[0:NS, 0, :]).then_inc(kk_["st"], 16)
            for base, off in ((U_Q, 0), (U_Z, ZOFF)):
                with sp.Fori(1 if base == U_Q else 0, NH // 2) as i:
                    for ff in range(2):
                        unit((base + ff) % 2, base + 2 * i + ff, pair(w_in_b[0], off, i, ff))
            for ff in range(2):
                unit((U_O + ff) % 2, U_O + ff, slab(w_out_b[0], 0, ff * P))
            sp.wait_ge(w_used, U_O)
            for b in range(DEC_B):
                if b >= 2:
                    sp.wait_ge(sa["pv"], b - 1)
                for g in range(NPAGE):
                    page = sp.value_load(ptab[0:1, b * NPAGE + g:b * NPAGE + g + 1],
                                         min_val=0, max_val=cache_k.shape[0] - 1)
                    for dst, src in ((kpg, cache_k), (vpg, cache_v)):
                        sp.dma_start(dst[b % 2][:, g, :],
                                     src[bass.ds(page, 1), 0].rearrange("a s g d -> s (a g d)")).then_inc(kvp[b % 2], 16)
            sp.wait_ge(sa["o"], DEC_B)
            sp.dma_start(xT[:].rearrange("p f n -> p (f n)"), xs).then_inc(xs_in, 16)
            for q in range(2):
                sp.wait_ge(z_st[q], 16 * (KD // 2))
            for f in range(KD):
                if f >= 2:
                    sp.wait_ge(oy["y"], f - 1)
                sp.dma_start(zst[f % 2][:], zs[f]).then_inc(z_in[f % 2], 16)
            with sp.Fori(1, KD // 2) as i:
                for ff in range(2):
                    unit((U_O + ff) % 2, U_O + 2 * i + ff, pair(w_out_b[0], 0, i, ff))
            gate_loads(1)
            sp.wait_ge(kk_["st"], 16 * 6)

        @block.gpsimd
        def _(pool):
            own = Tally(pool, gv_)
            nc.gpsimd.memset(ones[:], 1.0).then_inc(cst, 1)
            nc.gpsimd.memset(eps[:], EPS).then_inc(cst, 1)
            nc.gpsimd.memset(acc[:], 0.0).then_inc(cst, 1)
            nc.gpsimd.memset(xT[:, :, NT:TP], 0.0).then_inc(cst, 1)
            nc.gpsimd.memset(ss[:], 1.0).then_inc(cst, 1)
            nc.gpsimd.memset(sv[:], 1.0).then_inc(cst, 1)
            own.link(nc.gpsimd.memset(ident[:], 0.0))
            nc.gpsimd.affine_select(out=ident[:], in_=ident[:], compare_op=ALU.not_equal, fill=1.0, base=0,
                                    pattern=[[-1, P]], channel_multiplier=1).then_inc(cst, 1)
            own.link(nc.gpsimd.memset(wsbd[:], 0.0))
            pool.dma_start(wsraw[:], w_s_a[0].rearrange("g t s -> t g s")).then_inc(ws_in, 16)
            col = "(p o) -> p o"
            for j, src in ((0, g_q_b[0]), (1, g_k_b[0])):
                pool.dma_start(gqk[:, j:j + 1], src.rearrange(col, o=1)).then_inc(cst_dma, 16)
            for h in range(2):
                pool.dma_start(gqk[ID * h:ID * h + ID, 2:3], g_ik_b[0].rearrange(col, o=1)).then_inc(cst_dma, 16)
            for l in range(2):
                for dst, src in ((gn, g_norm), (gp, g_pe)):
                    pool.dma_start(dst[:, l, :], src[l].rearrange("(f p) -> p f", p=P),
                                   allow_slow_non_contiguous=True).then_inc(cst_dma, 16)
            pool.dma_start(gv[:], g_v_a[0].rearrange("(f p) -> p f", p=P),
                           allow_slow_non_contiguous=True).then_inc(cst_dma, 16)
            pool.dma_start(bsb[:].rearrange("p g t -> p (g t)"),
                           b_s_a[0].rearrange("g t -> (g t)").partition_broadcast(P)).then_inc(cst_dma, 16)
            pool.dma_start(gvb[:], g_v_a[0].partition_broadcast(NS)).then_inc(gvb_in, 16)
            split_lo(pool, 0, 0)
            pool.wait_ge(ws_ev, 2)
            own.link(nc.gpsimd.affine_select(out=wsT[:], in_=wsT[:], compare_op=ALU.is_ge, fill=0.0, base=0,
                                             pattern=[[0, NGRP], [1, P]], channel_multiplier=-1))
            for b in range(DEC_B):
                s = slice(DEC_T * b, DEC_T * b + DEC_T)
                pool.dma_start(wsbd[s, :, s], wsT[0:DEC_T, :, 0:DEC_T]).then_inc(bd_in, 16)

            def add_squares(sq, f, a, n):
                own.link(nc.gpsimd.tensor_tensor(sq, xT[:, f, a:a + n], xT[:, f, a:a + n], ALU.mult))
                own.link(nc.gpsimd.tensor_tensor(acc[:, a:a + n], acc[:, a:a + n], sq, ALU.add))

            for g in range(2):
                c0, n, _, _ = GROUPS[g]
                for base, trips in ((U_A[g], KA // 2), (U_A[g] + KA, KA)):
                    with pool.Fori(0, trips) as i:
                        for ff in range(2):
                            split_lo(pool, (ff + 1) % 2, base + 2 * i + ff + 1)
                pool.wait_ge(nA[g]["sum"], nA[g].at("sum", 2))
                own.link(nc.gpsimd.memset(acc[:, c0:c0 + n], 0.0))
                with pool.Fori(0, KD // 2) as i:
                    own.enter(i, 4)
                    for ff in range(2):
                        for half in range(2):
                            u = U_A[g] + 3 * KA + 4 * i + 2 * ff + half + 1
                            split_lo(pool, (half + 1) % 2, u)
                        pool.wait_ge(sA[g]["xup"], sA[g].at("xup", 2 * i + ff + 3))
                        add_squares(sqa[:, 0:n], bass.ds(2 * i + ff, 1), c0, n)
                own.leave(KD // 2)
                pool.sem_inc(stat, 1)

            def gate_pool(layer, last):
                s, base = sG[layer], U_GATE[layer]
                pool.wait_ge(nG[layer]["sum"], nG[layer].at("sum", 3))
                own.link(nc.gpsimd.memset(acc[:], 0.0))
                nc.gpsimd.memset(pThi[:, :, NT:TP].bitcast(F32), 0.0).then_inc(s["plo"], 1)
                nc.gpsimd.memset(pTlo[:, :, NT:TP].bitcast(F32), 0.0).then_inc(s["plo"], 1)

                def tile(i, ff):
                    f = 2 * i + ff
                    pool.wait_ge(s["wph"], s.at("wph", f + 1))
                    nc.gpsimd.tensor_tensor(pelo[:], peraw[:, :, bass.ds(f * P, P)], pehi[:].bitcast(F32),
                                            ALU.subtract).then_inc(s["wpl"], 1)
                    if not (last and f == KD - 1):
                        split_lo(pool, (base + ff + 1) % 2, base + f + 1)
                    if not last:
                        pool.wait_ge(s["xup"], s.at("xup", f + 2))
                        add_squares(sqb, bass.ds(f, 1), 0, TP)

                if last:
                    for f in range(KD):
                        tile(f // 2, f % 2)
                else:
                    with pool.Fori(0, KD // 2) as i:
                        own.enter(i, 4)
                        for ff in range(2):
                            tile(i, ff)
                    own.leave(KD // 2)
                    pool.sem_inc(stat, 1)

            gate_pool(0, False)
            for f in range(IH // 2):
                split_lo(pool, (U_IQ + f + 1) % 2, U_IQ + f + 1)
            split_lo(pool, 1, U_K)
            own.link(nc.gpsimd.memset(caus[:], 0.0))
            nc.gpsimd.affine_select(out=caus[:, P:2 * P], in_=caus[:, P:2 * P], compare_op=ALU.is_ge, fill=-BIG,
                                    base=0, pattern=[[-1, P]], channel_multiplier=1).then_inc(cs_ok, 1)
            pool.wait_ge(xs_out, 16)
            nc.gpsimd.memset(iqb[:], 0.0).then_inc(ss_["pre"], 1)
            nscore = 0
            for b in range(2, NBLK):
                nscore += IH * ((b + 4) // 4)
                pool.wait_ge(sc_ad, nscore)
                d = slice(block_off(b) + b * P, block_off(b) + (b + 1) * P)
                nc.gpsimd.affine_select(out=sc[:, d], in_=sc[:, d], compare_op=ALU.is_ge, fill=MASKED, base=0,
                                        pattern=[[-1, P]], channel_multiplier=1).then_inc(sc_ok, 1)
            pool.wait_ge(ss_["cp"], 1)
            new = scs[:, PAST:SLS]
            own.link(nc.gpsimd.affine_select(out=new, in_=new, compare_op=ALU.is_ge, fill=MASKED, base=0,
                                             pattern=[[-1, NS]], channel_multiplier=1))
            nc.gpsimd.affine_select(out=new.rearrange("p (b t) -> p b t", t=DEC_T),
                                    in_=new.rearrange("p (b t) -> p b t", t=DEC_T), compare_op=ALU.is_ge,
                                    fill=MASKED, base=DEC_T - 1, pattern=[[DEC_T, DEC_B], [0, DEC_T]],
                                    channel_multiplier=-1).then_inc(ss_["ok"], 1)
            for u in range(U_K + 1, U_Q + 1):
                split_lo(pool, u % 2, u)
            for base in (U_Q, U_Z):
                with pool.Fori(0, NH // 2) as i:
                    for ff in range(2):
                        split_lo(pool, (base + ff + 1) % 2, base + 2 * i + ff + 1)
            pool.wait_ge(nB["sum"], nB.at("sum", 3))
            own.link(nc.gpsimd.memset(acc[:], 0.0))
            with pool.Fori(0, KD // 2) as i:
                own.enter(i, 4)
                for ff in range(2):
                    split_lo(pool, (U_O + ff + 1) % 2, U_O + 2 * i + ff + 1)
                    pool.wait_ge(oy["xup"], 2 * i + ff + 3)
                    add_squares(sqt[:], bass.ds(2 * i + ff, 1), 0, TP)
            own.leave(KD // 2)
            pool.sem_inc(stat, 1)
            gate_pool(1, True)

        @block.scalar
        def _(act):
            own = Tally(act, av)
            for name, free in (("vev", 2), ("sz", 1)):
                act.sem_inc(gmlp[name], free)
            act.sem_inc(embed_sems["sig"], 1)
            act.sem_inc(iq["swa"], 2)
            act.sem_inc(qq["swa"], 2)
            act.sem_inc(z_ev, 2)
            act.wait_ge(cst, 7)
            for j in range(9):
                c0, n = tile_cols(j)
                act.wait_ge(x_in[j % 3], 16 * (j // 3 + 1))
                if j:
                    act.wait_ge(x_sq, j)
                nc.scalar.activation(sqdump[0:n, :], xstage[0:n, j % 3, :], ACT.Square,
                                     accum_out=ss[0:n, j:j + 1]).then_inc(x_sq, 1)
                act.wait_ge(x_tr, j + 1)
                nc.scalar.activation(xT[:, 4:8, c0:c0 + n],
                                     PSF[:, (2 * (j % 3) + 1) * BANK:(2 * (j % 3) + 2) * BANK]
                                     .rearrange("p (k t) -> p k t", k=4)[:, :, 0:n], ACT.Copy).then_inc(x_eva, 1)
            split_hi(act, 0, 1, 0)
            act.wait_ge(ws_tr, 2)
            for h in range(2):
                nc.scalar.activation(wsT[:, 4 * h:4 * h + 4, :].rearrange("p g t -> p (g t)"),
                                     PS[:, 6 + h, :], ACT.Copy).then_inc(ws_ev, 1)

            for g in range(2):
                c0, n, nch, has_s = GROUPS[g]
                h = n // 2
                s = sA[g]
                norm_act(act, nA[g], group_cols(g),
                         (lambda k: hhi_g[:, k, 0:n], lambda k: hfa[:, k % 2, 0:n]))
                with act.Fori(0, KA // 2) as i:
                    for ff in range(2):
                        u = U_A[g] + 2 * i + ff
                        split_hi(act, (ff + 1) % 2, (U_A[g] + ff + 1) // 2 + i + 1, u + 1)
                        act.wait_ge(w_used, u + 1)
                        act.wait_ge(s["vtr"], s.at("vtr", 2 * i + ff + 1))
                        nc.scalar.activation(vtmp[ff][:, 0:n].rearrange("p (b n) -> p b n", b=2),
                                             PS[:, 2 * ff:2 * ff + 2, 0:h], ACT.Copy).then_inc(s["vev"], 1)
                act.wait_ge(s["vst"], s.at("vst", KA + 2))
                for c in range(nch + has_s):
                    rows = P if c < nch else NS
                    if c:
                        act.wait_ge(s["vsq"], s.at("vsq", c))
                    nc.scalar.activation(vdump[0:rows], v_raw[0:rows, :, c * P:(c + 1) * P], ACT.Square,
                                         accum_out=sv[0:rows, c:c + 1]).then_inc(s["vsq"], 1)
                act.wait_ge(s["vsq"], s.at("vsq", nch + has_s))
                nc.scalar.activation(rv[:], sv[:], ACT.Sqrt, bias=eps[:], scale=1.0 / AW).then_inc(s["rv"], 1)
                if has_s:
                    act.wait_ge(vo_ok, 1)
                    act.dma_start(chunk_v_sample.rearrange("b l t w -> (b l t) w"), v_out[:]).then_inc(vo_st, 16)
                with act.Fori(0, KA) as f:
                    for half in range(2):
                        u = U_A[g] + KA + 2 * f + half
                        split_hi(act, (half + 1) % 2, (U_A[g] + KA + half + 1) // 2 + f + 1, u + 1)
                        if half == 0:
                            act.wait_ge(w_used, u + 1)
                            act.wait_ge(s["ut"], s.at("ut", f + 1))
                            nc.scalar.activation(szt[:, 0:n].rearrange("p (b n) -> p b n", b=2),
                                                 PS[:, 0:2, 0:h], ACT.Silu).then_inc(s["sz"], 1)
                    act.wait_ge(s["y"], s.at("y", f + 1))
                    nc.scalar.activation(yhi[:, bass.ds(f, 1), 0:n], t1a[:, 0:n].unsqueeze(1), ACT.Copy).then_inc(s["yhi"], 1)
                with act.Fori(0, KD) as f:
                    for half in range(2):
                        u = U_A[g] + 3 * KA + 2 * f + half
                        split_hi(act, (half + 1) % 2, (U_A[g] + 3 * KA + half + 1) // 2 + f + 1, u + 1)

            def gate_act(layer, last):
                s, base = sG[layer], U_GATE[layer]
                norm_act(act, nG[layer], ALL_COLS, (lambda k: hhi[:, k, :], lambda k: hfb[:, k % 2, :]))
                act.wait_ge(s["ptr"], s.at("ptr", 6))
                act.wait_ge(s["plo"], s.at("plo", 2))
                for kk in range(2):
                    for m, (a, n) in enumerate(((NS, 512), (NS + 512, 512), (0, NS))):
                        nc.scalar.activation(pThi[:, kk, a:a + n], PS[:, 3 * kk + m, 0:n], ACT.Copy).then_inc(s["phi"], 1)
                act.wait_ge(s["pein"], s.at("pein", 16))

                def tile(i, ff):
                    f = 2 * i + ff
                    act.wait_ge(s["pe"], s.at("pe", f + 1))
                    nc.scalar.activation(pehi[:], peraw[:, :, bass.ds(f * P, P)], ACT.Copy).then_inc(s["wph"], 1)
                    if not (last and f == KD - 1):
                        split_hi(act, (base + ff + 1) % 2, (base + ff + 1) // 2 + i + 1, base + f + 1)
                    act.wait_ge(w_used, base + f + 1)
                    act.wait_ge(s["t"], s.at("t", f + 1))
                    nc.scalar.activation(as3(sig[:]), slot3(0), ACT.Sigmoid).then_inc(s["sig"], 1)

                if last:
                    for f in range(KD):
                        tile(f // 2, f % 2)
                        if f >= 1:
                            store_tile(f - 1)
                    store_tile(KD - 1)
                else:
                    with act.Fori(0, KD // 2) as i:
                        for ff in range(2):
                            tile(i, ff)

            def store_tile(f):
                act.wait_ge(y_ev, 3 * f + 4)
                act.dma_start(y_sample.rearrange("b t d -> (b t) d")[:, f * P:(f + 1) * P],
                              ystage[0:NS, f % 2, 0, :]).then_inc(y_st[f % 2], 16)
                act.dma_start(y_prompt[0, :, f * P:(f + 1) * P].rearrange("(j p) d -> p j d", p=P),
                              ystage[:, f % 2, 1:9, :]).then_inc(y_st[f % 2], 16)

            gate_act(0, False)
            norm_act(act, nB, ALL_COLS, (lambda k: hhi[:, k, :], lambda k: hfb[:, k % 2, :]))

            def swap(dst, slot, size, scale, n=P):
                for p0 in range(0, n, 2 * size):
                    for a, b in ((p0, p0 + size), (p0 + size, p0)):
                        last = nc.scalar.activation(as3(dst[a:a + size, :]), slot3(slot)[b:b + size], ACT.Copy,
                                                    scale=1.0 if scale is None else scale[b:b + size])
                return last

            with act.Fori(0, IH // 4) as i:
                for ff in range(2):
                    f = 2 * i + ff
                    split_hi(act, (ff + 1) % 2, (U_IQ + ff + 1) // 2 + i + 1, U_IQ + f + 1)
                    act.wait_ge(w_used, U_IQ + f + 1)
                    act.wait_ge(iq["add"], f + 1)
                    act.wait_ge(iq["t1d"], f + 3)
                    swap(swp, ff, ID // 2, None).then_inc(iq["swa"], 1)
            split_hi(act, 1, (U_K) // 2 + 1, U_K)
            act.wait_ge(w_used, U_IK + 1)
            act.wait_ge(iq["add"], 5)
            nc.scalar.activation(as3(sqt[0:ID, :]), slot3(0)[0:ID], ACT.Square).then_inc(kk_["swa"], 1)
            for q in range(2):
                nc.scalar.activation(as3(ikT[ID * q:ID * q + ID, :]), slot3(0)[0:ID], ACT.Copy, scale=gqk[0:ID, 2:3])
                for a, b in ((0, ID // 2), (ID // 2, 0)):
                    nc.scalar.activation(as3(swp[ID * q + a:ID * q + a + ID // 2, :]), slot3(0)[b:b + ID // 2],
                                         ACT.Copy, scale=gqk[b:b + ID // 2, 2:3])
            nc.scalar.activation(as3(iwT[:]), slot3(0)[ID:ID + IH], ACT.Copy).then_inc(kk_["swa"], 1)

            def roots(n, dim):
                for c, (a, m) in enumerate(ALL_COLS):
                    act.wait_ge(kk_["sum"], 3 * n + c + 1)
                    nc.scalar.activation(rbc[:, a:a + m], PS[:, 6 + c % 2, 0:m], ACT.Sqrt, bias=eps[:],
                                         scale=1.0 / dim).then_inc(kk_["rt"], 1)

            roots(0, ID)
            for m, (b, c, h) in enumerate(SCORES):
                n = min(BANK, (b + 1) * P - c * BANK)
                act.wait_ge(sc_mm, m + 1)
                if m >= 2:
                    act.wait_ge(sc_ad, m - 1)
                nc.scalar.activation(pring[m % 2][:, 0:n], PS[:, m % 6, 0:n], ACT.Relu).then_inc(sc_re, 1)

            def ikT_evac(b):
                act.wait_ge(ss_["tr"], b + 1)
                if b >= 2:
                    act.wait_ge(ss_["mm"], b - 1)
                nc.scalar.activation(ikTb[b % 2][:], PSF[:, 6 * BANK:8 * BANK], ACT.Copy).then_inc(ss_["ev"], 1)

            act.wait_ge(ss_["wt"], 1)
            nc.scalar.activation(sbw[:].rearrange("p b n -> p (b n)"), PS[0:NS, 5, :], ACT.Copy).then_inc(ss_["wt"], 1)
            ikT_evac(0)
            for b in range(DEC_B):
                if b + 1 < DEC_B:
                    ikT_evac(b + 1)
                act.wait_ge(ss_["mm"], b + 1)
                if b:
                    act.wait_ge(ss_["sum"], b)
                nc.scalar.activation(rels[:], PSF[0:NS, 3 * BANK:3 * BANK + SLS], ACT.Relu).then_inc(ss_["re"], 1)

            for g in range(NKV):
                u = U_K + g
                split_hi(act, (u + 1) % 2, (u + 1) // 2 + 1, u + 1)
                act.wait_ge(w_used, u + 1)
                if g == 0:
                    act.wait_ge(sc_ad, len(SCORES))
                act.wait_ge(kk_["done"], g + 1)
                act.wait_ge(kk_["t1d"], g + 1)
                nc.scalar.activation(as3(sqt[:]), slot3(u % 2), ACT.Square).then_inc(kk_["swa"], 1)
                swap(swp, u % 2, DH // 2, gqk[:, 1:2]).then_inc(kk_["swa"], 1)
                roots(1 + g, DH)
            for g in range(NKV):
                u = U_V + g
                split_hi(act, (u + 1) % 2, (u + 1) // 2 + 1, u + 1)
                act.wait_ge(w_used, u + 1)
                act.wait_ge(kk_["done"], 3)
                if g:
                    act.wait_ge(tt_tr, 12)
                nc.scalar.activation(as3(sqt[:]), slot3(u % 2), ACT.Copy).then_inc(kk_["vev"], 1)
            act.wait_ge(tt_tr, 15)
            with act.Fori(0, NH // 2) as i:
                for ff in range(2):
                    f = 2 * i + ff
                    split_hi(act, (U_Q + ff + 1) % 2, (U_Q + ff + 1) // 2 + i + 1, U_Q + f + 1)
                    act.wait_ge(w_used, U_Q + f + 1)
                    act.wait_ge(qq["add"], f + 1)
                    act.wait_ge(qq["t1d"], f + 3)
                    act.wait_ge(qq["st"], f + 1)
                    slot = (U_Q + ff) % 2
                    nc.scalar.activation(as3(sqt[:]), slot3(slot), ACT.Square)
                    swap(swp, slot, DH // 2, gqk[:, 0:1]).then_inc(qq["swa"], 1)
            act.wait_ge(qq["end"], 1)
            for rows, j in ((NS, slice(0, 1)), (P, slice(1, 9))):
                nc.scalar.activation(qs[0:rows, j, :], PS[0:rows, 7, 0:9 * NH].rearrange("p (j h) -> p j h", h=NH)[:, j],
                                     ACT.Sqrt, bias=eps[0:rows], scale=1.0 / DH).then_inc(qq["rt"], 1)
            act.wait_ge(qq["add"], 9)
            for f in range(KD):
                split_hi(act, (U_Z + f + 1) % 2, (U_Z + f + 1) // 2 + 1, U_Z + f + 1)
                act.wait_ge(w_used, U_Z + f + 1)
                if f >= 2:
                    act.wait_ge(z_st[f % 2], 16 * (f // 2))
                nc.scalar.activation(as3(zst[f % 2][:]), slot3((U_Z + f) % 2), ACT.Silu).then_inc(z_ev, 1)
                act.wait_ge(z_ev, f + 3)
                act.dma_start(zs[f], zst[f % 2][:]).then_inc(z_st[f % 2], 16)

            def pieces_out(n):
                for i in range(FIRST[n], FIRST[n + 1]):
                    _, b, h, m = PIECES[i]
                    k = min(4, b + 1 - 4 * m)
                    act.wait_ge(at_["tr"], i + 1)
                    if h % REP == 0 and n >= REP:
                        act.wait_ge(at_["pv"], n // REP)
                    nc.scalar.activation(PTs[:, 4 * m:4 * m + k, h % REP, :],
                                         PS[:, 4 + i % 2, 0:k * P].rearrange("p (k q) -> p k q", q=P),
                                         ACT.Copy).then_inc(at_["pt"], 1)

            for n, (b, h) in enumerate(STEPS):
                w = (b + 1) * P
                act.wait_ge(at_["nb"], n + 1)
                nc.scalar.activation(pring[n % 2][:, 0:w], pring[n % 2][:, 0:w], ACT.Exp, bias=anb[:, n:n + 1],
                                     scale=qs[:, 1 + b, h:h + 1], accum_out=asm[:, n:n + 1]).then_inc(at_["ex"], 1)
                if n:
                    pieces_out(n - 1)
            pieces_out(len(STEPS) - 1)

            act.wait_ge(sa["qc"], 1)
            nc.scalar.activation(qcol[:], PS[0:NS, 3, 0:DEC_B], ACT.Copy)
            nc.scalar.activation(nqcol[:], PS[0:NS, 3, 0:DEC_B], ACT.Copy, scale=-1.0).then_inc(sa["qc"], 1)

            def kT_evac(b):
                act.wait_ge(sa["kt"], b + 1)
                if b:
                    act.wait_ge(sa["s"], b)
                for g in range(NKV):
                    last = nc.scalar.activation(kTb[:, g, :], PSF[:, (4 + 2 * g) * BANK:(6 + 2 * g) * BANK], ACT.Copy)
                last.then_inc(sa["ke"], 1)

            kT_evac(0)
            for b in range(DEC_B):
                act.wait_ge(sa["nb"], b + 1)
                if b:
                    act.wait_ge(sa["tr"], b)
                nc.scalar.activation(Ps[:], PSF[0:NS, 0:SLS], ACT.Exp, bias=snb[:, b:b + 1], scale=qcol[:, b:b + 1],
                                     accum_out=ssm[:, b:b + 1]).then_inc(sa["ex"], 1)
                if b + 1 < DEC_B:
                    kT_evac(b + 1)
                act.wait_ge(sa["tr"], b + 1)
                if b:
                    act.wait_ge(sa["pv"], b)
                nc.scalar.activation(PsT[:, 0:8, :].rearrange("p k n -> p (k n)"), PS[:, 3, :], ACT.Copy)
                nc.scalar.activation(PsT[0:NS, 8, :], PS[0:NS, 2, 2 * NS:3 * NS], ACT.Copy).then_inc(sa["pt"], 1)

            for f in range(KD):
                act.wait_ge(oy["y"], f + 1)
                nc.scalar.activation(hhi[:, f, :], qT[:, f, :], ACT.Copy).then_inc(oy["hi"], 1)
            with act.Fori(0, KD // 2) as i:
                for ff in range(2):
                    split_hi(act, (U_O + ff + 1) % 2, (U_O + ff + 1) // 2 + i + 1, U_O + 2 * i + ff + 1)
            gate_act(1, True)
            for q in range(2):
                act.wait_ge(y_st[q], 32 * KD // 2)
            act.wait_ge(vo_st, 16)

        @block.vector
        def _(dve):
            own = Tally(dve, dv)
            for name, free in (("vst", 2), ("ut", 1), ("mt", 1), ("xup", 2), ("ylo", 1)):
                dve.sem_inc(gmlp[name], free)
            for name in ("t", "xup"):
                dve.sem_inc(embed_sems[name], 1)
            dve.sem_inc(y_ev, 1)
            for q in (iq, qq):
                dve.sem_inc(q["t1d"], 2)
                dve.sem_inc(q["add"], 1)
            dve.sem_inc(oy["xup"], 2)
            dve.wait_ge(cst, 7)
            dve.wait_ge(cst_dma, 16 * 10)
            for j in range(9):
                c0, n = tile_cols(j)
                dve.wait_ge(x_tr, j + 1)
                nc.vector.tensor_copy(xT[:, 0:4, c0:c0 + n],
                                      PSF[:, 2 * (j % 3) * BANK:(2 * (j % 3) + 1) * BANK]
                                      .rearrange("p (k t) -> p k t", k=4)[:, :, 0:n]).then_inc(x_ev, 1)
                dve.wait_ge(x_sq, j + 1)
                nc.vector.tensor_scalar(acc[0:n, c0:c0 + n], ident[0:n, 0:n], ss[0:n, j:j + 1], None,
                                        ALU.mult).then_inc(x_dg, 1)

            for g in range(2):
                c0, n, nch, has_s = GROUPS[g]
                h = n // 2
                s = sA[g]
                if g:
                    dve.wait_ge(stat, g)
                norm_dve(dve, own, nA[g], group_cols(g), lambda k: gn[:, 0, k:k + 1],
                         lambda k: hfa[:, k % 2, 0:n], lambda k: hhi_g[:, k, 0:n], lambda k: hlo_g[:, k, 0:n])
                dve.wait_ge(bd_in, 16 * DEC_B)
                with dve.Fori(0, KA // 2) as i:
                    for ff in range(2):
                        f = 2 * i + ff
                        dve.wait_ge(s["vtr"], s.at("vtr", f + 3))
                        vdst = nc.vector.tensor_copy(v_raw[:, bass.ds(f, 1), 0:4 * P].rearrange("p o n -> p (o n)"),
                                                     PS[:, 4 + 2 * ff, :])
                        if has_s:
                            vdst = nc.vector.tensor_copy(
                                v_raw[0:NS, bass.ds(f, 1), 4 * P:5 * P].rearrange("p o n -> p (o n)"),
                                PS[0:NS, 5 + 2 * ff, 0:P])
                        vdst.then_inc(s["vst"], 1)
                dve.wait_ge(s["rv"], s.at("rv", 1))
                own.link(nc.vector.reciprocal(rv[:], rv[:]))
                if has_s:
                    dve.wait_ge(gvb_in, 16)
                    nc.vector.scalar_tensor_tensor(
                        v_out[:].rearrange("p (f d) -> p f d", d=P), v_raw[0:NS, :, 4 * P:5 * P], rv[0:NS, 4:5],
                        gvb[:].rearrange("p (f d) -> p f d", d=P), ALU.mult, ALU.mult).then_inc(vo_ok, 1)
                if n > nch * P + (NS if has_s else 0):
                    own.link(nc.vector.memset(t1a[:, nch * P:n], 0.0))
                po = NS if has_s else 0
                with dve.Fori(0, KA // 2) as i:
                    own.enter(i, 4)
                    for ff in range(2):
                        f = 2 * i + ff
                        for c in range(nch + has_s):
                            rows = P if c < nch else NS
                            scaled = nc.vector.tensor_scalar(
                                vs[0:rows, c * P:(c + 1) * P],
                                v_raw[0:rows, bass.ds(f, 1), c * P:(c + 1) * P].rearrange("p o n -> p (o n)"),
                                rv[0:rows, c:c + 1], None, ALU.mult)
                        scaled.then_inc(s["vs"], 1)
                        dve.wait_ge(w_used, U_A[g] + KA + 2 * f + 2)
                        dve.wait_ge(s["sz"], s.at("sz", f + 2))
                        nc.vector.tensor_tensor(t2a[:, 0:n].rearrange("p (b n) -> p b n", b=2),
                                                PS[:, 2:4, 0:h],
                                                szt[:, 0:n].rearrange("p (b n) -> p b n", b=2),
                                                ALU.mult).then_inc(s["ut"], 1)
                        dve.wait_ge(s["mix"], s.at("mix", f + 1))
                        dve.wait_ge(s["ylo"], s.at("ylo", f + 1))
                        if has_s:
                            nc.vector.scalar_tensor_tensor(
                                t1a[:, 0:NS].rearrange("p (b t) -> p b t", t=DEC_T),
                                PS[:, 5, 0:NS].rearrange("p (b t) -> p b t", t=DEC_T), gv[:, bass.ds(f, 1)],
                                bsb[:, bass.ds(i, 1), 0:DEC_T].broadcast_to((P, DEC_B, DEC_T)), ALU.mult, ALU.add)
                        own.link(nc.vector.scalar_tensor_tensor(
                            t1a[:, po:po + 4 * P].rearrange("p (c t) -> p c t", t=P),
                            PS[:, 4, :].rearrange("p (c t) -> p c t", t=P), gv[:, bass.ds(f, 1)],
                            bsb[:, bass.ds(i, 1), :].broadcast_to((P, 4, P)), ALU.mult, ALU.add))
                        dve.wait_ge(s["ut"], s.at("ut", f + 2))
                        own.link(nc.vector.tensor_tensor(t1a[:, 0:n], t1a[:, 0:n], t2a[:, 0:n], ALU.mult))
                        dve.sem_inc(s["mt"], 1)
                        dve.sem_inc(s["y"], 1)
                        if has_s:
                            dve.wait_ge(vo_st, 16)
                        dve.wait_ge(s["yhi"], s.at("yhi", f + 1))
                        nc.vector.tensor_tensor(ylo[:, bass.ds(f, 1), 0:n], t1a[:, 0:n].unsqueeze(1),
                                                yhi[:, bass.ds(f, 1), 0:n].bitcast(F32), ALU.subtract).then_inc(s["ylo"], 1)
                own.leave(KA // 2)
                with dve.Fori(0, KD // 2) as i:
                    for ff in range(2):
                        f = 2 * i + ff
                        dve.wait_ge(w_used, U_A[g] + 3 * KA + 2 * f + 2)
                        x = xT[:, bass.ds(f, 1), c0:c0 + n].rearrange("p o (b n) -> p (o b) n", b=2)
                        nc.vector.tensor_tensor(x, PS[:, 2 * ff:2 * ff + 2, 0:h], x, ALU.add).then_inc(s["xup"], 1)

            def gate_dve(layer, last):
                s, base = sG[layer], U_GATE[layer]
                norm_dve(dve, own, nG[layer], ALL_COLS, lambda k: gp[:, layer, k:k + 1],
                         lambda k: hfb[:, k % 2, :], lambda k: hhi[:, k, :], lambda k: hlo[:, k, :])
                for kk in range(2):
                    for m, (a, n) in enumerate(((NS, 512), (NS + 512, 512), (0, NS))):
                        dve.wait_ge(s["phi"], s.at("phi", 3 * kk + m + 1))
                        nc.vector.tensor_tensor(pTlo[:, kk, a:a + n], PS[:, 3 * kk + m, 0:n],
                                                pThi[:, kk, a:a + n].bitcast(F32), ALU.subtract).then_inc(s["plo"], 1)

                def tile(i, ff):
                    f = 2 * i + ff
                    dve.wait_ge(s["pe"], s.at("pe", f + 2))
                    dve.wait_ge(s["sig"], s.at("sig", f + 2))
                    dve.wait_ge(s["xup"], s.at("xup", f + 1))
                    nc.vector.tensor_tensor(as3(tpe[:]), slot3(1), as3(sig[:]), ALU.mult).then_inc(s["t"], 1)
                    dve.wait_ge(s["t"], s.at("t", f + 2))
                    if last:
                        nc.vector.tensor_tensor(xo[:, ff, :], xT[:, f, :], tpe[:], ALU.add).then_inc(s["xup"], 1)
                    else:
                        x = xT[:, bass.ds(f, 1), :].rearrange("p o n -> p (o n)")
                        nc.vector.tensor_tensor(x, x, tpe[:], ALU.add).then_inc(s["xup"], 1)

                if last:
                    for f in range(KD):
                        if f >= 1:
                            evac_out(f - 1)
                        tile(f // 2, f % 2)
                    evac_out(KD - 1)
                else:
                    with dve.Fori(0, KD // 2) as i:
                        for ff in range(2):
                            tile(i, ff)

            def evac_out(f):
                if f >= 2:
                    dve.wait_ge(y_st[f % 2], 32 * (f // 2))
                for m in range(3):
                    dve.wait_ge(y_tr, 3 * f + m + 1)
                    if m < 2:
                        nc.vector.tensor_copy(ystage[:, f % 2, 1 + 4 * m:5 + 4 * m, :],
                                              PS[:, 6 + m, :].rearrange("p (j d) -> p j d", d=P)).then_inc(y_ev, 1)
                    else:
                        nc.vector.tensor_copy(ystage[0:NS, f % 2, 0, :], PS[0:NS, 6, 0:P]).then_inc(y_ev, 1)

            gate_dve(0, False)
            norm_dve(dve, own, nB, ALL_COLS, lambda k: gn[:, 1, k:k + 1],
                     lambda k: hfb[:, k % 2, :], lambda k: hhi[:, k, :], lambda k: hlo[:, k, :])

            def rotate(s, used, f, slot, dst, cs, sn, g):
                dve.wait_ge(w_used, used + 1)
                dve.wait_ge(s["add"], f + 1)
                if g is None:
                    t = nc.vector.tensor_tensor(as3(tq[:]), slot3(slot), as3(cs[:]), ALU.mult)
                else:
                    t = nc.vector.scalar_tensor_tensor(as3(tq[:]), slot3(slot), g, as3(cs[:]), ALU.mult, ALU.mult)
                t.then_inc(s["t1d"], 1)
                dve.wait_ge(s["swa"], f + 3)
                own.link(nc.vector.tensor_tensor(swp[:], swp[:], sn[:], ALU.mult))
                dve.wait_ge(s["t1d"], f + 3)
                nc.vector.tensor_tensor(dst, tq[:], swp[:], ALU.add).then_inc(s["add"], 1)

            dve.wait_ge(tabI, 32)
            with dve.Fori(0, IH // 4) as i:
                own.enter(i, 2)
                for ff in range(2):
                    f = 2 * i + ff
                    rotate(iq, U_IQ + f, f, ff, iqT[:, bass.ds(f, 1), :].rearrange("p o n -> p (o n)"), csI, snI, None)
            own.leave(IH // 4)
            dve.wait_ge(kk_["swa"], 2)
            own.link(nc.vector.tensor_tensor(ikT[:], ikT[:], csI[:], ALU.mult))
            own.link(nc.vector.tensor_tensor(swp[:], swp[:], snI[:], ALU.mult))
            own.link(nc.vector.tensor_tensor(ikT[:], ikT[:], swp[:], ALU.add))
            dve.wait_ge(kk_["rt"], 3)
            own.link(nc.vector.reciprocal(rbc[:], rbc[:]))
            nc.vector.tensor_tensor(ikT[:], ikT[:], rbc[:], ALU.mult).then_inc(kk_["done"], 1)

            def tokens_out(n, dst, width, off=0):
                for m in range(3):
                    dve.wait_ge(tt_tr, 3 * n + m + 1)
                    if m < 2:
                        nc.vector.tensor_copy(dst[:, 1 + 4 * m:5 + 4 * m, off:off + width],
                                              PS[:, 6 + m, 0:4 * width].rearrange("p (j d) -> p j d", d=width)).then_inc(tt_ev, 1)
                    else:
                        nc.vector.tensor_copy(dst[0:NS, 0, off:off + width], PS[0:NS, 6, 0:width]).then_inc(tt_ev, 1)

            dve.wait_ge(xs_out, 16)
            tokens_out(0, ikout, ID)
            dve.wait_ge(iw_tr, 1)
            c = (ID ** -0.5) * (IH ** -0.5)
            nc.vector.tensor_scalar(iwt[:, 1:9, :], PS[:, 7, IH:9 * IH].rearrange("p (j h) -> p j h", h=IH), c, None, ALU.mult)
            own.link(nc.vector.tensor_scalar(iwt[0:NS, 0, :], PS[0:NS, 7, 0:IH], c, None, ALU.mult))
            dve.sem_inc(iw_ev, 1)
            dve.wait_ge(ss_["pre"], 1)
            for q in range(2):
                nc.vector.tensor_copy(
                    iqb[ID * q:ID * q + ID, :, 32 * q:32 * q + 32].rearrange("p b (r t) -> p r b t", t=DEC_T),
                    iqT[ID * q:ID * q + ID, :, 0:NS].rearrange("p r (b t) -> p r b t", t=DEC_T))
            idv = ident[0:NS, 0:NS].rearrange("p (b t) -> p b t", t=DEC_T).unsqueeze(2)
            for q in range(2):
                last = nc.vector.tensor_tensor(
                    sbT[:, :, 32 * q:32 * q + 32].rearrange("p b (r t) -> p b r t", t=DEC_T),
                    idv.broadcast_to((NS, DEC_B, IH // 2, DEC_T)),
                    iwt[0:NS, 0, q:IH:2].unsqueeze(1).unsqueeze(3).broadcast_to((NS, DEC_B, IH // 2, DEC_T)), ALU.mult)
            last.then_inc(ss_["pre"], 1)
            nc.vector.tensor_copy(repb[:].rearrange("p b (h t) -> p b h t", t=DEC_T),
                                  idv.broadcast_to((NS, DEC_B, NH, DEC_T))).then_inc(ss_["pre"], 1)

            for m, (b, c, h) in enumerate(SCORES):
                n = min(BANK, (b + 1) * P - c * BANK)
                x = sc[:, block_off(b) + c * BANK:block_off(b) + c * BANK + n]
                dve.wait_ge(sc_re, m + 1)
                if h == 0:
                    nc.vector.tensor_scalar(x, pring[m % 2][:, 0:n], iwt[:, 1 + b, h:h + 1], None,
                                            ALU.mult).then_inc(sc_ad, 1)
                else:
                    dve.wait_ge(sc_ad, m)
                    nc.vector.scalar_tensor_tensor(x, pring[m % 2][:, 0:n], iwt[:, 1 + b, h:h + 1], x,
                                                   ALU.mult, ALU.add).then_inc(sc_ad, 1)
            dve.wait_ge(ss_["sum"], DEC_B)
            nc.vector.tensor_copy(scs[:], PSF[0:NS, 0:SLS]).then_inc(ss_["cp"], 1)

            dve.wait_ge(tabQ, 32)
            for g in range(NKV):
                u = U_K + g
                dve.wait_ge(w_used, u + 1)
                own.link(nc.vector.scalar_tensor_tensor(as3(tq[:]), slot3(u % 2), gqk[:, 1:2], as3(csQ[:]),
                                                        ALU.mult, ALU.mult))
                dve.sem_inc(kk_["t1d"], 1)
                dve.wait_ge(kk_["swa"], 4 + 2 * g)
                own.link(nc.vector.tensor_tensor(swp[:], swp[:], snQ[:], ALU.mult))
                own.link(nc.vector.tensor_tensor(tq[:], tq[:], swp[:], ALU.add))
                dve.wait_ge(kk_["rt"], 6 + 3 * g)
                own.link(nc.vector.reciprocal(rbc[:], rbc[:]))
                own.link(nc.vector.tensor_tensor(kT[:, g, :], tq[:], rbc[:], ALU.mult))
                dve.sem_inc(kk_["done"], 1)
                tokens_out(1 + g, kout, DH, g * DH)
            for g in range(NKV):
                tokens_out(3 + g, vtok, DH, g * DH)

            dve.wait_ge(sc_ok, NBLK - 2)
            dve.wait_ge(ss_["ok"], 1)
            AREAS = [(P, sc[:, block_off(b):block_off(b + 1)], b - 2) for b in range(2, NBLK)] + [(NS, scs[:], 6)]

            def count(op, against):
                for rows, x, j in AREAS:
                    n = x.shape[1]
                    own.link(nc.vector.tensor_scalar(rbc[0:rows, 0:n], x,
                                                     0.0 if against is None else against[0:rows, j:j + 1], None,
                                                     op, ALU.add, accum_out=cnt[0:rows, j:j + 1]))

            own.link(nc.vector.memset(cnt[:], float(TOPK)))
            count(ALU.is_ge, None)
            own.link(nc.vector.tensor_scalar(sgn[:], cnt[:], TOPK - 0.5, None, ALU.is_ge))
            own.link(nc.vector.tensor_scalar(tbit[:], sgn[:], -1.0, 1.0, ALU.mult, ALU.add))
            own.link(nc.vector.tensor_scalar(tbit[:], tbit[:], 31, 31, ALU.logical_shift_left, ALU.arith_shift_right))
            own.link(nc.vector.tensor_scalar(tbit[:], tbit[:], 0x7FFFFFFF, None, ALU.bitwise_and))
            own.link(nc.vector.tensor_scalar(sgn[:], sgn[:], 2.0, -1.0, ALU.mult, ALU.add))
            own.link(nc.vector.memset(cnt[NS:P, 6:7], 0.0))
            own.link(nc.vector.memset(bitc[:], 1 << 30))

            def search_bit():
                own.link(nc.vector.tensor_tensor(cand[:], tbit[:], bitc[:], ALU.bitwise_xor))
                own.link(nc.vector.tensor_tensor(thr[:], cand[:].bitcast(F32), sgn[:], ALU.mult))
                count(ALU.is_ge, thr)
                own.link(nc.vector.scalar_tensor_tensor(mbit[:], cnt[:], TOPK - 0.5, bitc[:], ALU.is_ge, ALU.mult))
                own.link(nc.vector.tensor_tensor(tbit[:], tbit[:], mbit[:], ALU.bitwise_xor))
                own.link(nc.vector.tensor_scalar(bitc[:], bitc[:], 1, None, ALU.logical_shift_right))

            BIT_LINKS = 5 + 7

            dve.wait_ge(kk_["st"], 16 * 6)
            with dve.Fori(0, NH // 2) as i:
                own.enter(i, 2 + 2 * 2 * BIT_LINKS)
                for ff in range(2):
                    f = 2 * i + ff
                    rotate(qq, U_Q + f, f, (U_Q + ff) % 2, qT[:, bass.ds(f, 1), :].rearrange("p o n -> p (o n)"),
                           csQ, snQ, gqk[:, 0:1])
                    for _ in range(2):
                        search_bit()
            own.leave(NH // 2)
            for rows, j in ((NS, slice(0, 1)), (P, slice(1, 9))):
                dve.wait_ge(qq["rt"], 2)
                own.link(nc.vector.reciprocal(qs[0:rows, j, :], qs[0:rows, j, :]))
                own.link(nc.vector.tensor_scalar(qs[0:rows, j, :], qs[0:rows, j, :], DH ** -0.5, None, ALU.mult))
                own.link(nc.vector.tensor_scalar(nqs[0:rows, j, :], qs[0:rows, j, :], -1.0, None, ALU.mult))
            with dve.Fori(0, 8) as i:
                own.enter(i, 2 * BIT_LINKS)
                for _ in range(2):
                    search_bit()
            own.leave(8)

            dve.wait_ge(w_used, U_O)
            own.link(nc.vector.tensor_tensor(thr[:], tbit[:].bitcast(F32), sgn[:], ALU.mult))
            count(ALU.is_gt, thr)
            own.link(nc.vector.tensor_scalar(need[:], cnt[:], -1.0, float(TOPK), ALU.mult, ALU.add))
            for q in range(2):
                dve.wait_ge(z_st[q], 16 * (KD // 2))
            for rows, x, j in AREAS:
                n = x.shape[1]
                eq, cum, se = swp[0:rows, 0:n], tq[0:rows, 0:n], sqt[0:rows, 0:n]
                own.link(nc.vector.tensor_scalar(eq, x, thr[0:rows, j:j + 1], None, ALU.is_equal))
                own.link(nc.vector.tensor_tensor_scan(cum, eq, eq, 0.0, ALU.add, ALU.max))
                own.link(nc.vector.scalar_tensor_tensor(se, cum, need[0:rows, j:j + 1], eq, ALU.is_le, ALU.mult))
                own.link(nc.vector.scalar_tensor_tensor(cum, x, thr[0:rows, j:j + 1], se, ALU.is_gt, ALU.add))
                out = x if rows == P else scs[:].bitcast(BF16)[:, 0:SLS]
                own.link(nc.vector.tensor_scalar(out, cum, 1.0, BIG, ALU.subtract, ALU.mult))

            dve.wait_ge(cs_ok, 1)

            def mask_and_max(n):
                b, h = STEPS[n]
                w = (b + 1) * P
                off = caus[:, 2 * P - w:2 * P] if b < 2 else sc[:, block_off(b):block_off(b + 1)]
                dve.wait_ge(at_["s"], n + 1)
                if n >= 2:
                    dve.wait_ge(at_["tr"], FIRST[n - 1])
                nc.vector.tensor_tensor_reduce(
                    out=pring[n % 2][:, 0:w], in0=PSF[:, 2 * (n % 2) * BANK:2 * (n % 2) * BANK + w], in1=off,
                    scale=1.0, scalar=-3.0e38, op0=ALU.add, op1=ALU.max, accum_out=amx[:, n:n + 1]).then_inc(at_["mx"], 1)
                dve.wait_ge(at_["mx"], n + 1)
                nc.vector.tensor_tensor(anb[:, n:n + 1], amx[:, n:n + 1], nqs[:, 1 + b, h:h + 1], ALU.mult).then_inc(at_["nb"], 1)

            def normalise(n):
                b, h = STEPS[n]
                w = (b + 1) * P
                dve.wait_ge(at_["ex"], n + 1)
                own.link(nc.vector.reciprocal(ars[:, n:n + 1], asm[:, n:n + 1]))
                nc.vector.tensor_scalar(pring[n % 2][:, 0:w], pring[n % 2][:, 0:w], ars[:, n:n + 1], None,
                                        ALU.mult).then_inc(at_["nr"], 1)
                if h % REP == REP - 1 and n >= REP:
                    heads_out(n // REP - 1)

            def heads_out(i):
                b, g = i // NKV, i % NKV
                c0 = tile_cols(1 + b)[0]
                dve.wait_ge(at_["pv"], i + 1)
                nc.vector.tensor_copy(qT[:, REP * g:REP * g + REP, c0:c0 + P],
                                      PS[:, 6 + i % 2, :].rearrange("p (r q) -> p r q", q=P)).then_inc(at_["o"], 1)

            mask_and_max(0)
            for n in range(len(STEPS)):
                if n + 1 < len(STEPS):
                    mask_and_max(n + 1)
                normalise(n)
            heads_out(NBLK * NKV - 1)

            own.link(nc.vector.memset(qb[:], 0.0))
            for g in range(NKV):
                for q in range(REP):
                    nc.vector.tensor_copy(
                        qb[:, :, g, 32 * g + 8 * q:32 * g + 8 * q + 8],
                        qT[:, REP * g + q, 0:NS].rearrange("p (b t) -> p b t", t=DEC_T))
            idb = ident[0:NS, 0:NS].rearrange("p (b t) -> p b t", t=DEC_T)
            nc.vector.reduce_sum(bd8[:], idb, axis=AX.X)
            own.link(nc.vector.reduce_sum(d8[:], idb.rearrange("p b t -> p t b"), axis=AX.X))
            nc.vector.tensor_tensor(qa8[:], d8[:].unsqueeze(1).broadcast_to((NS, NH, DEC_T)),
                                    qs[0:NS, 0, :].unsqueeze(2).broadcast_to((NS, NH, DEC_T)), ALU.mult).then_inc(sa["pre"], 1)
            for b in range(DEC_B):
                dve.wait_ge(sa["s"], b + 1)
                own.link(nc.vector.reduce_max(smx[:, b:b + 1], PSF[0:NS, 0:SLS], axis=AX.X))
                dve.wait_ge(sa["qc"], 2)
                nc.vector.tensor_tensor(snb[:, b:b + 1], smx[:, b:b + 1], nqcol[:, b:b + 1], ALU.mult).then_inc(sa["nb"], 1)
                dve.wait_ge(sa["ex"], b + 1)
                own.link(nc.vector.reciprocal(srs[:, b:b + 1], ssm[:, b:b + 1]))
                nc.vector.tensor_scalar(Ps[:], Ps[:], srs[:, b:b + 1], None, ALU.mult).then_inc(sa["nr"], 1)
                dve.wait_ge(sa["pv"], b + 1)
                nc.vector.tensor_copy(qT[:, :, b * DEC_T:(b + 1) * DEC_T],
                                      PS[:, 3, 0:NS].rearrange("p (h t) -> p h t", t=DEC_T)).then_inc(sa["o"], 1)
            dve.wait_ge(sa["o"], DEC_B)
            for f in range(KD):
                dve.wait_ge(z_in[f % 2], 16 * (f // 2 + 1))
                nc.vector.tensor_tensor(qT[:, f, :], qT[:, f, :], zst[f % 2][:], ALU.mult).then_inc(oy["y"], 1)
                dve.wait_ge(oy["hi"], f + 1)
                nc.vector.tensor_tensor(hlo[:, f, :], qT[:, f, :], hhi[:, f, :].bitcast(F32), ALU.subtract).then_inc(oy["lo"], 1)
            dve.wait_ge(xs_in, 16)
            with dve.Fori(0, KD // 2) as i:
                for ff in range(2):
                    f = 2 * i + ff
                    dve.wait_ge(w_used, U_O + f + 1)
                    x = xT[:, bass.ds(f, 1), :].rearrange("p o (b n) -> p (o b) n", b=3)
                    nc.vector.tensor_tensor(x, slot3((U_O + ff) % 2), x, ALU.add).then_inc(oy["xup"], 1)
            gate_dve(1, True)

        @block.tensor
        def _(pe):
            pe.sem_inc(gmlp["vtr"], 2)
            pe.sem_inc(embed_sems["pe"], 1)
            pe.sem_inc(qq["st"], 1)
            pe.wait_ge(cst, 7)
            for j in range(9):
                c0, n = tile_cols(j)
                pe.wait_ge(x_in[j % 3], 16 * (j // 3 + 1))
                if j >= 3:
                    pe.wait_ge(x_ev, j - 2)
                    pe.wait_ge(x_eva, j - 2)
                for k in range(KD):
                    tr = nc.tensor.transpose(PS[:, 2 * (j % 3) + k // 4, (k % 4) * P:(k % 4) * P + n],
                                             xstage[0:n, j % 3, k * P:(k + 1) * P], ident[0:n, 0:n])
                tr.then_inc(x_tr, 1)
            pe.wait_ge(ws_in, 16)
            for q in range(NGRP):
                tr = nc.tensor.transpose(PS[:, 6 + q // 4, (q % 4) * P:(q % 4 + 1) * P], wsraw[:, q, :], ident[:])
                if q % 4 == 3:
                    tr.then_inc(ws_tr, 1)
            pe.wait_ge(x_ev, 9)
            pe.wait_ge(x_eva, 9)
            pe.wait_ge(x_dg, 9)
            pe.wait_ge(ws_ev, 2)

            for g in range(2):
                c0, n, nch, has_s = GROUPS[g]
                h = n // 2
                s = sA[g]
                halves = [(0, h), (h, h)]
                norm_pe(pe, nA[g], group_cols(g))
                po = NS if has_s else 0

                def v_unit(f, ff):
                    pe.wait_ge(w_lo, U_A[g] + f + 1)
                    pe.wait_ge(s["vev"], s.at("vev", f + 1))
                    gemm(pe, ff, [(PS[:, 2 * ff + m, 0:h], c) for m, c in enumerate(halves)],
                         lambda k, a, m: hhi_g[:, k, a:a + m], lambda k, a, m: hlo_g[:, k, a:a + m],
                         kwait=nA[g]).then_inc(w_used, 1)

                def v_transpose(f, ff):
                    pe.wait_ge(s["vev"], s.at("vev", f + 3))
                    pe.wait_ge(s["vst"], s.at("vst", f + 1))
                    for c in range(nch):
                        tr = nc.tensor.transpose(PS[:, 4 + 2 * ff, c * P:(c + 1) * P],
                                                 vtmp[ff][:, po + c * P:po + (c + 1) * P], ident[:])
                    if has_s:
                        tr = nc.tensor.transpose(PS[0:NS, 5 + 2 * ff, 0:P], vtmp[ff][:, 0:NS], ident[:])
                    tr.then_inc(s["vtr"], 1)

                v_unit(0, 0)
                with pe.Fori(0, KA // 2 - 1) as i:
                    v_unit(2 * i + 1, 1)
                    v_transpose(2 * i, 0)
                    v_unit(2 * i + 2, 0)
                    v_transpose(2 * i + 1, 1)
                v_unit(KA - 1, 1)
                v_transpose(KA - 2, 0)
                v_transpose(KA - 1, 1)

                with pe.Fori(0, KA // 2) as i:
                    for ff in range(2):
                        f = 2 * i + ff
                        for half in range(2):
                            pe.wait_ge(w_lo, U_A[g] + KA + 2 * f + half + 1)
                            free = "sz" if half == 0 else "ut"
                            pe.wait_ge(s[free], s.at(free, f + 1))
                            gemm(pe, half, [(PS[:, 2 * half + m, 0:h], c) for m, c in enumerate(halves)],
                                 lambda k, a, m: hhi_g[:, k, a:a + m],
                                 lambda k, a, m: hlo_g[:, k, a:a + m]).then_inc(w_used, 1)
                        pe.wait_ge(s["vs"], s.at("vs", f + 1))
                        pe.wait_ge(s["mt"], s.at("mt", f + 1))
                        for c in range(nch):
                            mm = nc.tensor.matmul(PS[:, 4, c * P:(c + 1) * P], vs[:, c * P:(c + 1) * P],
                                                  wsT[:, bass.ds(i, 1), :].rearrange("p o t -> p (o t)"),
                                                  start=True, stop=True)
                        if has_s:
                            mm = nc.tensor.matmul(PS[:, 5, 0:NS], vs[0:NS, 4 * P:5 * P],
                                                  wsbd[:, bass.ds(i, 1), :].rearrange("p o t -> p (o t)"),
                                                  start=True, stop=True)
                        mm.then_inc(s["mix"], 1)

                pe.wait_ge(s["ylo"], s.at("ylo", KA + 1))
                with pe.Fori(0, KD // 2) as i:
                    for ff in range(2):
                        pe.wait_ge(s["xup"], s.at("xup", 2 * i + ff + 1))
                        for half in range(2):
                            pe.wait_ge(w_lo, U_A[g] + 3 * KA + 4 * i + 2 * ff + half + 1)
                            gemm(pe, half, [(PS[:, 2 * ff + m, 0:h], c) for m, c in enumerate(halves)],
                                 lambda k, a, m: yhi[:, half * KD + k, a:a + m],
                                 lambda k, a, m: ylo[:, half * KD + k, a:a + m],
                                 first=half == 0, last=half == 1).then_inc(w_used, 1)

            def gate_pe(layer, last):
                s, base = sG[layer], U_GATE[layer]
                norm_pe(pe, nG[layer], ALL_COLS)
                pe.wait_ge(s["pin"], s.at("pin", 32))
                for kk in range(2):
                    for m in range(3):
                        for j in (range(1 + 4 * m, 5 + 4 * m) if m < 2 else (0,)):
                            rows = NS if j == 0 else P
                            q = (j - 1) % 4 if j else 0
                            tr = nc.tensor.transpose(PS[:, 3 * kk + m, q * P:q * P + rows],
                                                     pst[0:rows, j, kk * P:(kk + 1) * P], ident[0:rows, 0:rows])
                        tr.then_inc(s["ptr"], 1)
                pe.wait_ge(s["plo"], s.at("plo", 8))

                def gate_unit(f, ff):
                    pe.wait_ge(w_lo, base + f + 1)
                    pe.wait_ge(s["sig"], s.at("sig", f + 1))
                    par = (base + ff) % 2
                    gemm(pe, par, [(PS[:, m, 0:NC3], (m * NC3, NC3)) for m in range(3)],
                         lambda k, a, m: hhi[:, k, a:a + m], lambda k, a, m: hlo[:, k, a:a + m],
                         kwait=nG[layer]).then_inc(w_used, 1)

                def embed(f):
                    pe.wait_ge(s["wpl"], s.at("wpl", f + 1))
                    pe.wait_ge(s["t"], s.at("t", f + 1))
                    for k in range(2):
                        for n, (w, r) in enumerate(((pehi, pThi), (pehi, pTlo), (pelo, pThi))):
                            for m in range(3):
                                mm = nc.tensor.matmul(PS[:, 3 + m, 0:NC3], w[:, k, :],
                                                      r[:, k, m * NC3:(m + 1) * NC3],
                                                      start=k == 0 and n == 0, stop=k == 1 and n == 2)
                    mm.then_inc(s["pe"], 1)

                def transpose_out(f, ff):
                    pe.wait_ge(s["xup"], s.at("xup", f + 2))
                    for m in range(3):
                        pe.wait_ge(y_ev, 3 * f + 1 + m // 2)
                        for q in range(4 if m < 2 else 1):
                            c0, _ = tile_cols(1 + 4 * m + q if m < 2 else 0)
                            tr = nc.tensor.transpose(PS[:, 6 + m % 2, q * P:(q + 1) * P], xo[:, ff, c0:c0 + P],
                                                     ident[:])
                        tr.then_inc(y_tr, 1)

                if not last:
                    with pe.Fori(0, KD // 2) as i:
                        for ff in range(2):
                            gate_unit(2 * i + ff, ff)
                            embed(2 * i + ff)
                else:
                    gate_unit(0, 0)
                    embed(0)
                    with pe.Fori(0, KD // 2 - 1) as i:
                        for ff in range(2):
                            gate_unit(2 * i + 1 + ff, 1 - ff)
                            transpose_out(2 * i + ff, ff)
                            embed(2 * i + 1 + ff)
                    gate_unit(KD - 1, 1)
                    transpose_out(KD - 2, 0)
                    embed(KD - 1)
                    transpose_out(KD - 1, 1)

            pe.wait_ge(stat, 2)
            gate_pe(0, False)
            THREE = [(m * NC3, NC3) for m in range(3)]

            def full_unit(u, par, kwait=None):
                pe.wait_ge(w_lo, u + 1)
                gemm(pe, par, [(PS[:, 3 * par + m, 0:NC3], c) for m, c in enumerate(THREE)],
                     lambda k, a, m: hhi[:, k, a:a + m], lambda k, a, m: hlo[:, k, a:a + m],
                     kwait=kwait).then_inc(w_used, 1)

            pe.wait_ge(stat, 3)
            norm_pe(pe, nB, ALL_COLS)
            pe.wait_ge(sG[0]["t"], sG[0].at("t", KD + 1))
            with pe.Fori(0, IH // 4) as i:
                for ff in range(2):
                    f = 2 * i + ff
                    pe.wait_ge(iq["swa"], f + 1)
                    pe.wait_ge(iq["t1d"], f + 1)
                    full_unit(U_IQ + f, ff, nB)
            pe.wait_ge(iq["swa"], 5)
            pe.wait_ge(iq["t1d"], 5)
            full_unit(U_IK, 0)

            def head_sums(n, rows):
                pe.wait_ge(kk_["swa"], 2 * n + 1)
                if n:
                    pe.wait_ge(tt_ev, 3 * n)
                for c, (a, m) in enumerate(ALL_COLS):
                    if c == 2:
                        pe.wait_ge(kk_["rt"], 3 * n + 1)
                    nc.tensor.matmul(PS[:, 6 + c % 2, 0:m], ones[0:rows, :], sqt[0:rows, a:a + m],
                                     start=True, stop=True).then_inc(kk_["sum"], 1)

            def tokens(n, src, rows):
                for m in range(3):
                    if 3 * n + m >= 2:
                        pe.wait_ge(tt_ev, 3 * n + (1 if m == 2 else 0))
                    for q in range(4 if m < 2 else 1):
                        c0, cn = tile_cols(1 + 4 * m + q if m < 2 else 0)
                        tr = nc.tensor.transpose(PS[0:cn, 6 + m % 2, q * rows:(q + 1) * rows], src(c0, cn),
                                                 ident[0:rows, 0:rows])
                    tr.then_inc(tt_tr, 1)

            head_sums(0, ID)
            pe.wait_ge(kk_["done"], 1)
            pe.wait_ge(kk_["rt"], 3)
            tokens(0, lambda a, n: ikT[0:ID, a:a + n], ID)
            pe.wait_ge(tt_ev, 3)
            for j in range(9):
                c0, cn = tile_cols(j)
                tr = nc.tensor.transpose(PS[0:cn, 7, j * IH:(j + 1) * IH], iwT[:, c0:c0 + cn], ident[0:IH, 0:IH])
            tr.then_inc(iw_tr, 1)
            pe.wait_ge(iq["add"], 5)
            for m, (b, c, h) in enumerate(SCORES):
                n = min(BANK, (b + 1) * P - c * BANK)
                p0 = ID * (h % 2)
                c0 = tile_cols(1 + b)[0]
                if m >= 6:
                    pe.wait_ge(sc_re, m - 5)
                nc.tensor.matmul(PS[:, m % 6, 0:n], iqT[p0:p0 + ID, h // 2, c0:c0 + P],
                                 ikT[p0:p0 + ID, NS + c * BANK:NS + c * BANK + n], start=True,
                                 stop=True).then_inc(sc_mm, 1)
            pe.wait_ge(sc_re, len(SCORES))
            pe.wait_ge(ss_["pre"], 3)
            for b in range(DEC_B):
                tr = nc.tensor.transpose(PS[0:NS, 5, b * NS:(b + 1) * NS], sbT[:, b, :], ident[0:NS, 0:NS])
            tr.then_inc(ss_["wt"], 1)
            PARTS = ((0, BANK), (BANK, BANK), (2 * BANK, NS))

            def ik_pages(b):
                pe.wait_ge(ikp[b % 2], 16 * 2 * NPAGE * (b // 2 + 1))
                if b:
                    pe.wait_ge(ss_["ev"], b)
                else:
                    pe.wait_ge(iw_ev, 1)
                for g in range(NPAGE):
                    tr = nc.tensor.transpose(PS[:, 6 + g // 4, (g % 4) * P:(g % 4 + 1) * P],
                                             ikpg[b % 2][:, g].rearrange("p q d -> p (q d)"), ident[:])
                tr.then_inc(ss_["tr"], 1)

            def weigh(b):
                pe.wait_ge(ss_["re"], b + 1)
                for m, (a, n) in enumerate(PARTS):
                    mm = nc.tensor.matmul(PS[0:NS, m, 0:n], sbw[:, b, :], rels[:, a:a + n], start=b == 0,
                                          stop=b == DEC_B - 1)
                mm.then_inc(ss_["sum"], 1)

            ik_pages(0)
            pe.wait_ge(ss_["wt"], 2)
            for b in range(DEC_B):
                if b + 1 < DEC_B:
                    ik_pages(b + 1)
                if b:
                    weigh(b - 1)
                pe.wait_ge(ss_["ev"], b + 1)
                for m, (a, n) in enumerate(PARTS):
                    mm = nc.tensor.matmul(PS[0:NS, 3 + m, 0:n], iqb[:, b, :],
                                          ikTb[b % 2][:, a:a + n] if m < 2 else ikT[:, 0:NS], start=True, stop=True)
                mm.then_inc(ss_["mm"], 1)
            weigh(DEC_B - 1)
            pe.wait_ge(ss_["cp"], 1)

            for g in range(NKV):
                full_unit(U_K + g, (U_K + g) % 2)
                head_sums(1 + g, P)
                pe.wait_ge(kk_["done"], 2 + g)
                pe.wait_ge(kk_["rt"], 6 + 3 * g)
                tokens(1 + g, lambda a, n: kT[:, g, a:a + n], P)
            for g in range(NKV):
                full_unit(U_V + g, (U_V + g) % 2)
                pe.wait_ge(kk_["vev"], g + 1)
                tokens(3 + g, lambda a, n: sqt[:, a:a + n], P)
            pe.wait_ge(tt_ev, 15)

            def q_unit(f, ff):
                pe.wait_ge(qq["swa"], f + 1)
                pe.wait_ge(qq["t1d"], f + 1)
                full_unit(U_Q + f, (U_Q + ff) % 2)

            def q_sums(f):
                pe.wait_ge(qq["swa"], f + 3)
                for j in range(9):
                    c0, cn = tile_cols(j)
                    mm = nc.tensor.matmul(PS[0:cn, 7, bass.ds(f + NH * j, 1)], sqt[:, c0:c0 + cn], ones[:, 0:1],
                                          start=True, stop=True)
                mm.then_inc(qq["st"], 1)

            q_unit(0, 0)
            with pe.Fori(0, NH // 2 - 1) as i:
                q_unit(2 * i + 1, 1)
                q_sums(2 * i)
                q_unit(2 * i + 2, 0)
                q_sums(2 * i + 1)
            q_unit(NH - 1, 1)
            q_sums(NH - 2)
            q_sums(NH - 1)
            pe.wait_ge(qq["st"], NH + 1)
            pe.sem_inc(qq["end"], 1)
            pe.wait_ge(qq["swa"], NH + 2)
            pe.wait_ge(qq["t1d"], NH + 2)
            with pe.Fori(0, KD // 2) as i:
                for ff in range(2):
                    pe.wait_ge(z_ev, 2 * i + ff + 1)
                    full_unit(U_Z + 2 * i + ff, (U_Z + ff) % 2)

            def logits(n):
                b, h = STEPS[n]
                w, c0 = (b + 1) * P, tile_cols(1 + b)[0]
                if n >= 2:
                    pe.wait_ge(at_["mx"], n - 1)
                for a in range(0, w, BANK):
                    m = min(BANK, w - a)
                    mm = nc.tensor.matmul(PS[:, 2 * (n % 2) + a // BANK, 0:m], qT[:, h, c0:c0 + P],
                                          kT[:, h // REP, NS + a:NS + a + m], start=True, stop=True)
                mm.then_inc(at_["s"], 1)

            pe.wait_ge(z_ev, KD + 2)
            pe.wait_ge(qq["rt"], 2)
            pe.wait_ge(qq["add"], NH + 1)
            logits(0)
            for n, (b, h) in enumerate(STEPS):
                if n + 1 < len(STEPS):
                    logits(n + 1)
                pe.wait_ge(at_["nr"], n + 1)
                for i in range(FIRST[n], FIRST[n + 1]):
                    m = PIECES[i][3]
                    if i >= 2:
                        pe.wait_ge(at_["pt"], i - 1)
                    for k in range(4 * m, min(4 * m + 4, b + 1)):
                        tr = nc.tensor.transpose(PS[:, 4 + i % 2, (k - 4 * m) * P:(k - 4 * m + 1) * P],
                                                 pring[n % 2][:, k * P:(k + 1) * P], ident[:])
                    tr.then_inc(at_["tr"], 1)
                if h % REP == REP - 1:
                    i, g = n // REP, h // REP
                    pe.wait_ge(at_["pt"], FIRST[n + 1])
                    if i >= 2:
                        pe.wait_ge(at_["o"], i - 1)
                    for k in range(b + 1):
                        mm = nc.tensor.matmul(PS[:, 6 + i % 2, :], vtok[:, 1 + k, g * DH:(g + 1) * DH],
                                              PTs[:, k].rearrange("p r q -> p (r q)"), start=k == 0, stop=k == b)
                    mm.then_inc(at_["pv"], 1)

            pe.wait_ge(at_["o"], NBLK * NKV)
            pe.wait_ge(sa["pre"], 1)
            nc.tensor.matmul(PS[0:NS, 3, 0:DEC_B], qa8[:].rearrange("p h t -> p (h t)"), bd8[:], start=True,
                             stop=True).then_inc(sa["qc"], 1)

            def k_pages(b):
                pe.wait_ge(kvp[b % 2], 16 * 2 * NPAGE * (b // 2 + 1))
                if b:
                    pe.wait_ge(sa["ke"], b)
                for g in range(NKV):
                    for j in range(NPAGE):
                        tr = nc.tensor.transpose(PS[:, 4 + 2 * g + j // 4, (j % 4) * P:(j % 4 + 1) * P],
                                                 kpg[b % 2][:, j, g * DH:(g + 1) * DH], ident[:])
                tr.then_inc(sa["kt"], 1)

            k_pages(0)
            pe.wait_ge(sa["qc"], 2)
            for b in range(DEC_B):
                pe.wait_ge(sa["ke"], b + 1)
                if b:
                    pe.wait_ge(sa["ex"], b)
                    pe.wait_ge(sa["pt"], b)
                for m, (a, n) in enumerate(PARTS):
                    for g in range(NKV):
                        nc.tensor.matmul(PS[0:NS, m, 0:n], qb[:, b, g, :],
                                         kTb[:, g, a:a + n] if m < 2 else kT[:, g, 0:NS], start=g == 0, stop=False)
                    mm = nc.tensor.matmul(PS[0:NS, m, 0:n], repb[:, b, :], scs[:].bitcast(BF16)[:, a:a + n],
                                          start=False, stop=True)
                mm.then_inc(sa["s"], 1)
                if b + 1 < DEC_B:
                    k_pages(b + 1)
                pe.wait_ge(sa["nr"], b + 1)
                if b:
                    pe.wait_ge(sa["o"], b)
                for j in range(NPAGE):
                    nc.tensor.transpose(PS[:, 3, j * NS:(j + 1) * NS], Ps[:, j * P:(j + 1) * P], ident[0:NS, 0:NS])
                nc.tensor.transpose(PS[0:NS, 2, 2 * NS:3 * NS], Ps[:, PAST:SLS], ident[0:NS, 0:NS]).then_inc(sa["tr"], 1)
                pe.wait_ge(sa["pt"], b + 1)
                for g in range(NKV):
                    for j in range(NPAGE):
                        nc.tensor.matmul(PS[:, 3, 32 * g:32 * g + 32], vpg[b % 2][:, j, g * DH:(g + 1) * DH],
                                         PsT[:, j, 32 * g:32 * g + 32], start=j == 0, stop=False)
                    mm = nc.tensor.matmul(PS[:, 3, 32 * g:32 * g + 32], vtok[0:NS, 0, g * DH:(g + 1) * DH],
                                          PsT[0:NS, 8, 32 * g:32 * g + 32], start=False, stop=True)
                mm.then_inc(sa["pv"], 1)

            pe.wait_ge(sa["o"], DEC_B)
            with pe.Fori(0, KD // 2) as i:
                for ff in range(2):
                    pe.wait_ge(oy["xup"], 2 * i + ff + 1)
                    full_unit(U_O + 2 * i + ff, (U_O + ff) % 2, oy_turn)
            pe.wait_ge(stat, 4)
            gate_pe(1, True)


_INS = ['x_prompt', 'x_sample', 'cache_k', 'cache_v', 'cache_ik', 'page_table', 'p_prompt', 'p_sample', 'g_norm',
        'w_in_a', 'w_s_a', 'b_s_a', 'g_v_a', 'w_out_a', 'w_in_b', 'g_q_b', 'g_k_b', 'g_ik_b', 'w_out_b', 'g_pe',
        'w_pe_gate', 'w_pe_proj']
_OUTS = [(1, SEQ, D), (DEC_B, DEC_T, D), (1, 1, SEQ, NKV, DH), (1, 1, SEQ, NKV, DH), (1, 1, SEQ, ID),
         (DEC_B, 1, DEC_T, NKV, DH), (DEC_B, 1, DEC_T, NKV, DH), (DEC_B, 1, DEC_T, ID), (DEC_B, 1, DEC_T, AW)]


def kernel(**inputs):
    import concourse.bacc as bacc
    from concourse.bass_utils import run_bass_kernel_spmd as run

    nc = bacc.Bacc("TRN2", target_bir_lowering=False, num_devices=1)
    arrays, args = {}, []
    for name in _INS:
        a = np.ascontiguousarray(inputs[name])
        arrays[f"in_{name}_dram"] = a
        args.append(nc.dram_tensor(f"in_{name}_dram", a.shape, mybir.dt.from_np(a.dtype), kind="ExternalInput").ap())
    for i, shape in enumerate(_OUTS):
        args.append(nc.dram_tensor(f"out_{i}_dram", shape, F32, kind="ExternalOutput").ap())
    hybrid_trunk(nc, *args)
    r = run(nc, [arrays], core_ids=[0])
    return tuple(r.results[0][f"out_{i}_dram"] for i in range(len(_OUTS)))
```

```python
from contextlib import ExitStack

import numpy as np

import concourse.bass as bass
from concourse import mybir

F32 = mybir.dt.float32
F32R = mybir.dt.float32r
BF16 = mybir.dt.bfloat16
I32 = mybir.dt.int32
U32 = mybir.dt.uint32
ALU = mybir.AluOpType
ACT = mybir.ActivationFunctionType
AX = mybir.AxisListType

P = 128
D = 1024
KD = D // P
SEQ, DEC_B, DEC_T = 1024, 8, 8
NS = DEC_B * DEC_T
NT = NS + SEQ
TP = NT + 4
NC3 = TP // 3
CHUNK = 128
NBLK = SEQ // CHUNK
AW = 2 * D
KA = AW // P
NGRP = 8
PD = 256
EPS = 1e-6
THETA = 10000.0
PAGE, NPAGE = 128, 8
PAST = PAGE * NPAGE
NH, DH, NKV, REP = 8, 128, 2, 4
IH, ID = 8, 64
TOPK = 256
SLS = PAST + NS
QOFF, KOFF, VOFF, IQOFF, IKOFF, ZOFF = 0, 1024, 1280, 1536, 2048, 2120
MASKED = -2.0e38
BIG = 1.0e30
BANK = 512

GROUPS = [(0, 576, 4, True), (576, 516, 4, False)]
GW = 576
U_A = [0, 64]
U_GATE = [128, 169]
U_IQ, U_IK, U_K, U_V, U_Q, U_Z, U_O = 136, 140, 141, 143, 145, 153, 161
N_UNITS = 177


def tile_cols(j):
    return (0, NS) if j == 0 else (NS + CHUNK * (j - 1), CHUNK)


def block_off(b):
    return P * sum(c + 1 for c in range(2, b))


def rope_tables(half, heads):
    pos = np.concatenate([np.tile(PAST + np.arange(DEC_T), DEC_B), np.arange(SEQ), np.zeros(TP - NT)])
    e = (-np.arange(half, dtype=np.float32) / np.float32(half)).astype(np.float64)
    inv = (THETA ** e).astype(np.float32)
    ang = (inv[:, None] * pos.astype(np.float32)[None, :]).astype(np.float32).astype(np.float64)
    c, s = np.cos(ang).astype(np.float32), np.sin(ang).astype(np.float32)
    return (np.concatenate([c, c] * heads, 0), np.concatenate([-s, s] * heads, 0))


class Turn:

    def __init__(self, sems, before):
        self.sems, self.before = sems, before

    def __getitem__(self, name):
        return self.sems[name]

    def at(self, name, value):
        return self.before[name] + value


class Tally:

    def __init__(self, eng, sem):
        self.eng, self.sem, self.n, self.i, self.per = eng, sem, 0, 0, 0

    def link(self, instruction):
        instruction.then_inc(self.sem, 1)
        self.n += 1
        self.eng.wait_ge(self.sem, self.i * self.per + self.n)

    def enter(self, i, per):
        self.i, self.per, self.at = i, per, self.n

    def leave(self, trips):
        assert self.n - self.at == self.per, (self.n - self.at, self.per)
        self.n = self.at + self.per * trips
        self.i = self.per = 0


def hybrid_trunk(nc, x_prompt, x_sample, cache_k, cache_v, cache_ik, page_table, p_prompt, p_sample,
                 g_norm, w_in_a, w_s_a, b_s_a, g_v_a, w_out_a, w_in_b, g_q_b, g_k_b, g_ik_b, w_out_b,
                 g_pe, w_pe_gate, w_pe_proj,
                 y_prompt, y_sample, k_prompt, v_prompt, ik_prompt, k_sample, v_sample, ik_sample,
                 chunk_v_sample):
    ctx = ExitStack()
    with ctx:
        def sem(name):
            return ctx.enter_context(nc.semaphore(name))

        at = [(nc.sbuf_base + 63) // 64 * 64]

        def fixed(name, shape, dt=F32):
            size = int(np.prod(shape[1:])) * mybir.dt.size(dt)
            t = nc.alloc_sbuf_tensor_at(name, shape, dt, offset=at[0])
            at[0] += (size + 31) // 32 * 32
            return t

        def region(start, limit):
            pos = [start]

            def place(name, shape, dt=F32):
                size = int(np.prod(shape[1:])) * mybir.dt.size(dt)
                t = nc.alloc_sbuf_tensor_at(name, shape, dt, offset=pos[0])
                pos[0] += (size + 31) // 32 * 32
                assert pos[0] <= limit, (name, pos[0], limit)
                return t
            return place

        ident = fixed("ident", [P, P])
        ones = fixed("ones", [P, P])
        gn = fixed("gn", [P, 2, KD])
        gp = fixed("gp", [P, 2, KD])
        gv = fixed("gv", [P, KA])
        gqk = fixed("gqk", [P, 3])
        eps = fixed("eps", [P, 1])
        ss = fixed("ss", [P, 9])
        sv = fixed("sv", [P, 5])
        rv = fixed("rv", [P, 5])
        wraw = [fixed(f"wraw{s}", [P, KD, P]) for s in range(2)]
        whi = [fixed(f"whi{s}", [P, KD, P], F32R) for s in range(2)]
        wlo = [fixed(f"wlo{s}", [P, KD, P], F32R) for s in range(2)]
        acc = fixed("acc", [P, TP])
        rbc = fixed("rbc", [P, TP])
        fixed_ptab = nc.alloc_sbuf_tensor_at("ptab", [1, DEC_B * NPAGE], I32, offset=at[0])
        at[0] += 256
        X0 = at[0]
        xT = fixed("xT", [P, KD, TP])
        D0, END = at[0], nc.sbuf_usable_end

        pl = region(D0, END)
        hhi_g = pl("hhi_g", [P, KD, GW], F32R)
        hlo_g = pl("hlo_g", [P, KD, GW], F32R)
        V0 = D0 + 2 * KD * GW * 4
        v_raw = pl("v_raw", [P, KA, 5 * P])
        Y0 = V0 + KA * 5 * P * 4
        ylo = pl("ylo", [P, KA, GW], F32R)
        wsT = pl("wsT", [P, NGRP, P])
        wsbd = pl("wsbd", [NS, NGRP, NS])
        bsb = pl("bsb", [P, NGRP, P])
        szt = pl("szt", [P, GW])
        t1a = pl("t1a", [P, GW])
        t2a = pl("t2a", [P, GW])
        vs = pl("vs", [P, 5 * P])
        hfa = pl("hfa", [P, 2, GW])
        sqa = vs
        yhi = nc.alloc_sbuf_tensor_at("yhi", [P, KA, 5 * P], F32R, offset=V0)
        vtmp = [szt, t1a]
        pl = region(Y0, Y0 + KA * GW * 4)
        xstage = pl("xstage", [P, 3, D])
        sqdump = pl("sqdump", [P, D], BF16)
        vdump = nc.alloc_sbuf_tensor_at("vdump", [P, KA, P], F32, offset=Y0)
        wsraw = pl("wsraw", [P, NGRP, P])
        gvb = pl("gvb", [NS, AW])
        v_out = pl("v_out", [NS, AW])

        pl = region(D0, END)
        hhi = pl("hhi", [P, KD, TP], F32R)
        hlo = pl("hlo", [P, KD, TP], F32R)
        H1 = D0 + 2 * KD * TP * 4
        pl = region(H1, END)
        pst = pl("pst", [P, 9, PD])
        xo = nc.alloc_sbuf_tensor_at("xo", [P, 2, TP], F32, offset=H1)
        pThi = pl("pThi", [P, 2, TP], F32R)
        pTlo = pl("pTlo", [P, 2, TP], F32R)
        peraw = pl("peraw", [P, 2, D])
        pehi = pl("pehi", [P, 2, P], F32R)
        pelo = pl("pelo", [P, 2, P], F32R)
        sig = pl("sig", [P, TP])
        tpe = pl("tpe", [P, TP])
        hfb = pl("hfb", [P, 2, TP])
        sqb = hfb[:, 0, :]
        ystage = pl("ystage", [P, 2, 9, P])

        pl = region(H1, END)
        qT = pl("qT", [P, NH, TP])
        sc = pl("sc", [P, block_off(NBLK)])
        scs = pl("scs", [NS, SLS])
        swp = pl("swp", [P, TP])
        tq = pl("tq", [P, TP])
        sqt = pl("sqt", [P, TP])
        caus = pl("caus", [P, 2 * P])
        iwt = pl("iwt", [P, 9, IH])
        qs = pl("qs", [P, 9, NH])
        nqs = pl("nqs", [P, 9, NH])
        repb = pl("repb", [NS, DEC_B, NS], BF16)
        tbit, cand, mbit = (pl(n, [P, 7], U32) for n in ("tbit", "cand", "mbit"))
        bitc = pl("bitc", [P, 7], U32)
        sgn, thr, cnt, need = (pl(n, [P, 7]) for n in ("sgn", "thr", "cnt", "need"))
        pl = region(H1, H1 + NH * TP * 4)
        iqT = pl("iqT", [P, IH // 2, TP])
        csI, snI = pl("csI", [P, TP]), pl("snI", [P, TP])
        ikT = pl("ikT", [P, TP])
        iwT = nc.alloc_sbuf_tensor_at("iwT", [IH, TP], F32, offset=H1 + NH * TP * 4)
        pl = region(X0, X0 + KD * TP * 4)
        ikpg = [pl(f"ikpg{q}", [P, NPAGE, 2, ID]) for q in range(3)]
        ikTb = [pl(f"ikTb{q}", [P, PAST]) for q in range(2)]
        rels = pl("rels", [NS, SLS])
        sbT = pl("sbT", [NS, DEC_B, NS])
        sbw = pl("sbw", [NS, DEC_B, NS])
        iqb = pl("iqb", [P, DEC_B, NS])
        ikout = pl("ikout", [P, 9, ID])
        pl = region(X0, X0 + KD * TP * 4)
        kT = pl("kT", [P, NKV, TP])
        vtok = pl("vtok", [P, 9, NKV * DH])
        csQ, snQ = pl("csQ", [P, TP]), pl("snQ", [P, TP])
        qb = pl("qb", [P, DEC_B, NKV, NS])
        kout = nc.alloc_sbuf_tensor_at("kout", [P, 9, NKV * DH], F32, offset=H1 + (IH // 2) * TP * 4)
        pl = region(D0, H1)
        PTs = pl("PTs", [P, NBLK, REP, P])
        kpg = [pl(f"kpg{q}", [P, NPAGE, NKV * DH]) for q in range(2)]
        vpg = [pl(f"vpg{q}", [P, NPAGE, NKV * DH]) for q in range(2)]
        kTb = pl("kTb", [P, NKV, PAST])
        Ps = pl("Ps", [NS, SLS])
        PsT = pl("PsT", [P, 9, NS])
        amx, anb, asm, ars = (pl(n, [P, NBLK * NH]) for n in ("amx", "anb", "asm", "ars"))
        smx, snb, ssm, srs, qcol, nqcol = (pl(n, [NS, DEC_B]) for n in ("smx", "snb", "ssm", "srs", "qcol", "nqcol"))
        d8 = pl("d8", [NS, DEC_T])
        bd8 = pl("bd8", [NS, DEC_B])
        qa8 = pl("qa8", [NS, NH, DEC_T])
        pring = [swp, tq, sqt, rbc]
        NR = len(pring)
        zst = [swp, tq]
        ROW = (TP * 4 + 31) // 32 * 32
        zb = [nc.alloc_sbuf_tensor_at(f"zb{f}", [P, TP], F32,
                                      offset=(D0 if f < 3 else H1 + NH * TP * 4) + f % 3 * ROW)
              for f in range(6)] + [swp, tq]
        ptab = fixed_ptab

        PS = ctx.enter_context(nc.psum_tensor("PS", [P, 8, BANK], F32))
        PSF = PS[:].rearrange("p b n -> p (b n)")

        def slot3(s):
            return PS[:, 3 * s:3 * s + 3, 0:NC3]

        def as3(ap):
            return ap.rearrange("p (b n) -> p b n", b=3)

        w_raw = [sem("w_raw0"), sem("w_raw1")]
        w_hi, w_lo = sem("w_hi"), sem("w_lo")
        w_used = sem("w_used")
        cst, cst_dma = sem("cst"), sem("cst_dma")
        dv, av, gv_ = sem("dv"), sem("av"), sem("gp_own")
        x_in = [sem(f"x_in{s}") for s in range(3)]
        x_tr, x_sq, x_ev, x_eva, x_dg = (sem(n) for n in ("x_tr", "x_sq", "x_ev", "x_eva", "x_dg"))
        ws_in, ws_tr, ws_ev, bd_in, gvb_in = (sem(n) for n in
                                                     ("ws_in", "ws_tr", "ws_ev", "bd_in", "gvb_in"))

        norm = {n: sem(f"norm_{n}") for n in ("sum", "rt", "hf", "hi", "lo")}
        turns = [Turn(norm, {n: (0, 2, 4, 7, 10)[t] if n in ("sum", "rt") else KD * t for n in norm})
                 for t in range(5)]
        nA, nG, nB = turns[0:2], [turns[2], turns[4]], turns[3]
        gmlp = {n: sem(f"A_{n}") for n in ("vev", "vtr", "vst", "vsq", "rv", "vs", "mix", "mt", "sz", "ut",
                                           "y", "yhi", "ylo", "xup")}
        sA = [Turn(gmlp, {n: g * {"vsq": 5, "rv": 1, "xup": KD}.get(n, KA) for n in gmlp}) for g in range(2)]
        vo_ok, vo_st = sem("vo_ok"), sem("vo_st")
        embed_sems = {n: sem(f"G_{n}") for n in ("pin", "pein", "ptr", "phi", "plo", "wph", "wpl", "pe", "sig",
                                                 "t", "xup")}
        sG = [Turn(embed_sems, {n: l * {"pin": 32, "pein": 16, "ptr": 6, "phi": 6, "plo": 8}.get(n, KD)
                                for n in embed_sems}) for l in range(2)]
        stat = sem("stat")
        xs_out, xs_in, tabI, tabQ, pt_in = (sem(n) for n in ("xs_out", "xs_in", "tabI", "tabQ", "pt_in"))
        BITS, EARLY_BITS, KV_BITS = 31, 8, 2 * NKV
        SIDE = 25
        iq = {n: sem(f"iq_{n}") for n in ("swa", "t1d", "add")}
        qq = {n: sem(f"qq_{n}") for n in ("swa", "t1d", "add", "st", "end", "rt")}
        kk_ = {n: sem(f"k_{n}") for n in ("swa", "t1d", "sum", "rt", "done", "vev", "st")}
        tt_tr, tt_ev = sem("tt_tr"), sem("tt_ev")
        iw_tr, iw_ev = sem("iw_tr"), sem("iw_ev")
        sc_mm, sc_re, sc_ad, sc_ok = sem("sc_mm"), sem("sc_re"), sem("sc_ad"), sem("sc_ok")
        ikp = [sem(f"ikp{q}") for q in range(3)]
        ss_ = {n: sem(f"ss_{n}") for n in ("pre", "tr", "ev", "mm", "re", "sum", "wt", "cp", "ok")}
        cs_ok = sem("cs_ok")
        z_ev, z_in = sem("z_ev"), [sem(f"z_in{f}") for f in range(KD)]
        z_st = [sem("z_st0"), sem("z_st1")]
        at_ = {n: sem(f"at_{n}") for n in ("s", "mx", "nb", "ex", "nr", "tr", "pt", "pv", "o")}
        sa = {n: sem(f"sa_{n}") for n in ("pre", "qc", "kt", "ke", "s", "mx", "nb", "ex", "nr", "tr", "pt", "pv", "o")}
        kpin, vpin = ([sem(f"{n}{q}") for q in range(2)] for n in ("kpin", "vpin"))
        oy = {n: sem(f"oy_{n}") for n in ("y", "hi", "lo", "xup")}
        xs = nc.dram_tensor("xs", [P, KD * TP], F32).ap()
        zs = nc.dram_tensor("zs", [KD, P, TP], F32).ap()
        tab = {n: nc.inline_tensor(a, name=n).ap() for n, a in
               zip(("tcI", "tsI", "tcQ", "tsQ"), rope_tables(ID // 2, 2) + rope_tables(DH // 2, 1))}
        STEPS = [(b, h) for b in range(NBLK) for h in range(NH)]
        PIECES = [(n, b, h, m) for n, (b, h) in enumerate(STEPS) for m in range((b + 4) // 4)]
        FIRST = [next(i for i, x in enumerate(PIECES) if x[0] == n) for n in range(len(STEPS))] + [len(PIECES)]
        SCORES = [(b, c, h) for b in range(2, NBLK) for c in range((b + 4) // 4) for h in range(IH)]

        y_tr, y_ev = sem("y_tr"), sem("y_ev")
        y_st = [sem("y_st0"), sem("y_st1")]

        block = ctx.enter_context(nc.Block())

        def split_hi(act, par, n, u):
            act.wait_ge(w_raw[par], 16 * n)
            if not (isinstance(u, int) and u < 2):
                act.wait_ge(w_used, u - 1)
            nc.scalar.activation(whi[par][:], wraw[par][:], ACT.Copy).then_inc(w_hi, 1)

        def split_lo(pool, par, u):
            pool.wait_ge(w_hi, u + 1)
            nc.gpsimd.tensor_tensor(wlo[par][:], wraw[par][:], whi[par][:].bitcast(F32),
                                    ALU.subtract).then_inc(w_lo, 1)

        def gemm(pe, par, out, rhs_hi, rhs_lo, first=True, last=True, kwait=None, first_k=1):
            for k in range(KD):
                if kwait is not None:
                    pe.wait_ge(kwait, first_k + k)
                for n, (w, r) in enumerate(((whi, rhs_hi), (whi, rhs_lo), (wlo, rhs_hi))):
                    for o, (c0, cn) in out:
                        mm = nc.tensor.matmul(o, w[par][:, k, :], r(k, c0, cn),
                                              start=first and k == 0 and n == 0,
                                              stop=last and k == KD - 1 and n == 2)
            return mm

        def norm_pe(pe, s, cols):
            for c, (a, n) in enumerate(cols):
                if c >= 2:
                    pe.wait_ge(s["rt"], s.at("rt", c - 1))
                nc.tensor.matmul(PS[:, 6 + c % 2, 0:n], ones[:], acc[:, a:a + n],
                                 start=True, stop=True).then_inc(s["sum"], 1)

        def norm_roots(act, s, cols):
            for c, (a, n) in enumerate(cols):
                act.wait_ge(s["sum"], s.at("sum", c + 1))
                nc.scalar.activation(rbc[:, a:a + n], PS[:, 6 + c % 2, 0:n], ACT.Sqrt,
                                     bias=eps[:], scale=1.0 / D).then_inc(s["rt"], 1)

        def norm_hi(act, s, k, hi, hf):
            act.wait_ge(s["hf"], s.at("hf", k + 1))
            nc.scalar.activation(hi(k), hf(k), ACT.Copy).then_inc(s["hi"], 1)

        def norm_act(act, s, cols, hi):
            norm_roots(act, s, cols)
            for k in range(KD):
                norm_hi(act, s, k, *hi)

        def norm_inverse(dve, own, s, cols):
            for c, (a, n) in enumerate(cols):
                dve.wait_ge(s["rt"], s.at("rt", c + 1))
                own.link(nc.vector.reciprocal(rbc[:, a:a + n], rbc[:, a:a + n]))

        def norm_tile(dve, s, k, a, n, g, hf, hi, lo):
            if k < KD:
                if k >= 2:
                    dve.wait_ge(s["lo"], s.at("lo", k - 1))
                nc.vector.scalar_tensor_tensor(hf(k), xT[:, k, a:a + n], g(k), rbc[:, a:a + n],
                                               ALU.mult, ALU.mult).then_inc(s["hf"], 1)
            if k >= 1:
                dve.wait_ge(s["hi"], s.at("hi", k))
                dve.wait_ge(s["hf"], s.at("hf", k))
                nc.vector.tensor_tensor(lo(k - 1), hf(k - 1), hi(k - 1).bitcast(F32),
                                        ALU.subtract).then_inc(s["lo"], 1)

        def norm_dve(dve, own, s, cols, *tile):
            a, n = cols[0][0], sum(c[1] for c in cols)
            norm_inverse(dve, own, s, cols)
            for k in range(KD + 1):
                norm_tile(dve, s, k, a, n, *tile)

        def group_cols(g):
            c0, n, _, _ = GROUPS[g]
            return [(c0, n // 2), (c0 + n // 2, n // 2)]

        ALL_COLS = [(NC3 * c, NC3) for c in range(3)]

        PIECES_P = [(kk, m, ((3, 4, 5), (6, 7, 5))[kk][m], NS * kk if m == 2 else 0, *(((NS, 512), (NS + 512, 512), (0, NS))[m]))
                    for kk in range(2) for m in range(3)]

        @block.sync
        def _(sp):
            def unit(par, u, src):
                if not (isinstance(u, int) and u < 2):
                    sp.wait_ge(w_lo, u - 1)
                sp.dma_start(wraw[par][:], src.rearrange("(k p) c -> p k c", p=P)).then_inc(w_raw[par], 16)

            def slab(w, row, col):
                return w[row:row + D, bass.ds(col, P)]

            def pair(w, col, i, ff):
                return w[:, bass.ds(col + 2 * P * i, 2 * P)][:, ff * P:(ff + 1) * P]

            for j in range(9):
                c0, n = tile_cols(j)
                if j >= 3:
                    sp.wait_ge(x_tr, j - 2)
                    sp.wait_ge(x_sq, j - 2)
                src = (x_sample.rearrange("b t d -> (b t) d") if j == 0
                       else x_prompt[0, CHUNK * (j - 1):CHUNK * j, :])
                sp.dma_start(xstage[0:n, j % 3, :], src).then_inc(x_in[j % 3], 16)
                if j == 2:
                    unit(0, 0, slab(w_in_a[0], 0, AW))
                    unit(1, 1, slab(w_in_a[0], 0, AW + P))
            for g in range(2):
                with sp.Fori(1 if g == 0 else 0, KA // 2) as i:
                    for ff in range(2):
                        unit(ff, U_A[g] + 2 * i + ff, pair(w_in_a[0], AW, i, ff))
                with sp.Fori(0, KA) as i:
                    unit(0, U_A[g] + KA + 2 * i, slab(w_in_a[0], 0, 2 * AW + i * P))
                    unit(1, U_A[g] + KA + 2 * i + 1, slab(w_in_a[0], 0, (2 * i) * (P // 2)))
                with sp.Fori(0, KD) as i:
                    for half in range(2):
                        unit(half, U_A[g] + 3 * KA + 2 * i + half, slab(w_out_a[0], half * D, i * P))

            def gate_loads(layer):
                base, s = U_GATE[layer], sG[layer]
                for ff in range(2):
                    unit((base + ff) % 2, base + ff, slab(w_pe_gate[layer], 0, ff * P))
                sp.wait_ge(nG[layer]["sum"], nG[layer].at("sum", 3))
                sp.dma_start(pst[0:NS, 0, :], p_sample[layer].rearrange("b t d -> (b t) d")).then_inc(s["pin"], 16)
                sp.dma_start(pst[:, 1:9, :], p_prompt[layer, 0].rearrange("(j p) d -> p j d", p=P)).then_inc(s["pin"], 16)
                sp.dma_start(peraw[:], w_pe_proj[layer].rearrange("(k p) c -> p k c", p=P)).then_inc(s["pein"], 16)
                with sp.Fori(1, KD // 2) as i:
                    for ff in range(2):
                        unit((base + ff) % 2, base + 2 * i + ff, pair(w_pe_gate[layer], 0, i, ff))

            gate_loads(0)
            for ff in range(2):
                unit(ff, U_IQ + ff, slab(w_in_b[0], 0, IQOFF + ff * P))
            sp.dma_start(ptab[:], page_table.rearrange("b n -> (b n)").unsqueeze(0)).then_inc(pt_in, 16)
            sp.wait_ge(nB["sum"], nB.at("sum", 3))
            sp.dma_start(csI[:], tab["tcI"]).then_inc(tabI, 16)
            sp.dma_start(snI[:], tab["tsI"]).then_inc(tabI, 16)
            for ff in range(2):
                unit(ff, U_IQ + 2 + ff, slab(w_in_b[0], 0, IQOFF + (2 + ff) * P))
            sp.wait_ge(nB["hf"], nB.at("hf", KD))
            sp.dma_start(xs, xT[:].rearrange("p f n -> p (f n)")).then_inc(xs_out, 16)
            unit(0, U_IK, slab(w_in_b[0], 0, IKOFF))
            unit(1, U_K, slab(w_in_b[0], 0, KOFF))
            sp.wait_ge(xs_out, 16)
            sp.wait_ge(pt_in, 16)
            for b in range(DEC_B):
                if b >= 3:
                    sp.wait_ge(ss_["tr"], b - 2)
                for g in range(NPAGE):
                    page = sp.value_load(ptab[0:1, b * NPAGE + g:b * NPAGE + g + 1],
                                         min_val=0, max_val=cache_ik.shape[0] - 1)
                    sp.dma_start(ikpg[b % 3][:, g],
                                 cache_ik[bass.ds(page, 1), 0].rearrange("a s d -> s a d")
                                 .broadcast_to((P, 2, ID))).then_inc(ikp[b % 3], 16)
            sp.wait_ge(ss_["cp"], 1)
            sp.dma_start(ik_prompt[0, 0].rearrange("(j p) d -> p j d", p=P), ikout[:, 1:9, :]).then_inc(kk_["st"], 16)
            sp.dma_start(ik_sample.rearrange("b l t d -> (b l t) d"), ikout[0:NS, 0, :]).then_inc(kk_["st"], 16)
            sp.dma_start(csQ[:], tab["tcQ"]).then_inc(tabQ, 16)
            sp.dma_start(snQ[:], tab["tsQ"]).then_inc(tabQ, 16)
            unit(0, U_K + 1, slab(w_in_b[0], 0, KOFF + P))
            for f in range(2):
                unit((U_V + f) % 2, U_V + f, slab(w_in_b[0], 0, VOFF + f * P))
            for ff in range(2):
                unit((U_Q + ff) % 2, U_Q + ff, slab(w_in_b[0], 0, ff * P))
            sp.wait_ge(tt_ev, 15)
            for t, pr, sm in ((kout, k_prompt, k_sample), (vtok, v_prompt, v_sample)):
                sp.dma_start(pr[0, 0].rearrange("(j p) g d -> p j (g d)", p=P), t[:, 1:9, :]).then_inc(kk_["st"], 16)
                sp.dma_start(sm.rearrange("b l t g d -> (b l t) (g d)"), t[0:NS, 0, :]).then_inc(kk_["st"], 16)
            for base, off in ((U_Q, 0), (U_Z, ZOFF)):
                with sp.Fori(1 if base == U_Q else 0, NH // 2) as i:
                    for ff in range(2):
                        unit((base + ff) % 2, base + 2 * i + ff, pair(w_in_b[0], off, i, ff))
            for ff in range(2):
                unit((U_O + ff) % 2, U_O + ff, slab(w_out_b[0], 0, ff * P))
            sp.wait_ge(w_used, U_O)
            for b in range(DEC_B):
                if b == 4:
                    for q in range(2):
                        sp.wait_ge(z_st[q], 16 * (KD // 2))
                    sp.wait_ge(at_["o"], NBLK * NKV)
                for f in range(2 * b - 8, 2 * b - 6) if b >= 4 else ():
                    sp.dma_start(zb[f][:], zs[f]).then_inc(z_in[f], 16)
                for dst, src, used, done in ((kpg, cache_k, sa["kt"], kpin), (vpg, cache_v, sa["pv"], vpin)):
                    if b >= 2:
                        sp.wait_ge(used, b - 1)
                    for g in range(NPAGE):
                        page = sp.value_load(ptab[0:1, b * NPAGE + g:b * NPAGE + g + 1],
                                             min_val=0, max_val=cache_k.shape[0] - 1)
                        sp.dma_start(dst[b % 2][:, g, :],
                                     src[bass.ds(page, 1), 0].rearrange("a s g d -> s (a g d)")).then_inc(done[b % 2], 16)
            sp.wait_ge(sa["o"], DEC_B)
            sp.dma_start(xT[:].rearrange("p f n -> p (f n)"), xs).then_inc(xs_in, 16)
            with sp.Fori(1, KD // 2) as i:
                for ff in range(2):
                    unit((U_O + ff) % 2, U_O + 2 * i + ff, pair(w_out_b[0], 0, i, ff))
            gate_loads(1)
            sp.wait_ge(kk_["st"], 16 * 6)

        @block.gpsimd
        def _(pool):
            own = Tally(pool, gv_)
            nc.gpsimd.memset(ones[:], 1.0).then_inc(cst, 1)
            nc.gpsimd.memset(eps[:], EPS).then_inc(cst, 1)
            nc.gpsimd.memset(acc[:], 0.0).then_inc(cst, 1)
            nc.gpsimd.memset(xT[:, :, NT:TP], 0.0).then_inc(cst, 1)
            nc.gpsimd.memset(ss[:], 1.0).then_inc(cst, 1)
            nc.gpsimd.memset(sv[:], 1.0).then_inc(cst, 1)
            own.link(nc.gpsimd.memset(ident[:], 0.0))
            nc.gpsimd.affine_select(out=ident[:], in_=ident[:], compare_op=ALU.not_equal, fill=1.0, base=0,
                                    pattern=[[-1, P]], channel_multiplier=1).then_inc(cst, 1)
            own.link(nc.gpsimd.memset(wsbd[:], 0.0))
            pool.dma_start(wsraw[:], w_s_a[0].rearrange("g t s -> t g s")).then_inc(ws_in, 16)
            col = "(p o) -> p o"
            for j, src in ((0, g_q_b[0]), (1, g_k_b[0])):
                pool.dma_start(gqk[:, j:j + 1], src.rearrange(col, o=1)).then_inc(cst_dma, 16)
            for h in range(2):
                pool.dma_start(gqk[ID * h:ID * h + ID, 2:3], g_ik_b[0].rearrange(col, o=1)).then_inc(cst_dma, 16)
            for l in range(2):
                for dst, src in ((gn, g_norm), (gp, g_pe)):
                    pool.dma_start(dst[:, l, :], src[l].rearrange("(f p) -> p f", p=P),
                                   allow_slow_non_contiguous=True).then_inc(cst_dma, 16)
            pool.dma_start(gv[:], g_v_a[0].rearrange("(f p) -> p f", p=P),
                           allow_slow_non_contiguous=True).then_inc(cst_dma, 16)
            pool.dma_start(bsb[:].rearrange("p g t -> p (g t)"),
                           b_s_a[0].rearrange("g t -> (g t)").partition_broadcast(P)).then_inc(cst_dma, 16)
            pool.dma_start(gvb[:], g_v_a[0].partition_broadcast(NS)).then_inc(gvb_in, 16)
            split_lo(pool, 0, 0)
            pool.wait_ge(ws_ev, 2)
            own.link(nc.gpsimd.affine_select(out=wsT[:], in_=wsT[:], compare_op=ALU.is_ge, fill=0.0, base=0,
                                             pattern=[[0, NGRP], [1, P]], channel_multiplier=-1))
            for b in range(DEC_B):
                s = slice(DEC_T * b, DEC_T * b + DEC_T)
                pool.dma_start(wsbd[s, :, s], wsT[0:DEC_T, :, 0:DEC_T]).then_inc(bd_in, 16)

            def add_squares(sq, f, a, n):
                own.link(nc.gpsimd.tensor_tensor(sq, xT[:, f, a:a + n], xT[:, f, a:a + n], ALU.mult))
                own.link(nc.gpsimd.tensor_tensor(acc[:, a:a + n], acc[:, a:a + n], sq, ALU.add))

            for g in range(2):
                c0, n, _, _ = GROUPS[g]
                for base, trips in ((U_A[g], KA // 2), (U_A[g] + KA, KA)):
                    with pool.Fori(0, trips) as i:
                        for ff in range(2):
                            split_lo(pool, (ff + 1) % 2, base + 2 * i + ff + 1)
                pool.wait_ge(nA[g]["sum"], nA[g].at("sum", 2))
                own.link(nc.gpsimd.memset(acc[:, c0:c0 + n], 0.0))
                with pool.Fori(0, KD // 2) as i:
                    own.enter(i, 4)
                    for ff in range(2):
                        for half in range(2):
                            u = U_A[g] + 3 * KA + 4 * i + 2 * ff + half + 1
                            split_lo(pool, (half + 1) % 2, u)
                        pool.wait_ge(sA[g]["xup"], sA[g].at("xup", 2 * i + ff + 3))
                        add_squares(sqa[:, 0:n], bass.ds(2 * i + ff, 1), c0, n)
                own.leave(KD // 2)
                pool.sem_inc(stat, 1)

            def gate_pool(layer, last):
                s, base = sG[layer], U_GATE[layer]
                pool.wait_ge(nG[layer]["sum"], nG[layer].at("sum", 3))
                own.link(nc.gpsimd.memset(acc[:], 0.0))
                nc.gpsimd.memset(pThi[:, :, NT:TP].bitcast(F32), 0.0).then_inc(s["plo"], 1)
                nc.gpsimd.memset(pTlo[:, :, NT:TP].bitcast(F32), 0.0).then_inc(s["plo"], 1)

                def tile(i, ff):
                    f = 2 * i + ff
                    pool.wait_ge(s["wph"], s.at("wph", f + 1))
                    nc.gpsimd.tensor_tensor(pelo[:], peraw[:, :, bass.ds(f * P, P)], pehi[:].bitcast(F32),
                                            ALU.subtract).then_inc(s["wpl"], 1)
                    if not (last and f == KD - 1):
                        split_lo(pool, (base + ff + 1) % 2, base + f + 1)
                    if not last:
                        pool.wait_ge(s["xup"], s.at("xup", f + 2))
                        add_squares(sqb, bass.ds(f, 1), 0, TP)

                if last:
                    for f in range(KD):
                        tile(f // 2, f % 2)
                else:
                    with pool.Fori(0, KD // 2) as i:
                        own.enter(i, 4)
                        for ff in range(2):
                            tile(i, ff)
                    own.leave(KD // 2)
                    pool.sem_inc(stat, 1)

            gate_pool(0, False)
            for f in range(IH // 2):
                split_lo(pool, (U_IQ + f + 1) % 2, U_IQ + f + 1)
            split_lo(pool, 1, U_K)
            own.link(nc.gpsimd.memset(caus[:], 0.0))
            nc.gpsimd.affine_select(out=caus[:, P:2 * P], in_=caus[:, P:2 * P], compare_op=ALU.is_ge, fill=-BIG,
                                    base=0, pattern=[[-1, P]], channel_multiplier=1).then_inc(cs_ok, 1)
            pool.wait_ge(xs_out, 16)
            nc.gpsimd.memset(iqb[:], 0.0).then_inc(ss_["pre"], 1)
            nscore = 0
            for b in range(2, NBLK):
                nscore += IH * ((b + 4) // 4)
                pool.wait_ge(sc_ad, nscore)
                d = slice(block_off(b) + b * P, block_off(b) + (b + 1) * P)
                nc.gpsimd.affine_select(out=sc[:, d], in_=sc[:, d], compare_op=ALU.is_ge, fill=MASKED, base=0,
                                        pattern=[[-1, P]], channel_multiplier=1).then_inc(sc_ok, 1)
            pool.wait_ge(ss_["cp"], 1)
            new = scs[:, PAST:SLS]
            own.link(nc.gpsimd.affine_select(out=new, in_=new, compare_op=ALU.is_ge, fill=MASKED, base=0,
                                             pattern=[[-1, NS]], channel_multiplier=1))
            nc.gpsimd.affine_select(out=new.rearrange("p (b t) -> p b t", t=DEC_T),
                                    in_=new.rearrange("p (b t) -> p b t", t=DEC_T), compare_op=ALU.is_ge,
                                    fill=MASKED, base=DEC_T - 1, pattern=[[DEC_T, DEC_B], [0, DEC_T]],
                                    channel_multiplier=-1).then_inc(ss_["ok"], 1)
            for u in range(U_K + 1, U_Q + 1):
                split_lo(pool, u % 2, u)
            for base in (U_Q, U_Z):
                with pool.Fori(0, NH // 2) as i:
                    for ff in range(2):
                        split_lo(pool, (base + ff + 1) % 2, base + 2 * i + ff + 1)
            pool.wait_ge(at_["o"], NBLK * NKV)
            own.link(nc.gpsimd.memset(acc[:], 0.0))
            with pool.Fori(0, KD // 2) as i:
                own.enter(i, 4)
                for ff in range(2):
                    split_lo(pool, (U_O + ff + 1) % 2, U_O + 2 * i + ff + 1)
                    pool.wait_ge(oy["xup"], 2 * i + ff + 3)
                    add_squares(sqt[:], bass.ds(2 * i + ff, 1), 0, TP)
            own.leave(KD // 2)
            pool.sem_inc(stat, 1)
            gate_pool(1, True)

        @block.scalar
        def _(act):
            own = Tally(act, av)
            for name, free in (("vev", 2), ("sz", 1)):
                act.sem_inc(gmlp[name], free)
            act.sem_inc(embed_sems["sig"], 1)
            act.sem_inc(iq["swa"], 2)
            act.sem_inc(qq["swa"], 2)
            act.sem_inc(z_ev, 2)
            act.wait_ge(cst, 7)
            for j in range(9):
                c0, n = tile_cols(j)
                act.wait_ge(x_in[j % 3], 16 * (j // 3 + 1))
                if j:
                    act.wait_ge(x_sq, j)
                nc.scalar.activation(sqdump[0:n, :], xstage[0:n, j % 3, :], ACT.Square,
                                     accum_out=ss[0:n, j:j + 1]).then_inc(x_sq, 1)
                act.wait_ge(x_tr, j + 1)
                nc.scalar.activation(xT[:, 4:8, c0:c0 + n],
                                     PSF[:, (2 * (j % 3) + 1) * BANK:(2 * (j % 3) + 2) * BANK]
                                     .rearrange("p (k t) -> p k t", k=4)[:, :, 0:n], ACT.Copy).then_inc(x_eva, 1)
            split_hi(act, 0, 1, 0)
            act.wait_ge(ws_tr, 2)
            for h in range(2):
                nc.scalar.activation(wsT[:, 4 * h:4 * h + 4, :].rearrange("p g t -> p (g t)"),
                                     PS[:, 6 + h, :], ACT.Copy).then_inc(ws_ev, 1)

            def split_unit(u):
                split_hi(act, u % 2, u // 2 + 1, u)

            def group_hi(g):
                n = GROUPS[g][1]
                return lambda k: hhi_g[:, k, 0:n], lambda k: hfa[:, k % 2, 0:n]

            for g in range(2):
                c0, n, nch, has_s = GROUPS[g]
                h = n // 2
                s = sA[g]
                if g == 0:
                    norm_act(act, nA[g], group_cols(g), group_hi(g))
                def v_out_of_psum(f, ff):
                    act.wait_ge(w_used, U_A[g] + f + 1)
                    act.wait_ge(s["vtr"], s.at("vtr", f + 1))
                    nc.scalar.activation(vtmp[ff][:, 0:n].rearrange("p (b n) -> p b n", b=2),
                                         PS[:, 2 * ff:2 * ff + 2, 0:h], ACT.Copy).then_inc(s["vev"], 1)

                with act.Fori(0, KA // 2) as i:
                    for ff in range(2):
                        split_hi(act, (ff + 1) % 2, (U_A[g] + ff + 1) // 2 + i + 1, U_A[g] + 2 * i + ff + 1)
                        v_out_of_psum(2 * i + ff, ff)
                split_unit(U_A[g] + KA + 1)
                act.wait_ge(s["vst"], s.at("vst", KA + 2))
                for c in range(nch + has_s):
                    rows = P if c < nch else NS
                    if c:
                        act.wait_ge(s["vsq"], s.at("vsq", c))
                    nc.scalar.activation(vdump[0:rows], v_raw[0:rows, :, c * P:(c + 1) * P], ACT.Square,
                                         accum_out=sv[0:rows, c:c + 1]).then_inc(s["vsq"], 1)
                act.wait_ge(s["vsq"], s.at("vsq", nch + has_s))
                nc.scalar.activation(rv[:], sv[:], ACT.Sqrt, bias=eps[:], scale=1.0 / AW).then_inc(s["rv"], 1)
                if has_s:
                    act.wait_ge(vo_ok, 1)
                    act.dma_start(chunk_v_sample.rearrange("b l t w -> (b l t) w"), v_out[:]).then_inc(vo_st, 16)
                with act.Fori(0, KA) as f:
                    act.wait_ge(w_used, U_A[g] + KA + 2 * f + 1)
                    act.wait_ge(s["ut"], s.at("ut", f + 1))
                    nc.scalar.activation(szt[:, 0:n].rearrange("p (b n) -> p b n", b=2),
                                         PS[:, 0:2, 0:h], ACT.Silu).then_inc(s["sz"], 1)
                    for half in range(2):
                        split_hi(act, half, (U_A[g] + KA + 2) // 2 + f + 1, U_A[g] + KA + 2 * f + 2 + half)
                    act.wait_ge(s["y"], s.at("y", f + 1))
                    nc.scalar.activation(yhi[:, bass.ds(f, 1), 0:n], t1a[:, 0:n].unsqueeze(1), ACT.Copy).then_inc(s["yhi"], 1)
                if g == 0:
                    norm_roots(act, nA[1], group_cols(1))
                for f in range(KD):
                    if f:
                        split_unit(U_A[g] + 3 * KA + 2 * f + 1)
                    split_unit(U_A[g] + 3 * KA + 2 * f + 2)
                    if g == 0:
                        norm_hi(act, nA[1], f, *group_hi(1))

            def gate_act(layer, last):
                s, base = sG[layer], U_GATE[layer]
                norm_act(act, nG[layer], ALL_COLS, (lambda k: hhi[:, k, :], lambda k: hfb[:, k % 2, :]))
                act.wait_ge(s["ptr"], s.at("ptr", 6))
                act.wait_ge(s["plo"], s.at("plo", 2))
                for kk, m, bank, q, a, n in PIECES_P:
                    nc.scalar.activation(pThi[:, kk, a:a + n], PS[:, bank, q:q + n], ACT.Copy).then_inc(s["phi"], 1)
                act.wait_ge(s["pein"], s.at("pein", 16))

                def tile(i, ff):
                    f = 2 * i + ff
                    act.wait_ge(s["pe"], s.at("pe", f + 1))
                    nc.scalar.activation(pehi[:], peraw[:, :, bass.ds(f * P, P)], ACT.Copy).then_inc(s["wph"], 1)
                    if not (last and f == KD - 1):
                        split_hi(act, (base + ff + 1) % 2, (base + ff + 1) // 2 + i + 1, base + f + 1)
                    act.wait_ge(w_used, base + f + 1)
                    act.wait_ge(s["t"], s.at("t", f + 1))
                    nc.scalar.activation(as3(sig[:]), slot3(0), ACT.Sigmoid).then_inc(s["sig"], 1)

                if last:
                    for f in range(KD):
                        tile(f // 2, f % 2)
                        if f >= 1:
                            store_tile(f - 1)
                    store_tile(KD - 1)
                else:
                    with act.Fori(0, KD // 2) as i:
                        for ff in range(2):
                            tile(i, ff)

            def store_tile(f):
                act.wait_ge(y_ev, 3 * f + 4)
                act.dma_start(y_sample.rearrange("b t d -> (b t) d")[:, f * P:(f + 1) * P],
                              ystage[0:NS, f % 2, 0, :]).then_inc(y_st[f % 2], 16)
                act.dma_start(y_prompt[0, :, f * P:(f + 1) * P].rearrange("(j p) d -> p j d", p=P),
                              ystage[:, f % 2, 1:9, :]).then_inc(y_st[f % 2], 16)

            gate_act(0, False)
            norm_roots(act, nB, ALL_COLS)
            split_unit(U_IQ + 1)
            for k in range(KD):
                norm_hi(act, nB, k, lambda k: hhi[:, k, :], lambda k: hfb[:, k % 2, :])

            def swap(dst, slot, size, scale, n=P):
                for p0 in range(0, n, 2 * size):
                    for a, b in ((p0, p0 + size), (p0 + size, p0)):
                        last = nc.scalar.activation(as3(dst[a:a + size, :]), slot3(slot)[b:b + size], ACT.Copy,
                                                    scale=1.0 if scale is None else scale[b:b + size])
                return last

            for f in range(IH // 2):
                if f:
                    split_unit(U_IQ + f + 1)
                act.wait_ge(w_used, U_IQ + f + 1)
                act.wait_ge(iq["add"], f + 1)
                act.wait_ge(iq["t1d"], f + 3)
                swap(swp, f % 2, ID // 2, None).then_inc(iq["swa"], 1)
            split_hi(act, 1, (U_K) // 2 + 1, U_K)
            act.wait_ge(w_used, U_IK + 1)
            act.wait_ge(iq["add"], 5)
            nc.scalar.activation(as3(sqt[0:ID, :]), slot3(0)[0:ID], ACT.Square).then_inc(kk_["swa"], 1)
            for q in range(2):
                nc.scalar.activation(as3(ikT[ID * q:ID * q + ID, :]), slot3(0)[0:ID], ACT.Copy, scale=gqk[0:ID, 2:3])
                for a, b in ((0, ID // 2), (ID // 2, 0)):
                    nc.scalar.activation(as3(swp[ID * q + a:ID * q + a + ID // 2, :]), slot3(0)[b:b + ID // 2],
                                         ACT.Copy, scale=gqk[b:b + ID // 2, 2:3])
            nc.scalar.activation(as3(iwT[:]), slot3(0)[ID:ID + IH], ACT.Copy).then_inc(kk_["swa"], 1)

            def roots(n, dim):
                for c, (a, m) in enumerate(ALL_COLS):
                    act.wait_ge(kk_["sum"], 3 * n + c + 1)
                    nc.scalar.activation(rbc[:, a:a + m], PS[:, 6 + c % 2, 0:m], ACT.Sqrt, bias=eps[:],
                                         scale=1.0 / dim).then_inc(kk_["rt"], 1)

            roots(0, ID)
            for m, (b, c, h) in enumerate(SCORES):
                n = min(BANK, (b + 1) * P - c * BANK)
                act.wait_ge(sc_mm, m + 1)
                if m >= 2:
                    act.wait_ge(sc_ad, m - 1)
                nc.scalar.activation(pring[m % 2][:, 0:n], PS[:, m % 6, 0:n], ACT.Relu).then_inc(sc_re, 1)

            def ikT_evac(b):
                act.wait_ge(ss_["tr"], b + 1)
                if b >= 2:
                    act.wait_ge(ss_["mm"], b - 1)
                nc.scalar.activation(ikTb[b % 2][:], PSF[:, 6 * BANK:8 * BANK], ACT.Copy).then_inc(ss_["ev"], 1)

            act.wait_ge(ss_["wt"], 1)
            nc.scalar.activation(sbw[:].rearrange("p b n -> p (b n)"), PS[0:NS, 5, :], ACT.Copy).then_inc(ss_["wt"], 1)
            ikT_evac(0)
            for b in range(DEC_B):
                if b + 1 < DEC_B:
                    ikT_evac(b + 1)
                act.wait_ge(ss_["mm"], b + 1)
                if b:
                    act.wait_ge(ss_["sum"], b)
                nc.scalar.activation(rels[:], PSF[0:NS, 3 * BANK:3 * BANK + SLS], ACT.Relu).then_inc(ss_["re"], 1)

            for g in range(NKV):
                u = U_K + g
                split_hi(act, (u + 1) % 2, (u + 1) // 2 + 1, u + 1)
                act.wait_ge(w_used, u + 1)
                if g == 0:
                    act.wait_ge(sc_ad, len(SCORES))
                act.wait_ge(kk_["done"], g + 1)
                act.wait_ge(kk_["t1d"], g + 1)
                nc.scalar.activation(as3(sqt[:]), slot3(u % 2), ACT.Square).then_inc(kk_["swa"], 1)
                swap(swp, u % 2, DH // 2, gqk[:, 1:2]).then_inc(kk_["swa"], 1)
                roots(1 + g, DH)
            for g in range(NKV):
                u = U_V + g
                split_hi(act, (u + 1) % 2, (u + 1) // 2 + 1, u + 1)
                act.wait_ge(w_used, u + 1)
                act.wait_ge(kk_["done"], 3)
                if g:
                    act.wait_ge(tt_tr, 12)
                nc.scalar.activation(as3(sqt[:]), slot3(u % 2), ACT.Copy).then_inc(kk_["vev"], 1)
            act.wait_ge(tt_tr, 15)
            with act.Fori(0, NH // 2) as i:
                for ff in range(2):
                    f = 2 * i + ff
                    split_hi(act, (U_Q + ff + 1) % 2, (U_Q + ff + 1) // 2 + i + 1, U_Q + f + 1)
                    act.wait_ge(w_used, U_Q + f + 1)
                    act.wait_ge(qq["add"], f + 1)
                    act.wait_ge(qq["t1d"], f + 3)
                    act.wait_ge(qq["st"], f + 1)
                    slot = (U_Q + ff) % 2
                    nc.scalar.activation(as3(sqt[:]), slot3(slot), ACT.Square)
                    swap(swp, slot, DH // 2, gqk[:, 0:1]).then_inc(qq["swa"], 1)
            act.wait_ge(qq["add"], 9)
            for f in range(KD):
                split_hi(act, (U_Z + f + 1) % 2, (U_Z + f + 1) // 2 + 1, U_Z + f + 1)
                act.wait_ge(w_used, U_Z + f + 1)
                if f >= 2:
                    act.wait_ge(z_st[f % 2], 16 * (f // 2))
                nc.scalar.activation(as3(zst[f % 2][:]), slot3((U_Z + f) % 2), ACT.Silu).then_inc(z_ev, 1)
                act.wait_ge(z_ev, f + 3)
                act.dma_start(zs[f], zst[f % 2][:]).then_inc(z_st[f % 2], 16)
                if f == 1:
                    act.wait_ge(qq["end"], 1)
                    for rows, j in ((NS, slice(0, 1)), (P, slice(1, 9))):
                        nc.scalar.activation(qs[0:rows, j, :], PS[0:rows, 7, 0:9 * NH].rearrange("p (j h) -> p j h", h=NH)[:, j],
                                             ACT.Sqrt, bias=eps[0:rows], scale=1.0 / DH).then_inc(qq["rt"], 1)

            def pieces_out(n):
                for i in range(FIRST[n], FIRST[n + 1]):
                    _, b, h, m = PIECES[i]
                    k = min(4, b + 1 - 4 * m)
                    act.wait_ge(at_["tr"], i + 1)
                    if h % REP == 0 and n >= REP:
                        act.wait_ge(at_["pv"], n // REP)
                    nc.scalar.activation(PTs[:, 4 * m:4 * m + k, h % REP, :],
                                         PS[:, 4 + i % 2, 0:k * P].rearrange("p (k q) -> p k q", q=P),
                                         ACT.Copy).then_inc(at_["pt"], 1)

            for n, (b, h) in enumerate(STEPS):
                w = (b + 1) * P
                act.wait_ge(at_["nb"], n + 1)
                nc.scalar.activation(pring[n % NR][:, 0:w], pring[n % NR][:, 0:w], ACT.Exp, bias=anb[:, n:n + 1],
                                     scale=qs[:, 1 + b, h:h + 1], accum_out=asm[:, n:n + 1]).then_inc(at_["ex"], 1)
                if n:
                    pieces_out(n - 1)
            pieces_out(len(STEPS) - 1)

            act.wait_ge(sa["qc"], 1)
            nc.scalar.activation(qcol[:], PS[0:NS, 3, 0:DEC_B], ACT.Copy)
            nc.scalar.activation(nqcol[:], PS[0:NS, 3, 0:DEC_B], ACT.Copy, scale=-1.0).then_inc(sa["qc"], 1)

            def kT_evac(b):
                act.wait_ge(sa["kt"], b + 1)
                if b:
                    act.wait_ge(sa["s"], b)
                for g in range(NKV):
                    last = nc.scalar.activation(kTb[:, g, :], PSF[:, (4 + 2 * g) * BANK:(6 + 2 * g) * BANK], ACT.Copy)
                last.then_inc(sa["ke"], 1)

            kT_evac(0)
            for b in range(DEC_B):
                act.wait_ge(sa["nb"], b + 1)
                if b:
                    act.wait_ge(sa["tr"], b)
                nc.scalar.activation(Ps[:], PSF[0:NS, 0:SLS], ACT.Exp, bias=snb[:, b:b + 1], scale=qcol[:, b:b + 1],
                                     accum_out=ssm[:, b:b + 1]).then_inc(sa["ex"], 1)
                if b + 1 < DEC_B:
                    kT_evac(b + 1)
                act.wait_ge(sa["tr"], b + 1)
                if b:
                    act.wait_ge(sa["pv"], b)
                nc.scalar.activation(PsT[:, 0:8, :].rearrange("p k n -> p (k n)"), PS[:, 3, :], ACT.Copy)
                nc.scalar.activation(PsT[0:NS, 8, :], PS[0:NS, 4, 0:NS], ACT.Copy).then_inc(sa["pt"], 1)

            split_unit(U_O + 1)
            for f in range(KD):
                act.wait_ge(oy["y"], f + 1)
                nc.scalar.activation(hhi[:, f, :], qT[:, f, :], ACT.Copy).then_inc(oy["hi"], 1)
            for f in range(1, KD):
                split_unit(U_O + f + 1)
            gate_act(1, True)
            for q in range(2):
                act.wait_ge(y_st[q], 32 * KD // 2)
            act.wait_ge(vo_st, 16)

        @block.vector
        def _(dve):
            own = Tally(dve, dv)
            for name, free in (("vst", 2), ("ut", 1), ("mt", 1), ("xup", 2), ("ylo", 1)):
                dve.sem_inc(gmlp[name], free)
            for name in ("t", "xup"):
                dve.sem_inc(embed_sems[name], 1)
            dve.sem_inc(y_ev, 1)
            for q in (iq, qq):
                dve.sem_inc(q["t1d"], 2)
                dve.sem_inc(q["add"], 1)
            dve.sem_inc(oy["xup"], 2)
            dve.wait_ge(cst, 7)
            dve.wait_ge(cst_dma, 16 * 10)
            for j in range(9):
                c0, n = tile_cols(j)
                dve.wait_ge(x_tr, j + 1)
                nc.vector.tensor_copy(xT[:, 0:4, c0:c0 + n],
                                      PSF[:, 2 * (j % 3) * BANK:(2 * (j % 3) + 1) * BANK]
                                      .rearrange("p (k t) -> p k t", k=4)[:, :, 0:n]).then_inc(x_ev, 1)
                dve.wait_ge(x_sq, j + 1)
                nc.vector.tensor_scalar(acc[0:n, c0:c0 + n], ident[0:n, 0:n], ss[0:n, j:j + 1], None,
                                        ALU.mult).then_inc(x_dg, 1)

            def group_tile(g):
                n = GROUPS[g][1]
                return (lambda k: gn[:, 0, k:k + 1], lambda k: hfa[:, k % 2, 0:n],
                        lambda k: hhi_g[:, k, 0:n], lambda k: hlo_g[:, k, 0:n])

            for g in range(2):
                c0, n, nch, has_s = GROUPS[g]
                h = n // 2
                s = sA[g]
                if g == 0:
                    norm_dve(dve, own, nA[g], group_cols(g), *group_tile(g))
                dve.wait_ge(bd_in, 16 * DEC_B)
                with dve.Fori(0, KA // 2) as i:
                    for ff in range(2):
                        f = 2 * i + ff
                        dve.wait_ge(s["vtr"], s.at("vtr", f + 3))
                        vdst = nc.vector.tensor_copy(v_raw[:, bass.ds(f, 1), 0:4 * P].rearrange("p o n -> p (o n)"),
                                                     PS[:, 4 + 2 * ff, :])
                        if has_s:
                            vdst = nc.vector.tensor_copy(
                                v_raw[0:NS, bass.ds(f, 1), 4 * P:5 * P].rearrange("p o n -> p (o n)"),
                                PS[0:NS, 5 + 2 * ff, 0:P])
                        vdst.then_inc(s["vst"], 1)
                dve.wait_ge(s["rv"], s.at("rv", 1))
                own.link(nc.vector.reciprocal(rv[:], rv[:]))
                if has_s:
                    dve.wait_ge(gvb_in, 16)
                    nc.vector.scalar_tensor_tensor(
                        v_out[:].rearrange("p (f d) -> p f d", d=P), v_raw[0:NS, :, 4 * P:5 * P], rv[0:NS, 4:5],
                        gvb[:].rearrange("p (f d) -> p f d", d=P), ALU.mult, ALU.mult).then_inc(vo_ok, 1)
                if n > nch * P + (NS if has_s else 0):
                    own.link(nc.vector.memset(t1a[:, nch * P:n], 0.0))
                po = NS if has_s else 0
                if g:
                    dve.wait_ge(stat, g)
                with dve.Fori(0, KA // 2) as i:
                    own.enter(i, 4)
                    for ff in range(2):
                        f = 2 * i + ff
                        for c in range(nch + has_s):
                            rows = P if c < nch else NS
                            scaled = nc.vector.tensor_scalar(
                                vs[0:rows, c * P:(c + 1) * P],
                                v_raw[0:rows, bass.ds(f, 1), c * P:(c + 1) * P].rearrange("p o n -> p (o n)"),
                                rv[0:rows, c:c + 1], None, ALU.mult)
                        scaled.then_inc(s["vs"], 1)
                        dve.wait_ge(w_used, U_A[g] + KA + 2 * f + 2)
                        dve.wait_ge(s["sz"], s.at("sz", f + 2))
                        nc.vector.tensor_tensor(t2a[:, 0:n].rearrange("p (b n) -> p b n", b=2),
                                                PS[:, 2:4, 0:h],
                                                szt[:, 0:n].rearrange("p (b n) -> p b n", b=2),
                                                ALU.mult).then_inc(s["ut"], 1)
                        dve.wait_ge(s["mix"], s.at("mix", f + 1))
                        dve.wait_ge(s["ylo"], s.at("ylo", f + 1))
                        if has_s:
                            nc.vector.scalar_tensor_tensor(
                                t1a[:, 0:NS].rearrange("p (b t) -> p b t", t=DEC_T),
                                PS[:, 5, 0:NS].rearrange("p (b t) -> p b t", t=DEC_T), gv[:, bass.ds(f, 1)],
                                bsb[:, bass.ds(i, 1), 0:DEC_T].broadcast_to((P, DEC_B, DEC_T)), ALU.mult, ALU.add)
                        own.link(nc.vector.scalar_tensor_tensor(
                            t1a[:, po:po + 4 * P].rearrange("p (c t) -> p c t", t=P),
                            PS[:, 4, :].rearrange("p (c t) -> p c t", t=P), gv[:, bass.ds(f, 1)],
                            bsb[:, bass.ds(i, 1), :].broadcast_to((P, 4, P)), ALU.mult, ALU.add))
                        dve.wait_ge(s["ut"], s.at("ut", f + 2))
                        own.link(nc.vector.tensor_tensor(t1a[:, 0:n], t1a[:, 0:n], t2a[:, 0:n], ALU.mult))
                        dve.sem_inc(s["mt"], 1)
                        dve.sem_inc(s["y"], 1)
                        if has_s:
                            dve.wait_ge(vo_st, 16)
                        dve.wait_ge(s["yhi"], s.at("yhi", f + 1))
                        nc.vector.tensor_tensor(ylo[:, bass.ds(f, 1), 0:n], t1a[:, 0:n].unsqueeze(1),
                                                yhi[:, bass.ds(f, 1), 0:n].bitcast(F32), ALU.subtract).then_inc(s["ylo"], 1)
                own.leave(KA // 2)
                if g == 0:
                    norm_inverse(dve, own, nA[1], group_cols(1))
                for f in range(KD + 1):
                    if g == 0:
                        norm_tile(dve, nA[1], f, *GROUPS[1][0:2], *group_tile(1))
                    if f < KD:
                        dve.wait_ge(w_used, U_A[g] + 3 * KA + 2 * f + 2)
                        x = xT[:, f, c0:c0 + n].rearrange("p (b n) -> p b n", b=2)
                        b = 2 * (f % 2)
                        nc.vector.tensor_tensor(x, PS[:, b:b + 2, 0:h], x, ALU.add).then_inc(s["xup"], 1)

            def gate_dve(layer, last):
                s, base = sG[layer], U_GATE[layer]
                norm_dve(dve, own, nG[layer], ALL_COLS, lambda k: gp[:, layer, k:k + 1],
                         lambda k: hfb[:, k % 2, :], lambda k: hhi[:, k, :], lambda k: hlo[:, k, :])
                dve.wait_ge(s["phi"], s.at("phi", 6))
                for kk, m, bank, q, a, n in PIECES_P:
                    nc.vector.tensor_tensor(pTlo[:, kk, a:a + n], PS[:, bank, q:q + n],
                                            pThi[:, kk, a:a + n].bitcast(F32), ALU.subtract).then_inc(s["plo"], 1)

                def tile(i, ff):
                    f = 2 * i + ff
                    dve.wait_ge(s["pe"], s.at("pe", f + 2))
                    dve.wait_ge(s["sig"], s.at("sig", f + 2))
                    dve.wait_ge(s["xup"], s.at("xup", f + 1))
                    nc.vector.tensor_tensor(as3(tpe[:]), slot3(1), as3(sig[:]), ALU.mult).then_inc(s["t"], 1)
                    dve.wait_ge(s["t"], s.at("t", f + 2))
                    if last:
                        nc.vector.tensor_tensor(xo[:, ff, :], xT[:, f, :], tpe[:], ALU.add).then_inc(s["xup"], 1)
                    else:
                        x = xT[:, bass.ds(f, 1), :].rearrange("p o n -> p (o n)")
                        nc.vector.tensor_tensor(x, x, tpe[:], ALU.add).then_inc(s["xup"], 1)

                if last:
                    for f in range(KD):
                        if f >= 1:
                            evac_out(f - 1)
                        tile(f // 2, f % 2)
                    evac_out(KD - 1)
                else:
                    with dve.Fori(0, KD // 2) as i:
                        for ff in range(2):
                            tile(i, ff)

            def evac_out(f):
                if f >= 2:
                    dve.wait_ge(y_st[f % 2], 32 * (f // 2))
                for m in range(3):
                    dve.wait_ge(y_tr, 3 * f + m + 1)
                    if m < 2:
                        nc.vector.tensor_copy(ystage[:, f % 2, 1 + 4 * m:5 + 4 * m, :],
                                              PS[:, 6 + m, :].rearrange("p (j d) -> p j d", d=P)).then_inc(y_ev, 1)
                    else:
                        nc.vector.tensor_copy(ystage[0:NS, f % 2, 0, :], PS[0:NS, 6, 0:P]).then_inc(y_ev, 1)

            gate_dve(0, False)
            norm_dve(dve, own, nB, ALL_COLS, lambda k: gn[:, 1, k:k + 1],
                     lambda k: hfb[:, k % 2, :], lambda k: hhi[:, k, :], lambda k: hlo[:, k, :])

            def rotate(s, used, f, slot, dst, cs, sn, g):
                dve.wait_ge(w_used, used + 1)
                dve.wait_ge(s["add"], f + 1)
                if g is None:
                    t = nc.vector.tensor_tensor(as3(tq[:]), slot3(slot), as3(cs[:]), ALU.mult)
                else:
                    t = nc.vector.scalar_tensor_tensor(as3(tq[:]), slot3(slot), g, as3(cs[:]), ALU.mult, ALU.mult)
                t.then_inc(s["t1d"], 1)
                dve.wait_ge(s["swa"], f + 3)
                own.link(nc.vector.tensor_tensor(swp[:], swp[:], sn[:], ALU.mult))
                dve.wait_ge(s["t1d"], f + 3)
                nc.vector.tensor_tensor(dst, tq[:], swp[:], ALU.add).then_inc(s["add"], 1)

            dve.wait_ge(tabI, 32)
            with dve.Fori(0, IH // 4) as i:
                own.enter(i, 2)
                for ff in range(2):
                    f = 2 * i + ff
                    rotate(iq, U_IQ + f, f, ff, iqT[:, bass.ds(f, 1), :].rearrange("p o n -> p (o n)"), csI, snI, None)
            own.leave(IH // 4)
            dve.wait_ge(kk_["swa"], 2)
            own.link(nc.vector.tensor_tensor(ikT[:], ikT[:], csI[:], ALU.mult))
            own.link(nc.vector.tensor_tensor(swp[:], swp[:], snI[:], ALU.mult))
            own.link(nc.vector.tensor_tensor(ikT[:], ikT[:], swp[:], ALU.add))
            dve.wait_ge(kk_["rt"], 3)
            own.link(nc.vector.reciprocal(rbc[:], rbc[:]))
            nc.vector.tensor_tensor(ikT[:], ikT[:], rbc[:], ALU.mult).then_inc(kk_["done"], 1)

            def tokens_out(n, dst, width, off=0):
                for m in range(3):
                    dve.wait_ge(tt_tr, 3 * n + m + 1)
                    if m < 2:
                        nc.vector.tensor_copy(dst[:, 1 + 4 * m:5 + 4 * m, off:off + width],
                                              PS[:, 6 + m, 0:4 * width].rearrange("p (j d) -> p j d", d=width)).then_inc(tt_ev, 1)
                    else:
                        nc.vector.tensor_copy(dst[0:NS, 0, off:off + width], PS[0:NS, 6, 0:width]).then_inc(tt_ev, 1)

            dve.wait_ge(xs_out, 16)
            tokens_out(0, ikout, ID)
            dve.wait_ge(iw_tr, 1)
            c = (ID ** -0.5) * (IH ** -0.5)
            nc.vector.tensor_scalar(iwt[:, 1:9, :], PS[:, 7, IH:9 * IH].rearrange("p (j h) -> p j h", h=IH), c, None, ALU.mult)
            own.link(nc.vector.tensor_scalar(iwt[0:NS, 0, :], PS[0:NS, 7, 0:IH], c, None, ALU.mult))
            dve.sem_inc(iw_ev, 1)
            dve.wait_ge(ss_["pre"], 1)
            for q in range(2):
                nc.vector.tensor_copy(
                    iqb[ID * q:ID * q + ID, :, 32 * q:32 * q + 32].rearrange("p b (r t) -> p r b t", t=DEC_T),
                    iqT[ID * q:ID * q + ID, :, 0:NS].rearrange("p r (b t) -> p r b t", t=DEC_T))
            idv = ident[0:NS, 0:NS].rearrange("p (b t) -> p b t", t=DEC_T).unsqueeze(2)
            for q in range(2):
                last = nc.vector.tensor_tensor(
                    sbT[:, :, 32 * q:32 * q + 32].rearrange("p b (r t) -> p b r t", t=DEC_T),
                    idv.broadcast_to((NS, DEC_B, IH // 2, DEC_T)),
                    iwt[0:NS, 0, q:IH:2].unsqueeze(1).unsqueeze(3).broadcast_to((NS, DEC_B, IH // 2, DEC_T)), ALU.mult)
            last.then_inc(ss_["pre"], 1)
            nc.vector.tensor_copy(repb[:].rearrange("p b (h t) -> p b h t", t=DEC_T),
                                  idv.broadcast_to((NS, DEC_B, NH, DEC_T))).then_inc(ss_["pre"], 1)

            for m, (b, c, h) in enumerate(SCORES):
                n = min(BANK, (b + 1) * P - c * BANK)
                x = sc[:, block_off(b) + c * BANK:block_off(b) + c * BANK + n]
                dve.wait_ge(sc_re, m + 1)
                if h == 0:
                    nc.vector.tensor_scalar(x, pring[m % 2][:, 0:n], iwt[:, 1 + b, h:h + 1], None,
                                            ALU.mult).then_inc(sc_ad, 1)
                else:
                    dve.wait_ge(sc_ad, m)
                    nc.vector.scalar_tensor_tensor(x, pring[m % 2][:, 0:n], iwt[:, 1 + b, h:h + 1], x,
                                                   ALU.mult, ALU.add).then_inc(sc_ad, 1)

            PROMPT = (P, slice(0, NBLK - 2), [sc[:, block_off(b):block_off(b + 1)] for b in range(2, NBLK)])
            SAMPLE = (NS, slice(NBLK - 2, NBLK - 1), [scs[:]])

            def count(group, op, against):
                rows, cols, areas = group
                for j, x in enumerate(areas, cols.start):
                    own.link(nc.vector.tensor_scalar(acc[0:rows, 0:x.shape[1]], x,
                                                     0.0 if against is None else against[0:rows, j:j + 1], None,
                                                     op, ALU.add, accum_out=cnt[0:rows, j:j + 1]))

            def start_search(group):
                r, c = slice(0, group[0]), group[1]
                count(group, ALU.is_ge, None)
                own.link(nc.vector.tensor_scalar(sgn[r, c], cnt[r, c], TOPK - 0.5, None, ALU.is_ge))
                own.link(nc.vector.tensor_scalar(tbit[r, c], sgn[r, c], -1.0, 1.0, ALU.mult, ALU.add))
                own.link(nc.vector.tensor_scalar(tbit[r, c], tbit[r, c], 31, 31, ALU.logical_shift_left, ALU.arith_shift_right))
                own.link(nc.vector.tensor_scalar(tbit[r, c], tbit[r, c], 0x7FFFFFFF, None, ALU.bitwise_and))
                own.link(nc.vector.tensor_scalar(sgn[r, c], sgn[r, c], 2.0, -1.0, ALU.mult, ALU.add))
                own.link(nc.vector.memset(bitc[r, c], 1 << 30))

            def search_bit(group):
                r, c = slice(0, group[0]), group[1]
                own.link(nc.vector.tensor_tensor(cand[r, c], tbit[r, c], bitc[r, c], ALU.bitwise_xor))
                own.link(nc.vector.tensor_tensor(thr[r, c], cand[r, c].bitcast(F32), sgn[r, c], ALU.mult))
                count(group, ALU.is_ge, thr)
                own.link(nc.vector.scalar_tensor_tensor(mbit[r, c], cnt[r, c], TOPK - 0.5, bitc[r, c], ALU.is_ge, ALU.mult))
                own.link(nc.vector.tensor_tensor(tbit[r, c], tbit[r, c], mbit[r, c], ALU.bitwise_xor))
                own.link(nc.vector.tensor_scalar(bitc[r, c], bitc[r, c], 1, None, ALU.logical_shift_right))

            BIT_LINKS = 5 + len(PROMPT[2])

            def search_bits(trips):
                with dve.Fori(0, trips) as i:
                    own.enter(i, BIT_LINKS)
                    search_bit(PROMPT)
                own.leave(trips)

            RESOLVE_AT = [(0, 1), (2, 3), (4,), (5,), (6,), (7,), (), ()]

            def resolve(group, j, x, t1, t2, part):
                r, c, n = slice(0, group[0]), slice(j, j + 1), x.shape[1]
                eq, cum = t1[r, 0:n], t2[r, 0:n]
                if part == 0:
                    own.link(nc.vector.tensor_tensor(thr[r, c], tbit[r, c].bitcast(F32), sgn[r, c], ALU.mult))
                elif part == 1:
                    own.link(nc.vector.tensor_scalar(cum, x, thr[r, c], None, ALU.is_gt, ALU.add, accum_out=cnt[r, c]))
                elif part == 2:
                    own.link(nc.vector.tensor_scalar(need[r, c], cnt[r, c], -1.0, float(TOPK), ALU.mult, ALU.add))
                elif part == 3:
                    own.link(nc.vector.tensor_scalar(eq, x, thr[r, c], None, ALU.is_equal))
                elif part == 4:
                    own.link(nc.vector.tensor_tensor_scan(cum, eq, eq, 0.0, ALU.add, ALU.max))
                elif part == 5:
                    own.link(nc.vector.scalar_tensor_tensor(eq, cum, need[r, c], eq, ALU.is_le, ALU.mult))
                elif part == 6:
                    own.link(nc.vector.scalar_tensor_tensor(cum, x, thr[r, c], eq, ALU.is_gt, ALU.add))
                else:
                    out = x if group is PROMPT else scs[:].bitcast(BF16)[:, 0:SLS]
                    own.link(nc.vector.tensor_scalar(out, cum, 1.0, BIG, ALU.subtract, ALU.mult))

            dve.wait_ge(sc_ok, NBLK - 2)
            start_search(PROMPT)
            search_bits(EARLY_BITS)
            dve.wait_ge(ss_["sum"], DEC_B)
            nc.vector.tensor_copy(scs[:], PSF[0:NS, 0:SLS]).then_inc(ss_["cp"], 1)

            dve.wait_ge(tabQ, 32)
            for g in range(NKV):
                u = U_K + g
                dve.wait_ge(w_used, u + 1)
                own.link(nc.vector.scalar_tensor_tensor(as3(tq[:]), slot3(u % 2), gqk[:, 1:2], as3(csQ[:]),
                                                        ALU.mult, ALU.mult))
                dve.sem_inc(kk_["t1d"], 1)
                dve.wait_ge(kk_["swa"], 4 + 2 * g)
                own.link(nc.vector.tensor_tensor(swp[:], swp[:], snQ[:], ALU.mult))
                own.link(nc.vector.tensor_tensor(tq[:], tq[:], swp[:], ALU.add))
                dve.wait_ge(kk_["rt"], 6 + 3 * g)
                own.link(nc.vector.reciprocal(rbc[:], rbc[:]))
                own.link(nc.vector.tensor_tensor(kT[:, g, :], tq[:], rbc[:], ALU.mult))
                dve.sem_inc(kk_["done"], 1)
                search_bit(PROMPT)
                tokens_out(1 + g, kout, DH, g * DH)
            for g in range(NKV):
                tokens_out(3 + g, vtok, DH, g * DH)
                search_bit(PROMPT)

            dve.wait_ge(ss_["ok"], 1)
            start_search(SAMPLE)

            dve.wait_ge(kk_["st"], 16 * 6)
            with dve.Fori(0, NH // 2) as i:
                own.enter(i, 2 + 2 * BIT_LINKS)
                for ff in range(2):
                    f = 2 * i + ff
                    rotate(qq, U_Q + f, f, (U_Q + ff) % 2, qT[:, bass.ds(f, 1), :].rearrange("p o n -> p (o n)"),
                           csQ, snQ, gqk[:, 0:1])
                    search_bit(PROMPT)
            own.leave(NH // 2)
            search_bits(BITS - EARLY_BITS - KV_BITS - NH)
            for rows, j in ((NS, slice(0, 1)), (P, slice(1, 9))):
                dve.wait_ge(qq["rt"], 2)
                own.link(nc.vector.reciprocal(qs[0:rows, j, :], qs[0:rows, j, :]))
                own.link(nc.vector.tensor_scalar(qs[0:rows, j, :], qs[0:rows, j, :], DH ** -0.5, None, ALU.mult))
                own.link(nc.vector.tensor_scalar(nqs[0:rows, j, :], qs[0:rows, j, :], -1.0, None, ALU.mult))

            dve.wait_ge(w_used, U_O)
            for q in range(2):
                dve.wait_ge(z_st[q], 16 * (KD // 2))

            dve.wait_ge(cs_ok, 1)

            def mask_and_max(n):
                b, h = STEPS[n]
                w = (b + 1) * P
                off = caus[:, 2 * P - w:2 * P] if b < 2 else sc[:, block_off(b):block_off(b + 1)]
                dve.wait_ge(at_["s"], n + 1)
                if n >= NR:
                    dve.wait_ge(at_["tr"], FIRST[n - NR + 1])
                nc.vector.tensor_tensor_reduce(
                    out=pring[n % NR][:, 0:w], in0=PSF[:, 2 * (n % 2) * BANK:2 * (n % 2) * BANK + w], in1=off,
                    scale=1.0, scalar=-3.0e38, op0=ALU.add, op1=ALU.max, accum_out=amx[:, n:n + 1]).then_inc(at_["mx"], 1)
                dve.wait_ge(at_["mx"], n + 1)
                nc.vector.tensor_tensor(anb[:, n:n + 1], amx[:, n:n + 1], nqs[:, 1 + b, h:h + 1], ALU.mult).then_inc(at_["nb"], 1)

            def normalise(n):
                b, h = STEPS[n]
                w = (b + 1) * P
                dve.wait_ge(at_["ex"], n + 1)
                own.link(nc.vector.reciprocal(ars[:, n:n + 1], asm[:, n:n + 1]))
                nc.vector.tensor_scalar(pring[n % NR][:, 0:w], pring[n % NR][:, 0:w], ars[:, n:n + 1], None,
                                        ALU.mult).then_inc(at_["nr"], 1)
                if h % REP == REP - 1 and n >= REP:
                    heads_out(n // REP - 1)

            def heads_out(i):
                b, g = i // NKV, i % NKV
                c0 = tile_cols(1 + b)[0]
                dve.wait_ge(at_["pv"], i + 1)
                nc.vector.tensor_copy(qT[:, REP * g:REP * g + REP, c0:c0 + P],
                                      PS[:, 6 + i % 2, :].rearrange("p (r q) -> p r q", q=P)).then_inc(at_["o"], 1)

            def sample_operands():
                own.link(nc.vector.memset(qb[:], 0.0))
                for g in range(NKV):
                    for q in range(REP):
                        nc.vector.tensor_copy(
                            qb[:, :, g, 32 * g + 8 * q:32 * g + 8 * q + 8],
                            qT[:, REP * g + q, 0:NS].rearrange("p (b t) -> p b t", t=DEC_T))
                idb = ident[0:NS, 0:NS].rearrange("p (b t) -> p b t", t=DEC_T)
                nc.vector.reduce_sum(bd8[:], idb, axis=AX.X)
                own.link(nc.vector.reduce_sum(d8[:], idb.rearrange("p b t -> p t b"), axis=AX.X))
                nc.vector.tensor_tensor(qa8[:], d8[:].unsqueeze(1).broadcast_to((NS, NH, DEC_T)),
                                        qs[0:NS, 0, :].unsqueeze(2).broadcast_to((NS, NH, DEC_T)), ALU.mult).then_inc(sa["pre"], 1)

            mask_and_max(0)
            mask_and_max(1)
            for n in range(len(STEPS)):
                normalise(n)
                if STEPS[n][0] >= 1 and n + NH < len(STEPS):
                    b = STEPS[n][0] + 1
                    for part in RESOLVE_AT[STEPS[n][1]]:
                        resolve(PROMPT, b - 2, sc[:, block_off(b):block_off(b + 1)], kTb[:, 0], kTb[:, 1], part)
                if n == NH:
                    sample_operands()
                if SIDE <= n < SIDE + BITS:
                    search_bit(SAMPLE)
                elif n >= SIDE + BITS:
                    resolve(SAMPLE, NBLK - 2, scs[:], Ps, acc, n - SIDE - BITS)
                if n + 2 < len(STEPS):
                    mask_and_max(n + 2)
            heads_out(NBLK * NKV - 1)

            def gate_z(f, cols):
                dve.wait_ge(z_in[f], 16)
                return nc.vector.tensor_tensor(qT[:, f, cols], qT[:, f, cols], zb[f][:, cols], ALU.mult)

            def sample_max(b):
                dve.wait_ge(sa["s"], b + 1)
                own.link(nc.vector.reduce_max(smx[:, b:b + 1], PSF[0:NS, 0:SLS], axis=AX.X))
                dve.wait_ge(sa["qc"], 2)
                nc.vector.tensor_tensor(snb[:, b:b + 1], smx[:, b:b + 1], nqcol[:, b:b + 1], ALU.mult).then_inc(sa["nb"], 1)

            sample_max(0)
            for b in range(DEC_B):
                dve.wait_ge(sa["ex"], b + 1)
                own.link(nc.vector.reciprocal(srs[:, b:b + 1], ssm[:, b:b + 1]))
                nc.vector.tensor_scalar(Ps[:], Ps[:], srs[:, b:b + 1], None, ALU.mult).then_inc(sa["nr"], 1)
                if b + 1 < DEC_B:
                    sample_max(b + 1)
                dve.wait_ge(sa["pv"], b + 1)
                nc.vector.tensor_copy(qT[:, :, b * DEC_T:(b + 1) * DEC_T],
                                      PS[:, 3, 0:NS].rearrange("p (h t) -> p h t", t=DEC_T)).then_inc(sa["o"], 1)
                for f in range(2 * b - 10, 2 * b - 8) if b >= 5 else ():
                    own.link(gate_z(f, slice(NS, TP)))
            own.link(gate_z(KD - 2, slice(NS, TP)))
            own.link(gate_z(KD - 1, slice(NS, TP)))
            dve.wait_ge(sa["o"], DEC_B)
            for f in range(KD):
                gate_z(f, slice(0, NS)).then_inc(oy["y"], 1)
                dve.wait_ge(oy["y"], f + 1)
                dve.wait_ge(oy["hi"], f + 1)
                nc.vector.tensor_tensor(hlo[:, f, :], qT[:, f, :], hhi[:, f, :].bitcast(F32), ALU.subtract).then_inc(oy["lo"], 1)
            dve.wait_ge(xs_in, 16)
            with dve.Fori(0, KD // 2) as i:
                for ff in range(2):
                    f = 2 * i + ff
                    dve.wait_ge(w_used, U_O + f + 1)
                    x = xT[:, bass.ds(f, 1), :].rearrange("p o (b n) -> p (o b) n", b=3)
                    nc.vector.tensor_tensor(x, slot3((U_O + ff) % 2), x, ALU.add).then_inc(oy["xup"], 1)
            gate_dve(1, True)

        @block.tensor
        def _(pe):
            pe.sem_inc(gmlp["vtr"], 2)
            pe.sem_inc(embed_sems["pe"], 1)
            pe.sem_inc(qq["st"], 1)
            pe.wait_ge(cst, 7)
            for j in range(9):
                c0, n = tile_cols(j)
                pe.wait_ge(x_in[j % 3], 16 * (j // 3 + 1))
                if j >= 3:
                    pe.wait_ge(x_ev, j - 2)
                    pe.wait_ge(x_eva, j - 2)
                for k in range(KD):
                    tr = nc.tensor.transpose(PS[:, 2 * (j % 3) + k // 4, (k % 4) * P:(k % 4) * P + n],
                                             xstage[0:n, j % 3, k * P:(k + 1) * P], ident[0:n, 0:n])
                tr.then_inc(x_tr, 1)
            pe.wait_ge(ws_in, 16)
            for q in range(NGRP):
                tr = nc.tensor.transpose(PS[:, 6 + q // 4, (q % 4) * P:(q % 4 + 1) * P], wsraw[:, q, :], ident[:])
                if q % 4 == 3:
                    tr.then_inc(ws_tr, 1)
            pe.wait_ge(x_ev, 9)
            pe.wait_ge(x_eva, 9)
            pe.wait_ge(x_dg, 9)
            pe.wait_ge(ws_ev, 2)

            for g in range(2):
                c0, n, nch, has_s = GROUPS[g]
                h = n // 2
                s = sA[g]
                halves = [(0, h), (h, h)]
                if g == 0:
                    norm_pe(pe, nA[g], group_cols(g))
                po = NS if has_s else 0

                def v_unit(f, ff):
                    pe.wait_ge(w_lo, U_A[g] + f + 1)
                    pe.wait_ge(s["vev"], s.at("vev", f + 1))
                    gemm(pe, ff, [(PS[:, 2 * ff + m, 0:h], c) for m, c in enumerate(halves)],
                         lambda k, a, m: hhi_g[:, k, a:a + m], lambda k, a, m: hlo_g[:, k, a:a + m],
                         kwait=nA[g]["lo"], first_k=nA[g].at("lo", 1)).then_inc(w_used, 1)

                def v_transpose(f, ff):
                    pe.wait_ge(s["vev"], s.at("vev", f + 3))
                    pe.wait_ge(s["vst"], s.at("vst", f + 1))
                    for c in range(nch):
                        tr = nc.tensor.transpose(PS[:, 4 + 2 * ff, c * P:(c + 1) * P],
                                                 vtmp[ff][:, po + c * P:po + (c + 1) * P], ident[:])
                    if has_s:
                        tr = nc.tensor.transpose(PS[0:NS, 5 + 2 * ff, 0:P], vtmp[ff][:, 0:NS], ident[:])
                    tr.then_inc(s["vtr"], 1)

                v_unit(0, 0)
                with pe.Fori(0, KA // 2 - 1) as i:
                    v_unit(2 * i + 1, 1)
                    v_transpose(2 * i, 0)
                    v_unit(2 * i + 2, 0)
                    v_transpose(2 * i + 1, 1)
                v_unit(KA - 1, 1)
                v_transpose(KA - 2, 0)
                v_transpose(KA - 1, 1)

                with pe.Fori(0, KA // 2) as i:
                    for ff in range(2):
                        f = 2 * i + ff
                        for half in range(2):
                            pe.wait_ge(w_lo, U_A[g] + KA + 2 * f + half + 1)
                            free = "sz" if half == 0 else "ut"
                            pe.wait_ge(s[free], s.at(free, f + 1))
                            gemm(pe, half, [(PS[:, 2 * half + m, 0:h], c) for m, c in enumerate(halves)],
                                 lambda k, a, m: hhi_g[:, k, a:a + m],
                                 lambda k, a, m: hlo_g[:, k, a:a + m]).then_inc(w_used, 1)
                        pe.wait_ge(s["vs"], s.at("vs", f + 1))
                        pe.wait_ge(s["mt"], s.at("mt", f + 1))
                        for c in range(nch):
                            mm = nc.tensor.matmul(PS[:, 4, c * P:(c + 1) * P], vs[:, c * P:(c + 1) * P],
                                                  wsT[:, bass.ds(i, 1), :].rearrange("p o t -> p (o t)"),
                                                  start=True, stop=True)
                        if has_s:
                            mm = nc.tensor.matmul(PS[:, 5, 0:NS], vs[0:NS, 4 * P:5 * P],
                                                  wsbd[:, bass.ds(i, 1), :].rearrange("p o t -> p (o t)"),
                                                  start=True, stop=True)
                        mm.then_inc(s["mix"], 1)

                if g == 0:
                    norm_pe(pe, nA[1], group_cols(1))
                with pe.Fori(0, KD // 2) as i:
                    for ff in range(2):
                        pe.wait_ge(s["xup"], s.at("xup", 2 * i + ff + 1))
                        for half in range(2):
                            pe.wait_ge(w_lo, U_A[g] + 3 * KA + 4 * i + 2 * ff + half + 1)
                            gemm(pe, half, [(PS[:, 2 * ff + m, 0:h], c) for m, c in enumerate(halves)],
                                 lambda k, a, m: yhi[:, half * KD + k, a:a + m],
                                 lambda k, a, m: ylo[:, half * KD + k, a:a + m],
                                 first=half == 0, last=half == 1,
                                 kwait=None if ff else s["ylo"],
                                 first_k=s.at("ylo", half * KD + 2)).then_inc(w_used, 1)

            def gate_pe(layer, last):
                s, base = sG[layer], U_GATE[layer]
                norm_pe(pe, nG[layer], ALL_COLS)
                pe.wait_ge(s["pin"], s.at("pin", 32))
                pe.wait_ge(nG[layer]["rt"], nG[layer].at("rt", 3))
                for kk, m, bank, q0, _, _ in PIECES_P:
                    for j in (range(1 + 4 * m, 5 + 4 * m) if m < 2 else (0,)):
                        rows = NS if j == 0 else P
                        q = q0 + ((j - 1) % 4 * P if j else 0)
                        tr = nc.tensor.transpose(PS[:, bank, q:q + rows],
                                                 pst[0:rows, j, kk * P:(kk + 1) * P], ident[0:rows, 0:rows])
                    tr.then_inc(s["ptr"], 1)

                def gate_unit(f, ff):
                    pe.wait_ge(w_lo, base + f + 1)
                    pe.wait_ge(s["sig"], s.at("sig", f + 1))
                    par = (base + ff) % 2
                    gemm(pe, par, [(PS[:, m, 0:NC3], (m * NC3, NC3)) for m in range(3)],
                         lambda k, a, m: hhi[:, k, a:a + m], lambda k, a, m: hlo[:, k, a:a + m],
                         kwait=nG[layer]["lo"],
                         first_k=nG[layer].at("lo", 1)).then_inc(w_used, 1)

                def embed(f):
                    if isinstance(f, int) and f == 0 or not last:
                        pe.wait_ge(s["plo"], s.at("plo", 8))
                    pe.wait_ge(s["wpl"], s.at("wpl", f + 1))
                    pe.wait_ge(s["t"], s.at("t", f + 1))
                    for k in range(2):
                        for n, (w, r) in enumerate(((pehi, pThi), (pehi, pTlo), (pelo, pThi))):
                            for m in range(3):
                                mm = nc.tensor.matmul(PS[:, 3 + m, 0:NC3], w[:, k, :],
                                                      r[:, k, m * NC3:(m + 1) * NC3],
                                                      start=k == 0 and n == 0, stop=k == 1 and n == 2)
                    mm.then_inc(s["pe"], 1)

                def transpose_out(f, ff):
                    pe.wait_ge(s["xup"], s.at("xup", f + 2))
                    for m in range(3):
                        pe.wait_ge(y_ev, 3 * f + 1 + m // 2)
                        for q in range(4 if m < 2 else 1):
                            c0, _ = tile_cols(1 + 4 * m + q if m < 2 else 0)
                            tr = nc.tensor.transpose(PS[:, 6 + m % 2, q * P:(q + 1) * P], xo[:, ff, c0:c0 + P],
                                                     ident[:])
                        tr.then_inc(y_tr, 1)

                if not last:
                    with pe.Fori(0, KD // 2) as i:
                        for ff in range(2):
                            gate_unit(2 * i + ff, ff)
                            embed(2 * i + ff)
                else:
                    gate_unit(0, 0)
                    embed(0)
                    with pe.Fori(0, KD // 2 - 1) as i:
                        for ff in range(2):
                            gate_unit(2 * i + 1 + ff, 1 - ff)
                            transpose_out(2 * i + ff, ff)
                            embed(2 * i + 1 + ff)
                    gate_unit(KD - 1, 1)
                    transpose_out(KD - 2, 0)
                    embed(KD - 1)
                    transpose_out(KD - 1, 1)

            pe.wait_ge(stat, 2)
            gate_pe(0, False)
            THREE = [(m * NC3, NC3) for m in range(3)]

            def full_unit(u, par, kwait=None, first_k=1):
                pe.wait_ge(w_lo, u + 1)
                gemm(pe, par, [(PS[:, 3 * par + m, 0:NC3], c) for m, c in enumerate(THREE)],
                     lambda k, a, m: hhi[:, k, a:a + m], lambda k, a, m: hlo[:, k, a:a + m],
                     kwait=kwait, first_k=first_k).then_inc(w_used, 1)

            pe.wait_ge(stat, 3)
            norm_pe(pe, nB, ALL_COLS)
            pe.wait_ge(sG[0]["t"], sG[0].at("t", KD + 1))
            for f in range(IH // 2):
                pe.wait_ge(iq["swa"], f + 1)
                pe.wait_ge(iq["t1d"], f + 1)
                full_unit(U_IQ + f, f % 2, None if f else nB["lo"], nB.at("lo", 1))
            pe.wait_ge(iq["swa"], 5)
            pe.wait_ge(iq["t1d"], 5)
            full_unit(U_IK, 0)

            def head_sums(n, rows):
                pe.wait_ge(kk_["swa"], 2 * n + 1)
                if n:
                    pe.wait_ge(tt_ev, 3 * n)
                for c, (a, m) in enumerate(ALL_COLS):
                    if c == 2:
                        pe.wait_ge(kk_["rt"], 3 * n + 1)
                    nc.tensor.matmul(PS[:, 6 + c % 2, 0:m], ones[0:rows, :], sqt[0:rows, a:a + m],
                                     start=True, stop=True).then_inc(kk_["sum"], 1)

            def tokens(n, src, rows):
                for m in range(3):
                    if 3 * n + m >= 2:
                        pe.wait_ge(tt_ev, 3 * n + (1 if m == 2 else 0))
                    for q in range(4 if m < 2 else 1):
                        c0, cn = tile_cols(1 + 4 * m + q if m < 2 else 0)
                        tr = nc.tensor.transpose(PS[0:cn, 6 + m % 2, q * rows:(q + 1) * rows], src(c0, cn),
                                                 ident[0:rows, 0:rows])
                    tr.then_inc(tt_tr, 1)

            head_sums(0, ID)
            pe.wait_ge(kk_["done"], 1)
            pe.wait_ge(kk_["rt"], 3)
            tokens(0, lambda a, n: ikT[0:ID, a:a + n], ID)
            pe.wait_ge(tt_ev, 3)
            for j in range(9):
                c0, cn = tile_cols(j)
                tr = nc.tensor.transpose(PS[0:cn, 7, j * IH:(j + 1) * IH], iwT[:, c0:c0 + cn], ident[0:IH, 0:IH])
            tr.then_inc(iw_tr, 1)
            pe.wait_ge(iq["add"], 5)
            for m, (b, c, h) in enumerate(SCORES):
                n = min(BANK, (b + 1) * P - c * BANK)
                p0 = ID * (h % 2)
                c0 = tile_cols(1 + b)[0]
                if m >= 6:
                    pe.wait_ge(sc_re, m - 5)
                nc.tensor.matmul(PS[:, m % 6, 0:n], iqT[p0:p0 + ID, h // 2, c0:c0 + P],
                                 ikT[p0:p0 + ID, NS + c * BANK:NS + c * BANK + n], start=True,
                                 stop=True).then_inc(sc_mm, 1)
            pe.wait_ge(sc_re, len(SCORES))
            pe.wait_ge(ss_["pre"], 3)
            for b in range(DEC_B):
                tr = nc.tensor.transpose(PS[0:NS, 5, b * NS:(b + 1) * NS], sbT[:, b, :], ident[0:NS, 0:NS])
            tr.then_inc(ss_["wt"], 1)
            PARTS = ((0, BANK), (BANK, BANK), (2 * BANK, NS))

            def ik_pages(b):
                pe.wait_ge(ikp[b % 3], 16 * NPAGE * (b // 3 + 1))
                if b:
                    pe.wait_ge(ss_["ev"], b)
                else:
                    pe.wait_ge(iw_ev, 1)
                for g in range(NPAGE):
                    tr = nc.tensor.transpose(PS[:, 6 + g // 4, (g % 4) * P:(g % 4 + 1) * P],
                                             ikpg[b % 3][:, g].rearrange("p q d -> p (q d)"), ident[:])
                tr.then_inc(ss_["tr"], 1)

            def weigh(b):
                pe.wait_ge(ss_["re"], b + 1)
                for m, (a, n) in enumerate(PARTS):
                    mm = nc.tensor.matmul(PS[0:NS, m, 0:n], sbw[:, b, :], rels[:, a:a + n], start=b == 0,
                                          stop=b == DEC_B - 1)
                mm.then_inc(ss_["sum"], 1)

            ik_pages(0)
            pe.wait_ge(ss_["wt"], 2)
            for b in range(DEC_B):
                if b + 1 < DEC_B:
                    ik_pages(b + 1)
                if b:
                    weigh(b - 1)
                pe.wait_ge(ss_["ev"], b + 1)
                for m, (a, n) in enumerate(PARTS):
                    mm = nc.tensor.matmul(PS[0:NS, 3 + m, 0:n], iqb[:, b, :],
                                          ikTb[b % 2][:, a:a + n] if m < 2 else ikT[:, 0:NS], start=True, stop=True)
                mm.then_inc(ss_["mm"], 1)
            weigh(DEC_B - 1)
            pe.wait_ge(ss_["cp"], 1)

            def key_tokens(g):
                pe.wait_ge(kk_["done"], 2 + g)
                pe.wait_ge(kk_["rt"], 6 + 3 * g)
                tokens(1 + g, lambda a, n: kT[:, g, a:a + n], P)

            def value_tokens(g):
                pe.wait_ge(kk_["vev"], g + 1)
                tokens(3 + g, lambda a, n: sqt[:, a:a + n], P)

            full_unit(U_K, U_K % 2)
            head_sums(1, P)
            full_unit(U_K + 1, (U_K + 1) % 2)
            key_tokens(0)
            head_sums(2, P)
            full_unit(U_V, U_V % 2)
            key_tokens(1)
            full_unit(U_V + 1, (U_V + 1) % 2)
            value_tokens(0)
            value_tokens(1)
            pe.wait_ge(tt_ev, 15)

            def q_unit(f, ff):
                pe.wait_ge(qq["swa"], f + 1)
                pe.wait_ge(qq["t1d"], f + 1)
                full_unit(U_Q + f, (U_Q + ff) % 2)

            def q_sums(f):
                pe.wait_ge(qq["swa"], f + 3)
                for j in range(9):
                    c0, cn = tile_cols(j)
                    mm = nc.tensor.matmul(PS[0:cn, 7, bass.ds(f + NH * j, 1)], sqt[:, c0:c0 + cn], ones[:, 0:1],
                                          start=True, stop=True)
                mm.then_inc(qq["st"], 1)

            q_unit(0, 0)
            with pe.Fori(0, NH // 2 - 1) as i:
                q_unit(2 * i + 1, 1)
                q_sums(2 * i)
                q_unit(2 * i + 2, 0)
                q_sums(2 * i + 1)
            q_unit(NH - 1, 1)
            q_sums(NH - 2)
            pe.wait_ge(qq["swa"], NH + 1)
            pe.wait_ge(qq["t1d"], NH + 1)
            full_unit(U_Z, U_Z % 2)
            q_sums(NH - 1)
            pe.wait_ge(qq["st"], NH + 1)
            pe.sem_inc(qq["end"], 1)
            pe.wait_ge(qq["swa"], NH + 2)
            pe.wait_ge(qq["t1d"], NH + 2)
            full_unit(U_Z + 1, (U_Z + 1) % 2)
            with pe.Fori(1, KD // 2) as i:
                for ff in range(2):
                    pe.wait_ge(z_ev, 2 * i + ff + 1)
                    full_unit(U_Z + 2 * i + ff, (U_Z + ff) % 2)

            def logits(n):
                b, h = STEPS[n]
                w, c0 = (b + 1) * P, tile_cols(1 + b)[0]
                if n >= 2:
                    pe.wait_ge(at_["mx"], n - 1)
                for a in range(0, w, BANK):
                    m = min(BANK, w - a)
                    mm = nc.tensor.matmul(PS[:, 2 * (n % 2) + a // BANK, 0:m], qT[:, h, c0:c0 + P],
                                          kT[:, h // REP, NS + a:NS + a + m], start=True, stop=True)
                mm.then_inc(at_["s"], 1)

            pe.wait_ge(z_ev, KD + 2)
            pe.wait_ge(qq["rt"], 2)
            pe.wait_ge(qq["add"], NH + 1)
            logits(0)
            logits(1)
            for n, (b, h) in enumerate(STEPS):
                if n + 2 < len(STEPS):
                    logits(n + 2)
                pe.wait_ge(at_["nr"], n + 1)
                for i in range(FIRST[n], FIRST[n + 1]):
                    m = PIECES[i][3]
                    if i >= 2:
                        pe.wait_ge(at_["pt"], i - 1)
                    for k in range(4 * m, min(4 * m + 4, b + 1)):
                        tr = nc.tensor.transpose(PS[:, 4 + i % 2, (k - 4 * m) * P:(k - 4 * m + 1) * P],
                                                 pring[n % NR][:, k * P:(k + 1) * P], ident[:])
                    tr.then_inc(at_["tr"], 1)
                if h % REP == REP - 1:
                    i, g = n // REP, h // REP
                    pe.wait_ge(at_["pt"], FIRST[n + 1])
                    if i >= 2:
                        pe.wait_ge(at_["o"], i - 1)
                    for k in range(b + 1):
                        mm = nc.tensor.matmul(PS[:, 6 + i % 2, :], vtok[:, 1 + k, g * DH:(g + 1) * DH],
                                              PTs[:, k].rearrange("p r q -> p (r q)"), start=k == 0, stop=k == b)
                    mm.then_inc(at_["pv"], 1)

            pe.wait_ge(at_["o"], NBLK * NKV)
            pe.wait_ge(sa["pre"], 1)
            nc.tensor.matmul(PS[0:NS, 3, 0:DEC_B], qa8[:].rearrange("p h t -> p (h t)"), bd8[:], start=True,
                             stop=True).then_inc(sa["qc"], 1)

            def k_pages(b):
                pe.wait_ge(kpin[b % 2], 16 * NPAGE * (b // 2 + 1))
                if b:
                    pe.wait_ge(sa["ke"], b)
                for g in range(NKV):
                    for j in range(NPAGE):
                        tr = nc.tensor.transpose(PS[:, 4 + 2 * g + j // 4, (j % 4) * P:(j % 4 + 1) * P],
                                                 kpg[b % 2][:, j, g * DH:(g + 1) * DH], ident[:])
                tr.then_inc(sa["kt"], 1)

            def sample_logits(b):
                pe.wait_ge(sa["ke"], b + 1)
                if b:
                    pe.wait_ge(sa["ex"], b)
                for m, (a, n) in enumerate(PARTS):
                    for g in range(NKV):
                        nc.tensor.matmul(PS[0:NS, m, 0:n], qb[:, b, g, :],
                                         kTb[:, g, a:a + n] if m < 2 else kT[:, g, 0:NS], start=g == 0, stop=False)
                    mm = nc.tensor.matmul(PS[0:NS, m, 0:n], repb[:, b, :], scs[:].bitcast(BF16)[:, a:a + n],
                                          start=False, stop=True)
                mm.then_inc(sa["s"], 1)

            k_pages(0)
            pe.wait_ge(sa["qc"], 2)
            sample_logits(0)
            for b in range(DEC_B):
                if b + 1 < DEC_B:
                    k_pages(b + 1)
                    pe.wait_ge(sa["ke"], b + 2)
                pe.wait_ge(sa["nr"], b + 1)
                if b:
                    pe.wait_ge(sa["o"], b)
                for j in range(NPAGE):
                    nc.tensor.transpose(PS[:, 3, j * NS:(j + 1) * NS], Ps[:, j * P:(j + 1) * P], ident[0:NS, 0:NS])
                nc.tensor.transpose(PS[0:NS, 4, 0:NS], Ps[:, PAST:SLS], ident[0:NS, 0:NS]).then_inc(sa["tr"], 1)
                if b + 1 < DEC_B:
                    sample_logits(b + 1)
                pe.wait_ge(sa["pt"], b + 1)
                pe.wait_ge(vpin[b % 2], 16 * NPAGE * (b // 2 + 1))
                for g in range(NKV):
                    for j in range(NPAGE):
                        nc.tensor.matmul(PS[:, 3, 32 * g:32 * g + 32], vpg[b % 2][:, j, g * DH:(g + 1) * DH],
                                         PsT[:, j, 32 * g:32 * g + 32], start=j == 0, stop=False)
                    mm = nc.tensor.matmul(PS[:, 3, 32 * g:32 * g + 32], vtok[0:NS, 0, g * DH:(g + 1) * DH],
                                          PsT[0:NS, 8, 32 * g:32 * g + 32], start=False, stop=True)
                mm.then_inc(sa["pv"], 1)

            pe.wait_ge(sa["o"], DEC_B)
            with pe.Fori(0, KD // 2) as i:
                for ff in range(2):
                    pe.wait_ge(oy["xup"], 2 * i + ff + 1)
                    full_unit(U_O + 2 * i + ff, (U_O + ff) % 2, oy["lo"])
            pe.wait_ge(stat, 4)
            gate_pe(1, True)


_INS = ['x_prompt', 'x_sample', 'cache_k', 'cache_v', 'cache_ik', 'page_table', 'p_prompt', 'p_sample', 'g_norm',
        'w_in_a', 'w_s_a', 'b_s_a', 'g_v_a', 'w_out_a', 'w_in_b', 'g_q_b', 'g_k_b', 'g_ik_b', 'w_out_b', 'g_pe',
        'w_pe_gate', 'w_pe_proj']
_OUTS = [(1, SEQ, D), (DEC_B, DEC_T, D), (1, 1, SEQ, NKV, DH), (1, 1, SEQ, NKV, DH), (1, 1, SEQ, ID),
         (DEC_B, 1, DEC_T, NKV, DH), (DEC_B, 1, DEC_T, NKV, DH), (DEC_B, 1, DEC_T, ID), (DEC_B, 1, DEC_T, AW)]


def kernel(**inputs):
    import concourse.bacc as bacc
    from concourse.bass_utils import run_bass_kernel_spmd as run

    nc = bacc.Bacc("TRN2", target_bir_lowering=False, num_devices=1)
    arrays, args = {}, []
    for name in _INS:
        a = np.ascontiguousarray(inputs[name])
        arrays[f"in_{name}_dram"] = a
        args.append(nc.dram_tensor(f"in_{name}_dram", a.shape, mybir.dt.from_np(a.dtype), kind="ExternalInput").ap())
    for i, shape in enumerate(_OUTS):
        args.append(nc.dram_tensor(f"out_{i}_dram", shape, F32, kind="ExternalOutput").ap())
    hybrid_trunk(nc, *args)
    r = run(nc, [arrays], core_ids=[0])
    return tuple(r.results[0][f"out_{i}_dram"] for i in range(len(_OUTS)))
```
